# Optimizing a Trainium2 kernel written in Bass

```python
import jax, jax.numpy as jnp
from jax import lax
import numpy as np

D_MODEL = 1024
BATCH = 1
SEQ = 256
DEPTH = 2

HEAD_DIM = 64
N_HEADS = D_MODEL // HEAD_DIM
H_DIL = (N_HEADS * 3) // 8
H_FOX = (N_HEADS - H_DIL) // 2
H_SB = N_HEADS - H_DIL - H_FOX
DIL_PATTERNS = ((128, 1), (512, 4), (2048, 16))
BLOCK = 128
D_FF = ((8 * D_MODEL // 3 + 127) // 128) * 128
N_EXPERTS = 8
TOP_K = 2
N_DENSE = (DEPTH + 1) // 2
N_MOE = DEPTH // 2
PROJ_OUT = 3 * D_MODEL + H_FOX
EPS = 1e-6
NEG = -1e30

kernel_name = "hybrid_dilated_fox_stickbreaking_moe_block"

def _rmsnorm(x, g):
    xf = x.astype(jnp.float32)
    y = xf * lax.rsqrt(jnp.mean(xf * xf, axis=-1, keepdims=True) + EPS)
    return (y * g.astype(jnp.float32)).astype(x.dtype)

def _dilated_pattern(q, k, v, slopes, window, dilation):
    B, S, H, Dh = q.shape
    W = window // dilation
    n_prev = -(-W // BLOCK)
    L = S // dilation
    nb = -(-L // BLOCK)
    Lp = nb * BLOCK
    KB = (n_prev + 1) * BLOCK
    scale = HEAD_DIM ** -0.5

    def streams(t):
        return t.reshape(B, L, dilation, H, Dh)

    qs = jnp.pad(streams(q), ((0, 0), (0, Lp - L), (0, 0), (0, 0), (0, 0)))
    qs = qs.reshape(B, nb, BLOCK, dilation, H, Dh)
    pad_kv = ((0, 0), (n_prev * BLOCK, Lp - L), (0, 0), (0, 0), (0, 0))
    kb = jnp.pad(streams(k), pad_kv).reshape(B, nb + n_prev, BLOCK, dilation, H, Dh)
    vb = jnp.pad(streams(v), pad_kv).reshape(B, nb + n_prev, BLOCK, dilation, H, Dh)
    k_band = jnp.concatenate([kb[:, i:i + nb] for i in range(n_prev + 1)], axis=2)
    v_band = jnp.concatenate([vb[:, i:i + nb] for i in range(n_prev + 1)], axis=2)

    s = jnp.einsum('bnqrhd,bnkrhd->bnrhqk', qs, k_band).astype(jnp.float32) * scale
    qi = jnp.arange(BLOCK)[:, None]
    kj = jnp.arange(KB)[None, :]
    dist = qi - kj + n_prev * BLOCK
    blk = jnp.arange(nb)[:, None, None]
    valid = (dist >= 0) & (dist <= W) & (blk * BLOCK + kj >= n_prev * BLOCK)
    s = s - slopes[:, None, None] * (dist * dilation).astype(jnp.float32)
    s = jnp.where(valid[None, :, None, None], s, NEG)
    m = jnp.max(s, axis=-1, keepdims=True)
    p = jnp.exp(s - m)
    den = jnp.sum(p, axis=-1)
    o = jnp.einsum('bnrhqk,bnkrhd->bnqrhd', p.astype(v.dtype), v_band).astype(jnp.float32)
    o = o / jnp.transpose(den, (0, 1, 4, 2, 3))[..., None]
    lse = jnp.transpose(m[..., 0] + jnp.log(den), (0, 1, 4, 2, 3))
    o = o.reshape(B, Lp, dilation, H, Dh)[:, :L].reshape(B, S, H, Dh)
    lse = lse.reshape(B, Lp, dilation, H)[:, :L].reshape(B, S, H)
    return o, lse

def _dilated_attention(q, k, v):
    slopes = 2.0 ** (-8.0 * jnp.arange(1, H_DIL + 1, dtype=jnp.float32) / H_DIL)
    outs, lses = [], []
    for window, dilation in DIL_PATTERNS:
        o, lse = _dilated_pattern(q, k, v, slopes, window, dilation)
        outs.append(o)
        lses.append(lse)
    wts = jax.nn.softmax(jnp.stack(lses, axis=0), axis=0)
    return jnp.sum(wts[..., None] * jnp.stack(outs, axis=0), axis=0)

def _fox_attention(q, k, v, log_f_cum):
    B, S, H, Dh = q.shape
    nq = S // BLOCK
    scale = HEAD_DIM ** -0.5
    qb = q.reshape(B, nq, BLOCK, H, Dh).transpose(1, 0, 2, 3, 4)
    cb = log_f_cum.reshape(B, nq, BLOCK, H).transpose(1, 0, 3, 2)
    c_keys = jnp.transpose(log_f_cum, (0, 2, 1))
    kpos = jnp.arange(S)

    def block(args):
        qblk, cblk, start = args
        s = jnp.einsum('bqhd,bkhd->bhqk', qblk, k).astype(jnp.float32) * scale
        s = s + cblk[..., None] - c_keys[:, :, None, :]
        qpos = start + jnp.arange(BLOCK)
        s = jnp.where(kpos[None, :] <= qpos[:, None], s, NEG)
        p = jax.nn.softmax(s, axis=-1)
        return jnp.einsum('bhqk,bkhd->bqhd', p.astype(v.dtype), v).astype(jnp.float32)

    out = lax.map(block, (qb, cb, jnp.arange(nq) * BLOCK))
    return out.transpose(1, 0, 2, 3, 4).reshape(B, S, H, Dh)

def _stick_breaking_attention(q, k, v):
    B, S, H, Dh = q.shape
    nq = S // BLOCK
    scale = HEAD_DIM ** -0.5
    qb = q.reshape(B, nq, BLOCK, H, Dh).transpose(1, 0, 2, 3, 4)
    kpos = jnp.arange(S)

    def block(args):
        qblk, start = args
        z = jnp.einsum('bqhd,bkhd->bhqk', qblk, k).astype(jnp.float32) * scale
        qpos = start + jnp.arange(BLOCK)
        mask = kpos[None, :] < qpos[:, None]
        log_keep = jnp.where(mask, jax.nn.log_sigmoid(-z), 0.0)
        tail = lax.cumsum(log_keep, axis=3, reverse=True) - log_keep
        a = jnp.where(mask, jnp.exp(jax.nn.log_sigmoid(z) + tail), 0.0)
        return jnp.einsum('bhqk,bkhd->bqhd', a.astype(v.dtype), v).astype(jnp.float32)

    out = lax.map(block, (qb, jnp.arange(nq) * BLOCK))
    return out.transpose(1, 0, 2, 3, 4).reshape(B, S, H, Dh)

def _token_mixer(u, w_in, forget_bias, head_norm, w_out):
    B, S, D = u.shape
    proj = jnp.einsum('bsd,de->bse', u, w_in)
    q = proj[..., :D].reshape(B, S, N_HEADS, HEAD_DIM)
    k = proj[..., D:2 * D].reshape(B, S, N_HEADS, HEAD_DIM)
    v = proj[..., 2 * D:3 * D].reshape(B, S, N_HEADS, HEAD_DIM)
    f_logit = proj[..., 3 * D:].astype(jnp.float32) + forget_bias.astype(jnp.float32)
    log_f_cum = lax.cumsum(jax.nn.log_sigmoid(f_logit), axis=1)

    a, b = H_DIL, H_DIL + H_FOX
    o_dil = _dilated_attention(q[:, :, :a], k[:, :, :a], v[:, :, :a])
    o_fox = _fox_attention(q[:, :, a:b], k[:, :, a:b], v[:, :, a:b], log_f_cum)
    o_sb = _stick_breaking_attention(q[:, :, b:], k[:, :, b:], v[:, :, b:])
    o = jnp.concatenate([o_dil, o_fox, o_sb], axis=2)
    o = o * lax.rsqrt(jnp.mean(o * o, axis=-1, keepdims=True) + EPS)
    o = o * head_norm.astype(jnp.float32).reshape(N_HEADS, HEAD_DIM)
    o = o.astype(u.dtype).reshape(B, S, D)
    return jnp.einsum('bsd,de->bse', o, w_out)

def _swiglu(u, w_gate, w_up, w_down):
    hid = jax.nn.silu(jnp.einsum('bsd,df->bsf', u, w_gate)) * jnp.einsum('bsd,df->bsf', u, w_up)
    return jnp.einsum('bsf,fd->bsd', hid, w_down)

def _moe(u, router_w, w_gate, w_up, w_down):
    logits = jnp.einsum('bsd,de->bse', u, router_w).astype(jnp.float32)
    top_val, top_idx = lax.top_k(logits, TOP_K)
    gates = jax.nn.softmax(top_val, axis=-1)
    combine = jnp.sum(jax.nn.one_hot(top_idx, N_EXPERTS, dtype=jnp.float32) * gates[..., None], axis=-2)
    y = combine[..., 0:1] * _swiglu(u, w_gate[0], w_up[0], w_down[0]).astype(jnp.float32)
    for e in range(1, N_EXPERTS):
        y = y + combine[..., e:e + 1] * _swiglu(u, w_gate[e], w_up[e], w_down[e]).astype(jnp.float32)
    return y.astype(u.dtype)

def setup_inputs(seed: int = 0) -> dict:
    key = jax.random.key(seed)
    ks = jax.random.split(key, 16)
    f32 = jnp.float32
    sd = D_MODEL ** -0.5
    sf = D_FF ** -0.5
    return {
        "x": jax.random.normal(ks[0], (BATCH, SEQ, D_MODEL), f32),
        "mix_norm": 1.0 + 0.05 * jax.random.normal(ks[1], (DEPTH, D_MODEL), f32),
        "w_in": sd * jax.random.normal(ks[2], (DEPTH, D_MODEL, PROJ_OUT), f32),
        "forget_bias": 1.0 + 0.5 * jax.random.normal(ks[3], (DEPTH, H_FOX), f32),
        "head_norm": 1.0 + 0.05 * jax.random.normal(ks[4], (DEPTH, D_MODEL), f32),
        "w_out": sd * jax.random.normal(ks[5], (DEPTH, D_MODEL, D_MODEL), f32),
        "ffn_norm": 1.0 + 0.05 * jax.random.normal(ks[6], (DEPTH, D_MODEL), f32),
        "dense_w_gate": sd * jax.random.normal(ks[7], (N_DENSE, D_MODEL, D_FF), f32),
        "dense_w_up": sd * jax.random.normal(ks[8], (N_DENSE, D_MODEL, D_FF), f32),
        "dense_w_down": sf * jax.random.normal(ks[9], (N_DENSE, D_FF, D_MODEL), f32),
        "router_w": sd * jax.random.normal(ks[10], (N_MOE, D_MODEL, N_EXPERTS), f32),
        "moe_w_gate": sd * jax.random.normal(ks[11], (N_MOE, N_EXPERTS, D_MODEL, D_FF), f32),
        "moe_w_up": sd * jax.random.normal(ks[12], (N_MOE, N_EXPERTS, D_MODEL, D_FF), f32),
        "moe_w_down": sf * jax.random.normal(ks[13], (N_MOE, N_EXPERTS, D_FF, D_MODEL), f32),
        "final_norm": 1.0 + 0.05 * jax.random.normal(ks[14], (D_MODEL,), f32),
    }

def reference(x, mix_norm, w_in, forget_bias, head_norm, w_out, ffn_norm,
              dense_w_gate, dense_w_up, dense_w_down, router_w,
              moe_w_gate, moe_w_up, moe_w_down, final_norm):
    h = x
    for layer in range(DEPTH):
        u = _rmsnorm(h, mix_norm[layer])
        h = h + _token_mixer(u, w_in[layer], forget_bias[layer], head_norm[layer], w_out[layer])
        u = _rmsnorm(h, ffn_norm[layer])
        if layer % 2 == 0:
            i = layer // 2
            h = h + _swiglu(u, dense_w_gate[i], dense_w_up[i], dense_w_down[i])
        else:
            i = layer // 2
            h = h + _moe(u, router_w[i], moe_w_gate[i], moe_w_up[i], moe_w_down[i])
    return _rmsnorm(h, final_norm)


_drawn_inputs = setup_inputs


def setup_inputs(seed=0):
    import zlib

    import numpy as np

    out = dict(_drawn_inputs(seed))
    spreads = {}
    factors = {}
    for name, (base, spread) in spreads.items():
        noise = np.random.default_rng([zlib.crc32(name.encode()), seed]).standard_normal(out[name].shape)
        drawn = base * np.exp(spread * noise) if base else spread * noise
        out[name] = __import__('jax').numpy.asarray(drawn.astype(out[name].dtype))
    for name, factor in factors.items():
        out[name] = (out[name] * factor).astype(out[name].dtype)
    return out
```

```python
from contextlib import ExitStack

import concourse.bass as bass
from concourse import mybir

F32 = mybir.dt.float32
F32R = mybir.dt.float32r
BF16 = mybir.dt.bfloat16
I32 = mybir.dt.int32
ALU = mybir.AluOpType
ACT = mybir.ActivationFunctionType
AX_X = mybir.AxisListType.X

P = 128
HEAD_DIM = 64
DIL_PATTERNS = ((128, 1), (512, 4), (2048, 16))
TOP_K = 2
EPS = 1e-6
MASKED = -1e30


def hybrid_trunk(nc, x, mix_norm, w_in, forget_bias, head_norm, w_out, ffn_norm,
                 dense_w_gate, dense_w_up, dense_w_down, router_w,
                 moe_w_gate, moe_w_up, moe_w_down, final_norm, out, slots=P):
    _, S, D = x.shape
    DEPTH = mix_norm.shape[0]
    H_FOX = forget_bias.shape[1]
    HEADS = D // HEAD_DIM
    H_DIL = HEADS * 3 // 8
    H_SB = HEADS - H_DIL - H_FOX
    FF = dense_w_gate.shape[2]
    EXPERTS = moe_w_gate.shape[1]
    TB = S // P
    KC = D // P
    HALF = D // 2
    assert DEPTH == 2 and TB == 2 and D == 1024 and HALF == 512 and FF % 256 == 0
    SCALE = HEAD_DIM ** -0.5
    SOFT = H_DIL + H_FOX

    UNIT = 2048
    QK_UNITS, V_UNITS, OUT_UNITS = 2 * D // 256, 4, 4
    MIX_UNITS = QK_UNITS + V_UNITS + OUT_UNITS
    STEPS = FF // 256
    FFN_UNITS = 3 * STEPS
    PAIRS = (STEPS - 1) // 2
    assert STEPS % 2 == 1 and STEPS >= 5 and MIX_UNITS == 16
    MIX_BASE = [0, MIX_UNITS + FFN_UNITS]
    DENSE_BASE = MIX_UNITS
    MOE_BASE = 2 * MIX_UNITS + FFN_UNITS
    SPLITS = 3

    HEAD_ORDER = list(range(HEADS))
    slot_cols = 3 * P

    ctx = ExitStack()
    with ctx:
        def sb(name, shape, dt, stack=ctx):
            return stack.enter_context(nc.sbuf_tensor(name, shape, dt))

        def sem(name):
            return ctx.enter_context(nc.semaphore(name))

        raw = sb("raw", [P, 9, UNIT], F32)
        w_high = sb("w_high", [P, SPLITS, UNIT], F32R)
        w_low = sb("w_low", [P, SPLITS, UNIT], F32R)
        resid = sb("resid", [P, TB, D], F32)
        rows = sb("rows", [P, TB, D], F32)
        gain = sb("gain", [P, D], F32)
        act_high = sb("act_high", [P, KC, S], F32R)
        act_low = sb("act_low", [P, KC, S], F32R)
        ident = sb("ident", [P, P], F32)
        iota_row = sb("iota_row", [P, P], F32)
        upto = sb("upto", [P, P], F32)
        before = sb("before", [P, P], F32)
        since = sb("since", [P, P], F32)
        ones = sb("ones", [P, P], F32)
        causal = sb("causal", [P, slot_cols], BF16)
        strict_t = sb("strict_t", [P, slot_cols], BF16)
        dil_dist = sb("dil_dist", [P, slot_cols], BF16)
        dil_times = sb("dil_times", [P, slot_cols], BF16)
        small_raw = sb("small_raw", [P, KC, EXPERTS], F32)
        small_high = sb("small_high", [P, KC, EXPERTS], F32R)
        small_low = sb("small_low", [P, KC, EXPERTS], F32R)
        forget_raw = sb("forget_raw", [P, KC, H_FOX + 1], F32)
        forget_high = sb("forget_high", [P, KC, H_FOX + 1], F32R)
        forget_low = sb("forget_low", [P, KC, H_FOX + 1], F32R)
        bias_row = sb("bias_row", [P, H_FOX], F32)
        ssq = sb("ssq", [P, TB], F32)
        rstd = sb("rstd", [P, TB], F32)
        half_power = sb("half_power", [P, TB * HEADS], F32)
        head_ssq = sb("head_ssq", [P, TB * HEADS], F32)
        head_rstd = sb("head_rstd", [P, TB * HEADS], F32)
        neg_max = sb("neg_max", [P, TB, HEADS], F32)
        den = sb("den", [P, TB, HEADS], F32)
        rden = sb("rden", [P, TB, HEADS], F32)
        f_logit = sb("f_logit", [P, TB, H_FOX], F32)
        f_soft = sb("f_soft", [P, TB, H_FOX], F32)
        f_log = sb("f_log", [P, TB, H_FOX], F32)

        mixer = ExitStack()
        q_t = sb("q_t", [P, KC, S], F32, mixer)
        k_t = sb("k_t", [P, KC, S], F32, mixer)
        v_rows = sb("v_rows", [P, TB, D], F32, mixer)
        prob = sb("prob", [P, 3, slot_cols], F32, mixer)
        stick = sb("stick", [P, 3, slot_cols], F32, mixer)
        prob_t = sb("prob_t", [P, 2, slot_cols], F32, mixer)
        alibi = sb("alibi", [P, 2, slot_cols], F32, mixer)
        forget_pos = sb("forget_pos", [H_FOX, S], F32, mixer)
        forget_neg = sb("forget_neg", [H_FOX, S], F32, mixer)
        pick = sb("pick", [H_FOX, H_FOX, P], F32, mixer)
        dist_i = alibi[:, 0, :].bitcast(I32)
        mixer.close()
        ffn = ExitStack()
        gated = sb("gated", [P, TB, 256], F32, ffn)
        hidden = sb("hidden", [P, TB, 256], F32, ffn)
        hid_high = sb("hid_high", [P, 2, S], F32R, ffn)
        hid_low = sb("hid_low", [P, 2, S], F32R, ffn)
        rows_high = sb("rows_high", [P, TB, D], F32R, ffn)
        rows_low = sb("rows_low", [P, TB, D], F32R, ffn)
        y_high = sb("y_high", [P, D], F32R, ffn)
        y_low = sb("y_low", [P, D], F32R, ffn)
        take = sb("take", [P, TB, P], F32R, ffn)
        give = sb("give", [P, S], F32R, ffn)
        logits = sb("logits", [P, TB, EXPERTS], F32, ffn)
        beats = sb("beats", [P, TB, EXPERTS, EXPERTS], F32, ffn)
        ties = sb("ties", [P, TB, EXPERTS, EXPERTS], F32, ffn)
        place = sb("place", [P, TB, EXPERTS], F32, ffn)
        chosen = sb("chosen", [P, TB, EXPERTS], F32, ffn)
        top = sb("top", [P, TB], F32, ffn)
        gate = sb("gate", [P, TB, EXPERTS], F32, ffn)
        gate_sum = sb("gate_sum", [P, TB], F32, ffn)
        rank = sb("rank", [P, TB, EXPERTS], F32, ffn)
        most = sb("most", [P, 1], F32, ffn)
        spill = sb("spill", [P, 1], I32, ffn)
        earlier = sb("earlier", [P, TB, EXPERTS, EXPERTS], F32, ffn)
        ffn.close()

        psum = ctx.enter_context(nc.psum_tensor("psum", [P, 8, 512], F32))

        x_loaded = sem("x_loaded")
        small_loaded = sem("small_loaded")
        router_loaded = sem("router_loaded")
        gain_loaded = sem("gain_loaded")
        landed = [sem(f"unit_landed_{s}") for s in range(9)]
        high_done = sem("high_done")
        low_done = sem("low_done")
        used = sem("used")
        const_done = sem("const_done")
        dist_ready = sem("dist_ready")
        table_chain = sem("table_chain")
        tables_done = sem("tables_done")
        small_high_done = sem("small_high_done")
        small_low_done = sem("small_low_done")
        squares = sem("squares")
        scale_ready = sem("scale_ready")
        pool_chain = sem("pool_chain")
        normed = sem("normed")
        turned = sem("turned")
        act_high_done = sem("act_high_done")
        act_low_done = sem("act_low_done")
        resid_done = sem("resid_done")
        f_done = sem("f_done")
        f_chain = sem("f_chain")
        f_soft_done = sem("f_soft_done")
        f_act_chain = sem("f_act_chain")
        f_log_done = sem("f_log_done")
        c_done = sem("c_done")
        c_copied = sem("c_copied")
        qk_copied = sem("qk_copied")
        v_copied = sem("v_copied")
        alibi_done = sem("alibi_done")
        pick_chain = sem("pick_chain")
        pick_done = sem("pick_done")
        scores = sem("scores")
        masked = sem("masked")
        expd = sem("expd")
        stick_chain = sem("stick_chain")
        weighed = sem("weighed")
        flipped = sem("flipped")
        arg_done = sem("arg_done")
        weights_t = sem("weights_t")
        mixed = sem("mixed")
        den_done = sem("den_done")
        o_scaled = sem("o_scaled")
        o_squares = sem("o_squares")
        o_summed = sem("o_summed")
        o_rstd_done = sem("o_rstd_done")
        o_normed = sem("o_normed")
        activated = sem("activated")
        hidden_done = sem("hidden_done")
        hid_turned = sem("hid_turned")
        hid_high_done = sem("hid_high_done")
        hid_low_done = sem("hid_low_done")
        rows_high_done = sem("rows_high_done")
        rows_low_done = sem("rows_low_done")
        logits_done = sem("logits_done")
        route_chain = sem("route_chain")
        shifted = sem("shifted")
        gate_exp = sem("gate_exp")
        chosen_done = sem("chosen_done")
        ranked = sem("ranked")
        spill_done = sem("spill_done")
        take_done = sem("take_done")
        gathered = sem("gathered")
        x_high_done = sem("x_high_done")
        x_low_done = sem("x_low_done")
        take_turned = sem("take_turned")
        give_done = sem("give_done")
        y_high_done = sem("y_high_done")
        y_low_done = sem("y_low_done")
        scattered = sem("scattered")
        summed = sem("summed")
        moe_done = sem("moe_done")
        stored = sem("stored")

        MIX_SLOTS = [0, 1, 3, 4, 5, 6, 7, 8]
        FIRST, LAST, RING_A, RING_B = (0, 1), 2, (3, 4, 5), (6, 7, 8)
        mix_loads = [2 * 16 if s != LAST else 0 for s in range(9)]
        ffn_loads = [32, 32, 16] + [PAIRS * 32, PAIRS * 32, PAIRS * 16] * 2
        at_mix = [[0] * 9, [mix_loads[s] + ffn_loads[s] for s in range(9)]]
        at_dense = mix_loads
        at_moe = [at_mix[1][s] + mix_loads[s] for s in range(9)]

        def mix_landed(layer, i):
            s = MIX_SLOTS[i % 8]
            return s, at_mix[layer][s] + 16 * (i // 8 + 1)

        def split_slot(base, i):
            return (base + i) % SPLITS

        def bank(i):
            return psum[:, i, :]

        def wrow(w, k0, kn, c0, cn):
            return w.rearrange("(k p) n -> p k n", p=P)[:, k0:k0 + kn, c0:c0 + cn]

        def raw_view(s, a):
            return raw[:, s, :].rearrange("p (a n) -> p a n", a=a)

        dil_slopes = [2.0 ** (-8.0 * (h + 1) / H_DIL) for h in range(H_DIL)]

        def kind(h):
            return "dil" if h < H_DIL else ("fox" if h < SOFT else "stick")

        def count_of(i, *kinds):
            return sum(kind(h) in kinds for h in HEAD_ORDER[:i + 1])

        def stick_before(layer, i):
            return layer * H_SB + (count_of(i - 3, "stick") if i >= 3 else 0)

        block = ctx.enter_context(nc.Block())

        @block.sync
        def _(sp):
            sp.dma_start(resid[:, :, :], x.rearrange("b (t p) d -> p (b t) d", p=P)).then_inc(x_loaded, 16)

            def mixer_units(layer):
                base = MIX_BASE[layer]
                for i in range(MIX_UNITS):
                    if i < QK_UNITS:
                        src, a = wrow(w_in[layer], 0, KC, i * 256, 256), KC
                    elif i < QK_UNITS + V_UNITS:
                        n = i - QK_UNITS
                        src, a = wrow(w_in[layer], 4 * (n % 2), 4, 2 * D + n // 2 * 512, 512), 4
                    else:
                        n = i - QK_UNITS - V_UNITS
                        src, a = wrow(w_out[layer], 4 * (n % 2), 4, n // 2 * 512, 512), 4
                    s, _ = mix_landed(layer, i)
                    if base + i >= 8:
                        sp.wait_ge(low_done, base + i - 7)
                    sp.dma_start(raw_view(s, a), src).then_inc(landed[s], 16)

            def gate_up_unit(w_gate, w_up, s, step, k0, number, back):
                sp.wait_ge(low_done, number - back)
                for w, c0 in ((w_gate, 0), (w_up, 256)):
                    src = w.rearrange("(k p) f -> p k f", p=P)[:, k0:k0 + 4, bass.ds(step * 256, 256)]
                    sp.dma_start(raw_view(s, 4)[:, :, c0:c0 + 256], src).then_inc(landed[s], 16)

            def down_unit(w_down, s, step, number, back):
                sp.wait_ge(low_done, number - back)
                src = w_down.rearrange("(j c p) n -> j p c n", c=2, p=P)[step]
                sp.dma_start(raw_view(s, 2), src).then_inc(landed[s], 16)

            def ffn_units(w_gate, w_up, w_down, base):
                for k in range(2):
                    gate_up_unit(w_gate, w_up, FIRST[k], 0, 4 * k, base + k, 7)
                with sp.Fori(0, PAIRS) as it:
                    for c, ring in enumerate((RING_A, RING_B)):
                        step = 2 * it + (1 + c)
                        number = base + it * 6 + (2 + 3 * c)
                        gate_up_unit(w_gate, w_up, ring[0], step, 0, number, 5)
                        gate_up_unit(w_gate, w_up, ring[1], step, 4, number + 1, 5)
                        down_unit(w_down, ring[2], step - 1, number + 2, 5)
                down_unit(w_down, LAST, STEPS - 1, base + FFN_UNITS - 1, 5)

            mixer_units(0)
            ffn_units(dense_w_gate[0], dense_w_up[0], dense_w_down[0], DENSE_BASE)
            mixer_units(1)

            def experts(base):
                with sp.Fori(0, EXPERTS) as e:
                    ffn_units(moe_w_gate[0, e], moe_w_up[0, e], moe_w_down[0, e], base + e * FFN_UNITS)

            experts(MOE_BASE)
            sp.wait_ge(spill_done, 1)
            with sp.If(sp.value_load(spill[0:1, 0:1], min_val=0, max_val=1) > 0):
                experts(MOE_BASE + EXPERTS * FFN_UNITS)

            sp.wait_ge(normed, 2 * 7)
            sp.dma_start(out.rearrange("b (t p) d -> p (b t) d", p=P), rows[:, :, :]).then_inc(stored, 16)
            sp.wait_ge(stored, 16)

        @block.gpsimd
        def _(pool):
            def load_gain(g):
                src = [mix_norm[0], head_norm[0], ffn_norm[0], mix_norm[1], head_norm[1], ffn_norm[1],
                       final_norm][g]
                if g:
                    pool.wait_ge(normed, 2 * g)
                pool.dma_start(gain[:, :], src.partition_broadcast(P)).then_inc(gain_loaded, 16)

            def load_forget(layer):
                pool.dma_start(forget_raw[:, :, 0:H_FOX], wrow(w_in[layer], 0, KC, 3 * D, H_FOX)
                               ).then_inc(small_loaded, 16)
                pool.dma_start(bias_row[:, :], forget_bias[layer].partition_broadcast(P)).then_inc(small_loaded, 16)

            load_gain(0)
            pool.memset(forget_raw[:, :, :], 0.0).then_inc(const_done, 1)
            pool.wait_ge(const_done, 1)
            load_forget(0)
            pool.dma_start(small_raw[:, :, :], router_w[0].rearrange("(k p) e -> p k e", p=P)).then_inc(router_loaded, 16)

            n = [1]

            def chain(ins):
                n[0] += 1
                ins.then_inc(const_done, 1)
                pool.wait_ge(const_done, n[0])

            chain(pool.memset(half_power[:, :], -0.5))
            chain(pool.memset(ones[:, :], 1.0))
            chain(pool.iota(iota_row[:, :], [[1, P]], base=0, channel_multiplier=0,
                            allow_small_or_imprecise_dtypes=True))
            ge, gt, eq = ALU.is_ge, ALU.is_gt, ALU.is_equal
            for t, cmp, cm, step in ((ident, eq, 1, -1), (upto, ge, -1, 1), (before, gt, -1, 1), (since, ge, 1, -1)):
                chain(pool.affine_select(out=t[:, :], in_=ones[:, :], compare_op=cmp, fill=0.0, base=0,
                                         pattern=[[step, P]], channel_multiplier=cm))
            chain(pool.memset(causal[:, :], 0.0))
            chain(pool.affine_select(out=causal[:, 0:P], in_=causal[:, 0:P], compare_op=ge, fill=MASKED, base=0,
                                     pattern=[[-1, P]], channel_multiplier=1))
            chain(pool.affine_select(out=causal[:, P:], in_=causal[:, P:], compare_op=ge, fill=MASKED, base=P,
                                     pattern=[[-1, S]], channel_multiplier=1))
            chain(pool.memset(strict_t[:, :], 0.0))
            chain(pool.affine_select(out=strict_t[:, 0:S], in_=strict_t[:, 0:S], compare_op=gt, fill=MASKED, base=0,
                                     pattern=[[1, S]], channel_multiplier=-1))
            chain(pool.affine_select(out=strict_t[:, S:], in_=strict_t[:, S:], compare_op=gt, fill=MASKED, base=0,
                                     pattern=[[1, P]], channel_multiplier=-1))
            chain(pool.iota(dist_i[:, 0:P], [[-1, P]], base=0, channel_multiplier=1))
            pool.iota(dist_i[:, P:], [[-1, S]], base=P, channel_multiplier=1).then_inc(dist_ready, 1)

            def scale_of(count):
                pool.wait_ge(squares, 2 * count)
                pool.tensor_scalar(ssq[:, :], ssq[:, :], 1.0 / D, EPS, ALU.mult, ALU.add).then_inc(pool_chain, 1)
                pool.wait_ge(pool_chain, count + 0 + pool_extra[0])
                pool.tensor_tensor(rstd[:, :], ssq[:, :], half_power[:, 0:TB], ALU.pow).then_inc(scale_ready, 1)

            pool_extra = [0]
            for layer in range(DEPTH):
                scale_of(2 * layer + 1)
                load_gain(3 * layer + 1)
                pool.memset(pick[:, :, :], 1.0).then_inc(pick_chain, 1)
                pool.wait_ge(pick_chain, layer + 1)
                pool.affine_select(out=pick[:, :, :], in_=pick[:, :, :], compare_op=eq, fill=0.0, base=0,
                                   pattern=[[-1, H_FOX], [0, P]], channel_multiplier=1).then_inc(pick_done, 1)
                if layer == 0:
                    pool.wait_ge(tables_done, 1)
                for i, h in enumerate(HEAD_ORDER):
                    if kind(h) != "dil":
                        continue
                    m = layer * H_DIL + count_of(i, "dil")
                    if layer * HEADS + i >= 2:
                        pool.wait_ge(masked, layer * HEADS + i - 1)
                    elif layer:
                        pool.wait_ge(masked, layer * HEADS)
                    pool.tensor_scalar(alibi[:, m % 2, :], dil_dist[:, :], -dil_slopes[h], None, ALU.mult
                                       ).then_inc(alibi_done, 1)
                pool.wait_ge(o_summed, layer + 1)
                pool.tensor_scalar(head_ssq[:, :], head_ssq[:, :], 1.0 / HEAD_DIM, EPS, ALU.mult, ALU.add
                                   ).then_inc(pool_chain, 1)
                pool_extra[0] += 1
                pool.wait_ge(pool_chain, 2 * layer + 1 + pool_extra[0])
                pool.tensor_tensor(head_rstd[:, :], head_ssq[:, :], half_power[:, :], ALU.pow).then_inc(o_rstd_done, 1)
                load_gain(3 * layer + 2)
                if layer + 1 < DEPTH:
                    pool.wait_ge(small_high_done, layer + 1)
                    pool.wait_ge(small_low_done, layer + 1)
                    pool.wait_ge(f_chain, layer + 1)
                    load_forget(layer + 1)
                scale_of(2 * layer + 2)
                load_gain(3 * layer + 3)
            scale_of(2 * DEPTH + 1)

        @block.scalar
        def _(act):
            def high(slot, need, number, split):
                act.wait_ge(landed[slot], need)
                if not (isinstance(number, int) and number < SPLITS):
                    act.wait_ge(used, number - (SPLITS - 1))
                act.activation(w_high[:, split, :], raw[:, slot, :], ACT.Copy).then_inc(high_done, 1)

            def mix_high(layer, i):
                slot, need = mix_landed(layer, i)
                high(slot, need, MIX_BASE[layer] + i, split_slot(MIX_BASE[layer], i))

            def sum_squares(count, waits):
                if waits:
                    act.wait_ge(resid_done, waits)
                    act.wait_ge(turned, 4 * (3 * (count - 1) // 2 + (count - 1) % 2))
                else:
                    act.wait_ge(x_loaded, 16)
                for t in range(TB):
                    act.activation(rows[:, t, :], resid[:, t, :], ACT.Square,
                                   accum_out=ssq[:, t:t + 1]).then_inc(squares, 1)

            def split_turned(times):
                for b in range(4):
                    act.wait_ge(turned, 4 * times + b + 1)
                    act.activation(act_high[:, 2 * b:2 * b + 2, :].rearrange("p k s -> p (k s)"), bank(b),
                                   ACT.Copy).then_inc(act_high_done, 1)

            def attention(layer):
                H0 = layer * HEADS

                def exps(i):
                    h = HEAD_ORDER[i]
                    act.wait_ge(masked, H0 + i + 1)
                    if kind(h) != "stick":
                        for t, (a, b) in enumerate(((0, P), (P, 3 * P))):
                            p = prob[:, i % 3, a:b]
                            acc = {"accum_out": den[:, t, h:h + 1]} if kind(h) == "fox" else {}
                            ins = act.activation(p, p, ACT.Exp, bias=neg_max[:, t, h:h + 1], scale=-1.0, **acc)
                        ins.then_inc(expd, 1)
                        return
                    m = 2 * (layer * H_SB + count_of(i, "stick") - 1)
                    if H0 + i >= 3:
                        act.wait_ge(flipped, H0 + i - 2)
                        act.wait_ge(weights_t, H0 + i - 2)
                    st = stick[:, i % 3, :]
                    act.activation(st, prob[:, i % 3, :], ACT.Abs).then_inc(stick_chain, 1)
                    act.wait_ge(stick_chain, m + 1)
                    act.activation(st, st, ACT.Exp, scale=-1.0).then_inc(stick_chain, 1)
                    act.wait_ge(stick_chain, m + 2)
                    act.activation(st, st, ACT.Ln, bias=1.0).then_inc(expd, 1)

                def turn(i):
                    h = HEAD_ORDER[i]
                    act.wait_ge(flipped, H0 + i + 1)
                    if i >= 2:
                        act.wait_ge(mixed, H0 + i - 1)
                    if kind(h) != "stick":
                        act.activation(prob_t[:, i % 2, :], bank(2 + i % 2)[:, 0:slot_cols], ACT.Copy
                                       ).then_inc(weights_t, 1)
                    else:
                        act.wait_ge(arg_done, layer * H_SB + count_of(i, "stick"))
                        act.activation(prob_t[:, i % 2, :], stick[:, i % 3, :], ACT.Exp).then_inc(weights_t, 1)

                for s in range(HEADS + 2):
                    if s < HEADS:
                        exps(s)
                    if s >= 2:
                        turn(s - 2)

            def mix(layer):
                sum_squares(2 * layer + 1, 8 * layer)
                if layer == 0:
                    act.wait_ge(small_loaded, 32)
                else:
                    act.wait_ge(small_loaded, 64)
                act.activation(forget_high[:, :, :], forget_raw[:, :, :], ACT.Copy).then_inc(small_high_done, 1)
                for i in range(SPLITS):
                    mix_high(layer, i)
                split_turned(3 * layer)
                act.wait_ge(f_chain, layer + 1)
                act.activation(f_soft[:, :, :], f_logit[:, :, :], ACT.Abs).then_inc(f_act_chain, 1)
                act.wait_ge(f_act_chain, 2 * layer + 1)
                act.activation(f_soft[:, :, :], f_soft[:, :, :], ACT.Exp, scale=-1.0).then_inc(f_act_chain, 1)
                act.wait_ge(f_act_chain, 2 * layer + 2)
                act.activation(f_soft[:, :, :], f_soft[:, :, :], ACT.Ln, bias=1.0).then_inc(f_soft_done, 1)
                for i in range(QK_UNITS):
                    act.wait_ge(used, MIX_BASE[layer] + i + 1)
                    dst, c = (q_t, i) if i < QK_UNITS // 2 else (k_t, i - QK_UNITS // 2)
                    act.activation(dst[:, 2 * c:2 * c + 2, :].rearrange("p k s -> p (k s)"), bank(i % 4), ACT.Copy,
                                   scale=SCALE if i < QK_UNITS // 2 else 1.0).then_inc(qk_copied, 1)
                    mix_high(layer, i + SPLITS)
                for i in range(QK_UNITS, QK_UNITS + V_UNITS):
                    mix_high(layer, i + SPLITS)
                attention(layer)
                for t in range(TB):
                    act.wait_ge(o_scaled, 4 * layer + 2 * t + 2)
                    act.activation(k_t[:, 4 * t:4 * t + 4, :].rearrange("p k s -> p (k s)"), rows[:, t, :],
                                   ACT.Square).then_inc(o_squares, 1)
                split_turned(3 * layer + 1)
                mix_high(layer, MIX_UNITS - 1)

            def ffn_steps(base, first_step, blocks, need):
                def unit_high(i, number, slot, times):
                    high(slot, need(slot, times), number, split_slot_of(i))

                def split_slot_of(i):
                    return (stage_split + i) % SPLITS

                stage_split = base_split(base)

                def step(j, number, count, ring, times):
                    o = 2 if not isinstance(j, int) else 3 * j - 1
                    if ring is not None:
                        unit_high(o + 3, number + 3, ring[0], times)
                    act.wait_ge(used, number + 2)
                    act.wait_ge(hidden_done, count)
                    act.activation(gated[:, 0:blocks, :], psum[:, 0:blocks, 0:256], ACT.Silu).then_inc(activated, 1)
                    if ring is not None and len(ring) > 1:
                        unit_high(o + 4, number + 4, ring[1], times)
                    act.wait_ge(hid_turned, count + 1)
                    act.activation(hid_high[:, :, 0:blocks * P], bank(2)[:, 0:2 * blocks * P]
                                   .rearrange("p (c s) -> p c s", c=2), ACT.Copy).then_inc(hid_high_done, 1)
                    if ring is not None and len(ring) > 2:
                        unit_high(o + 5, number + 5, ring[2], times)

                unit_high(0, base, FIRST[0], 1)
                unit_high(1, base + 1, FIRST[1], 1)
                unit_high(2, base + 2, RING_A[0], ring_times(base, 1))
                unit_high(3, base + 3, RING_A[1], ring_times(base, 1))
                act.wait_ge(used, base + 2)
                act.wait_ge(hidden_done, first_step)
                act.activation(gated[:, 0:blocks, :], psum[:, 0:blocks, 0:256], ACT.Silu).then_inc(activated, 1)
                unit_high(4, base + 4, RING_A[2], ring_times(base, 1))
                act.wait_ge(hid_turned, first_step + 1)
                act.activation(hid_high[:, :, 0:blocks * P], bank(2)[:, 0:2 * blocks * P]
                               .rearrange("p (c s) -> p c s", c=2), ACT.Copy).then_inc(hid_high_done, 1)
                with act.Fori(0, PAIRS - 1) as it:
                    step(it, base + it * 6 + 2, first_step + it * 2 + 1, RING_B, it + 1)
                    step(it, base + it * 6 + 5, first_step + it * 2 + 2, RING_A, it + 2)
                step(STEPS - 2, base + 3 * (STEPS - 2) - 1, first_step + STEPS - 2, RING_B, PAIRS)
                step(STEPS - 1, base + 3 * (STEPS - 1) - 1, first_step + STEPS - 1, (LAST,), 1)

            def base_split(base):
                return base_mod[0]

            def ring_times(base, t):
                return t

            base_mod = [0]

            mix(0)
            sum_squares(2, 4)
            split_turned(2)
            base_mod[0] = DENSE_BASE % SPLITS
            ffn_steps(DENSE_BASE, 0, TB, lambda s, t: at_dense[s] + (16 if s in (LAST, 5, 8) else 32) * t)
            mix(1)
            sum_squares(4, 12)
            act.wait_ge(router_loaded, 16)
            act.activation(small_high[:, :, :], small_raw[:, :, :], ACT.Copy).then_inc(small_high_done, 1)
            split_turned(5)
            for t in range(TB):
                act.activation(rows_high[:, t, :], rows[:, t, :], ACT.Copy).then_inc(rows_high_done, 1)
            act.wait_ge(shifted, 1)
            act.activation(gate[:, :, :], gate[:, :, :], ACT.Exp).then_inc(gate_exp, 1)

            def experts(number):
                unit0 = MOE_BASE + number * EXPERTS * FFN_UNITS
                base_mod[0] = unit0 % SPLITS
                with act.Fori(0, EXPERTS) as e:
                    n = e + number * EXPERTS
                    act.wait_ge(gathered, n + 1)
                    for b, g in enumerate((1, 3)):
                        act.activation(act_high[:, 4 * b:4 * b + 4, 0:P], bank(g)
                                       .rearrange("p (k s) -> p k s", k=4), ACT.Copy).then_inc(x_high_done, 1)
                    act.wait_ge(take_turned, n + 1)
                    act.activation(give[:, :], bank(2)[:, 0:S], ACT.Copy).then_inc(give_done, 1)

                    def need(s, t):
                        each = 16 if s in (LAST, 5, 8) else 32
                        per = 1 if s < 3 else PAIRS
                        return (n * per + t) * each + at_moe[s]

                    ffn_steps(unit0 + e * FFN_UNITS, STEPS + n * STEPS, 1, need)
                    act.wait_ge(used, unit0 + e * FFN_UNITS + FFN_UNITS)
                    act.activation(y_high[:, :], psum[:, 4:6, :].rearrange("p b n -> p (b n)"), ACT.Copy
                                   ).then_inc(y_high_done, 1)

            experts(0)
            act.wait_ge(spill_done, 1)
            with act.If(act.value_load(spill[0:1, 0:1], min_val=0, max_val=1) > 0):
                experts(1)
            act.wait_ge(moe_done, 1)
            for t in range(TB):
                act.activation(rows[:, t, :], resid[:, t, :], ACT.Square,
                               accum_out=ssq[:, t:t + 1]).then_inc(squares, 1)

        @block.vector
        def _(dve):
            def low(slot, number, split):
                dve.wait_ge(high_done, number + 1)
                dve.tensor_tensor(w_low[:, split, :], raw[:, slot, :], w_high[:, split, :].bitcast(F32),
                                  ALU.subtract).then_inc(low_done, 1)

            def mix_low(layer, i):
                slot, _ = mix_landed(layer, i)
                low(slot, MIX_BASE[layer] + i, split_slot(MIX_BASE[layer], i))

            def norm(count, use):
                dve.wait_ge(scale_ready, count)
                dve.wait_ge(gain_loaded, 16 * use)
                for t in range(TB):
                    dve.scalar_tensor_tensor(rows[:, t, :], resid[:, t, :], rstd[:, t:t + 1], gain[:, :],
                                             ALU.mult, ALU.mult).then_inc(normed, 1)

            def split_turned(times):
                for b in range(4):
                    dve.wait_ge(act_high_done, 4 * times + b + 1)
                    hi = act_high[:, 2 * b:2 * b + 2, :].rearrange("p k s -> p (k s)")
                    lo = act_low[:, 2 * b:2 * b + 2, :].rearrange("p k s -> p (k s)")
                    dve.tensor_tensor(lo, bank(b), hi.bitcast(F32), ALU.subtract).then_inc(act_low_done, 1)

            def tables():
                n = [0]

                def chain(ins):
                    n[0] += 1
                    ins.then_inc(table_chain, 1)
                    dve.wait_ge(table_chain, n[0])

                dist, work, part = prob[:, 0, :], prob[:, 1, :], prob[:, 2, :]
                mod_i = stick[:, 0, :].bitcast(I32)
                dve.wait_ge(dist_ready, 1)
                chain(dve.tensor_copy(dist, dist_i))
                chain(dve.memset(work, 0.0))
                for window, dilation in DIL_PATTERNS:
                    assert dilation & (dilation - 1) == 0 and S % dilation == 0
                    chain(dve.tensor_scalar(mod_i, dist_i, dilation - 1, None, ALU.bitwise_and))
                    chain(dve.tensor_copy(part, mod_i))
                    chain(dve.tensor_scalar(part, part, 0.0, None, ALU.is_equal))
                    chain(dve.scalar_tensor_tensor(part, dist, float(window), part, ALU.is_le, ALU.mult))
                    chain(dve.tensor_tensor(work, work, part, ALU.add))
                chain(dve.scalar_tensor_tensor(work, dist, 0.0, work, ALU.is_ge, ALU.mult))
                chain(dve.tensor_copy(dil_times[:, :], work))
                chain(dve.tensor_scalar(part, work, 0.0, -MASKED, ALU.is_equal, ALU.mult))
                dve.tensor_tensor(dil_dist[:, :], part, dist, ALU.add).then_inc(tables_done, 1)

            def attention(layer):
                H0 = layer * HEADS

                def mask(i):
                    h = HEAD_ORDER[i]
                    dve.wait_ge(scores, H0 + i + 1)
                    if H0 + i >= 3:
                        dve.wait_ge(flipped, H0 + i - 2)
                        if stick_before(layer, i):
                            dve.wait_ge(arg_done, stick_before(layer, i))
                    sc = bank(i % 2)
                    if kind(h) == "stick":
                        dve.tensor_tensor(prob[:, i % 3, :], sc[:, 0:slot_cols], strict_t[:, :], ALU.add
                                          ).then_inc(masked, 1)
                        return
                    if kind(h) == "dil":
                        m = layer * H_DIL + count_of(i, "dil")
                        dve.wait_ge(alibi_done, m)
                        term = alibi[:, m % 2, :]
                    else:
                        term = causal[:, :]
                    for t, (a, b) in enumerate(((0, P), (P, 3 * P))):
                        ins = dve.tensor_tensor_reduce(prob[:, i % 3, a:b], sc[:, a:b], term[:, a:b], -1.0, 3e38,
                                                       ALU.add, ALU.min, neg_max[:, t, h:h + 1])
                    ins.then_inc(masked, 1)

                def weigh(i):
                    h = HEAD_ORDER[i]
                    if kind(h) == "fox":
                        return
                    dve.wait_ge(expd, H0 + i + 1)
                    if kind(h) == "dil":
                        for t, (a, b) in enumerate(((0, P), (P, 3 * P))):
                            p = prob[:, i % 3, a:b]
                            ins = dve.tensor_tensor_reduce(p, p, dil_times[:, a:b], 1.0, 0.0, ALU.mult, ALU.add,
                                                           den[:, t, h:h + 1])
                    else:
                        ins = dve.scalar_tensor_tensor(stick[:, i % 3, :], prob[:, i % 3, :], 0.0,
                                                       stick[:, i % 3, :], ALU.max, ALU.add)
                    ins.then_inc(weighed, 1)

                def subtract_tail(i):
                    if kind(HEAD_ORDER[i]) != "stick":
                        return
                    dve.wait_ge(flipped, H0 + i + 1)
                    dve.tensor_tensor(stick[:, i % 3, :], prob[:, i % 3, :], bank(2 + i % 2)[:, 0:slot_cols],
                                      ALU.subtract).then_inc(arg_done, 1)

                for s in range(HEADS + 2):
                    if s < HEADS:
                        mask(s)
                    if 1 <= s <= HEADS:
                        weigh(s - 1)
                    if s >= 2:
                        subtract_tail(s - 2)

            def mix(layer):
                base = MIX_BASE[layer]
                norm(2 * layer + 1, 3 * layer + 1)
                dve.wait_ge(small_high_done, layer + 1)
                dve.tensor_tensor(forget_low[:, :, :], forget_raw[:, :, :], forget_high[:, :, :].bitcast(F32),
                                  ALU.subtract).then_inc(small_low_done, 1)
                for i in range(SPLITS):
                    mix_low(layer, i)
                split_turned(3 * layer)
                dve.wait_ge(f_done, layer + 1)
                fl = bank(7)[:, 0:TB * 8].rearrange("p (t f) -> p t f", t=TB)[:, :, 0:H_FOX]
                dve.tensor_tensor(f_logit[:, :, :], fl, bias_row[:, :].unsqueeze(1).to_broadcast([P, TB, H_FOX]),
                                  ALU.add).then_inc(f_chain, 1)
                dve.wait_ge(f_soft_done, layer + 1)
                dve.scalar_tensor_tensor(f_log[:, :, :], f_logit[:, :, :], 0.0, f_soft[:, :, :],
                                         ALU.min, ALU.subtract).then_inc(f_log_done, 1)
                dve.wait_ge(c_done, layer + 1)
                dve.tensor_copy(forget_pos[:, :], bank(7)[0:H_FOX, P:P + S]).then_inc(c_copied, 1)
                dve.tensor_scalar(forget_neg[:, :], bank(7)[0:H_FOX, P:P + S], -1.0, None, ALU.mult
                                  ).then_inc(c_copied, 1)
                for i in range(SPLITS, QK_UNITS + V_UNITS):
                    mix_low(layer, i)
                for half in range(2):
                    dve.wait_ge(used, base + QK_UNITS + 2 * half + 2)
                    for t in range(TB):
                        dve.tensor_copy(v_rows[:, t, half * HALF:(half + 1) * HALF], bank(4 + 2 * half + t)
                                        ).then_inc(v_copied, 1)
                for i in range(QK_UNITS + V_UNITS, MIX_UNITS - 1):
                    mix_low(layer, i)
                attention(layer)
                dve.wait_ge(expd, (layer + 1) * HEADS)
                if layer == 0:
                    dve.memset(rden[:, :, SOFT:], 1.0).then_inc(den_done, 1)
                    dve.wait_ge(den_done, 1)
                dve.wait_ge(weighed, (layer + 1) * (H_DIL + H_SB))
                dve.reciprocal(rden[:, :, 0:SOFT], den[:, :, 0:SOFT]).then_inc(den_done, 1)
                dve.wait_ge(den_done, 2 + layer)
                dve.wait_ge(mixed, (layer + 1) * HEADS)
                for t in range(TB):
                    for half in range(2):
                        hs = slice(half * HEADS // 2, (half + 1) * HEADS // 2)
                        dve.tensor_tensor(rows[:, t, half * HALF:(half + 1) * HALF]
                                          .rearrange("p (h d) -> p h d", d=HEAD_DIM),
                                          bank(4 + 2 * t + half).rearrange("p (h d) -> p h d", d=HEAD_DIM),
                                          rden[:, t, hs].unsqueeze(2).to_broadcast([P, HEADS // 2, HEAD_DIM]),
                                          ALU.mult).then_inc(o_scaled, 1)
                dve.wait_ge(o_squares, 2 * layer + 2)
                dve.tensor_reduce(head_ssq[:, :], k_t[:, :, :].rearrange("p k s -> p (k s)")
                                  .rearrange("p (h d) -> p h d", d=HEAD_DIM), AX_X, ALU.add).then_inc(o_summed, 1)
                dve.wait_ge(o_rstd_done, layer + 1)
                o3 = rows[:, :, :].rearrange("p t d -> p (t d)").rearrange("p (h d) -> p h d", d=HEAD_DIM)
                for t in range(TB):
                    hs = slice(t * HEADS, (t + 1) * HEADS)
                    dve.tensor_tensor(o3[:, hs, :], o3[:, hs, :],
                                      head_rstd[:, hs].unsqueeze(2).to_broadcast([P, HEADS, HEAD_DIM]),
                                      ALU.mult).then_inc(o_normed, 1)
                dve.wait_ge(gain_loaded, 16 * (3 * layer + 2))
                for t in range(TB):
                    dve.wait_ge(o_normed, 2 * layer + t + 1)
                    dve.tensor_tensor(rows[:, t, :], rows[:, t, :], gain[:, :], ALU.mult).then_inc(normed, 1)
                split_turned(3 * layer + 1)
                mix_low(layer, MIX_UNITS - 1)
                for half in range(2):
                    dve.wait_ge(used, base + MIX_UNITS - 2 + 2 * half)
                    for t in range(TB):
                        r = resid[:, t, half * HALF:(half + 1) * HALF]
                        dve.tensor_tensor(r, r, bank(4 + 2 * half + t), ALU.add).then_inc(resid_done, 1)

            def ffn_steps(base, first_step, blocks):
                def unit_low(i, number, slot):
                    low(slot, number, (base_mod[0] + i) % SPLITS)

                def mul(count, number):
                    dve.wait_ge(activated, count + 1)
                    dve.wait_ge(hid_turned, count)
                    dve.tensor_tensor(hidden[:, 0:blocks, :], gated[:, 0:blocks, :], psum[:, 0:blocks, 256:512],
                                      ALU.mult).then_inc(hidden_done, 1)

                def hid(count):
                    dve.wait_ge(hid_high_done, count + 1)
                    dve.tensor_tensor(hid_low[:, :, 0:blocks * P],
                                      bank(2)[:, 0:2 * blocks * P].rearrange("p (c s) -> p c s", c=2),
                                      hid_high[:, :, 0:blocks * P].bitcast(F32), ALU.subtract
                                      ).then_inc(hid_low_done, 1)

                def step(number, count, ring):
                    unit_low(2, number + 3, ring[0])
                    mul(count, number)
                    if len(ring) > 1:
                        unit_low(3, number + 4, ring[1])
                    hid(count)
                    if len(ring) > 2:
                        unit_low(4, number + 5, ring[2])

                unit_low(0, base, FIRST[0])
                unit_low(1, base + 1, FIRST[1])
                unit_low(2, base + 2, RING_A[0])
                unit_low(3, base + 3, RING_A[1])
                mul(first_step, base)
                unit_low(4, base + 4, RING_A[2])
                hid(first_step)
                with dve.Fori(0, PAIRS - 1) as it:
                    step(base + it * 6 + 2, first_step + it * 2 + 1, RING_B)
                    step(base + it * 6 + 5, first_step + it * 2 + 2, RING_A)
                step(base + 3 * (STEPS - 2) - 1, first_step + STEPS - 2, RING_B)
                step(base + 3 * (STEPS - 1) - 1, first_step + STEPS - 1, (LAST,))

            base_mod = [0]
            tables()
            mix(0)
            norm(2, 3)
            split_turned(2)
            base_mod[0] = DENSE_BASE % SPLITS
            ffn_steps(DENSE_BASE, 0, TB)
            dve.wait_ge(used, DENSE_BASE + FFN_UNITS)
            for t in range(TB):
                for half in range(2):
                    r = resid[:, t, half * HALF:(half + 1) * HALF]
                    dve.tensor_tensor(r, r, bank(4 + 2 * t + half), ALU.add).then_inc(resid_done, 1)
            mix(1)
            norm(4, 6)
            dve.wait_ge(small_high_done, 3)
            dve.tensor_tensor(small_low[:, :, :], small_raw[:, :, :], small_high[:, :, :].bitcast(F32),
                              ALU.subtract).then_inc(small_low_done, 1)
            split_turned(5)
            for t in range(TB):
                dve.wait_ge(rows_high_done, t + 1)
                dve.tensor_tensor(rows_low[:, t, :], rows[:, t, :], rows_high[:, t, :].bitcast(F32),
                                  ALU.subtract).then_inc(rows_low_done, 1)

            n = [0]

            def chain(ins):
                n[0] += 1
                ins.then_inc(route_chain, 1)
                dve.wait_ge(route_chain, n[0])

            E = EXPERTS
            chain(dve.memset(earlier[:, :, :, :], 0.0))
            for e in range(1, E):
                chain(dve.memset(earlier[:, :, e, 0:e], 1.0))
            dve.wait_ge(logits_done, 1)
            chain(dve.tensor_copy(logits[:, :, :], bank(4)[:, 0:TB * E].rearrange("p (t e) -> p t e", t=TB)))
            by_j = logits[:, :, :].unsqueeze(2).to_broadcast([P, TB, E, E])
            by_e = logits[:, :, :].unsqueeze(3).to_broadcast([P, TB, E, E])
            chain(dve.tensor_tensor(beats[:, :, :, :], by_j, by_e, ALU.is_gt))
            chain(dve.tensor_tensor(ties[:, :, :, :], by_j, by_e, ALU.is_equal))
            chain(dve.tensor_tensor(ties[:, :, :, :], ties[:, :, :, :], earlier[:, :, :, :], ALU.mult))
            chain(dve.tensor_tensor(beats[:, :, :, :], beats[:, :, :, :], ties[:, :, :, :], ALU.add))
            chain(dve.tensor_reduce(place[:, :, :], beats[:, :, :, :], AX_X, ALU.add))
            dve.tensor_scalar(chosen[:, :, :], place[:, :, :], float(TOP_K), None, ALU.is_lt).then_inc(chosen_done, 1)
            chain(dve.tensor_reduce(top[:, :], logits[:, :, :], AX_X, ALU.max))
            dve.tensor_tensor(gate[:, :, :], logits[:, :, :], top[:, :].unsqueeze(2).to_broadcast([P, TB, E]),
                              ALU.subtract).then_inc(shifted, 1)
            dve.wait_ge(gate_exp, 1)
            dve.wait_ge(chosen_done, 1)
            chain(dve.tensor_tensor(gate[:, :, :], gate[:, :, :], chosen[:, :, :], ALU.mult))
            chain(dve.tensor_reduce(gate_sum[:, :], gate[:, :, :], AX_X, ALU.add))
            chain(dve.reciprocal(gate_sum[:, :], gate_sum[:, :]))
            chain(dve.tensor_tensor(gate[:, :, :], gate[:, :, :],
                                    gate_sum[:, :].unsqueeze(2).to_broadcast([P, TB, E]), ALU.mult))
            dve.wait_ge(ranked, 1)
            chain(dve.tensor_copy(rank[:, :, :], bank(5)[:, 0:TB * E].rearrange("p (t e) -> p t e", t=TB)))
            chain(dve.tensor_reduce(most[:, :], bank(5)[:, TB * E:(TB + 1) * E], AX_X, ALU.max))
            dve.tensor_scalar(spill[:, :], most[:, :], float(slots), None, ALU.is_gt).then_inc(spill_done, 1)

            def experts(number):
                unit0 = MOE_BASE + number * EXPERTS * FFN_UNITS
                base_mod[0] = unit0 % SPLITS
                if number:
                    chain(dve.tensor_scalar(rank[:, :, :], rank[:, :, :], -float(slots), None, ALU.add))
                with dve.Fori(0, EXPERTS) as e:
                    n = e + number * EXPERTS
                    dve.wait_ge(used, unit0 + e * FFN_UNITS)
                    for t in range(TB):
                        dve.tensor_scalar(take[:, t, 0:slots], iota_row[:, 0:slots], rank[:, t, bass.ds(e, 1)],
                                          chosen[:, t, bass.ds(e, 1)], ALU.is_equal, ALU.mult
                                          ).then_inc(take_done, 1)
                    dve.wait_ge(gathered, n + 1)
                    for b, g in enumerate((6, 7)):
                        dve.tensor_copy(act_low[:, 4 * b:4 * b + 4, 0:P], bank(g)
                                        .rearrange("p (k s) -> p k s", k=4)).then_inc(x_low_done, 1)
                    ffn_steps(unit0 + e * FFN_UNITS, STEPS + n * STEPS, 1)
                    dve.wait_ge(y_high_done, n + 1)
                    dve.tensor_tensor(y_low[:, :], psum[:, 4:6, :].rearrange("p b n -> p (b n)"),
                                      y_high[:, :].bitcast(F32), ALU.subtract).then_inc(y_low_done, 1)
                    for m, (half, t, g) in enumerate(((0, 0, 0), (0, 1, 2), (1, 0, 4), (1, 1, 5))):
                        dve.wait_ge(scattered, n * 4 + m + 1)
                        r = resid[:, t, half * HALF:(half + 1) * HALF]
                        dve.scalar_tensor_tensor(r, bank(g), gate[:, t, bass.ds(e, 1)], r, ALU.mult, ALU.add
                                                 ).then_inc(summed, 1)

            if slots < P:
                chain(dve.memset(take[:, :, :].bitcast(F32), 0.0))
            experts(0)
            with dve.If(dve.value_load(spill[0:1, 0:1], min_val=0, max_val=1) > 0):
                experts(1)
            dve.memset(most[:, :], 0.0).then_inc(moe_done, 1)
            norm(5, 7)

        @block.tensor
        def _(pe):
            def turn_rows(times, use):
                pe.wait_ge(normed, 2 * use)
                for b in range(4):
                    for k in (2 * b, 2 * b + 1):
                        for t in range(TB):
                            c = (k % 2) * S + t * P
                            ins = pe.transpose(bank(b)[:, c:c + P], rows[:, t, k * P:(k + 1) * P], ident[:, :])
                    ins.then_inc(turned, 1)

            def three(dst, lhs_high, lhs_low, rhs_high, rhs_low, first, last):
                pe.matmul(dst, lhs_high, rhs_high, start=first, stop=False)
                pe.matmul(dst, lhs_high, rhs_low, start=False, stop=False)
                return pe.matmul(dst, lhs_low, rhs_high, start=False, stop=last)

            def parts(split, a):
                return (w_high[:, split, :].rearrange("p (a n) -> p a n", a=a),
                        w_low[:, split, :].rearrange("p (a n) -> p a n", a=a))

            def attention(layer):
                H0 = layer * HEADS

                def score(i):
                    h = HEAD_ORDER[i]
                    if H0 + i >= 2 and i >= 2:
                        pe.wait_ge(masked, H0 + i - 1)
                    rows_of = slice(HEAD_DIM * (h % 2), HEAD_DIM * (h % 2) + HEAD_DIM)
                    q, k = q_t[rows_of, h // 2, :], k_t[rows_of, h // 2, :]
                    sc = bank(i % 2)
                    if kind(h) == "stick":
                        pe.matmul(sc[:, 0:S], k[:, 0:P], q, start=True, stop=True)
                        ins = pe.matmul(sc[:, S:S + P], k[:, P:S], q[:, P:S], start=True, stop=True)
                    else:
                        for t in range(TB):
                            dst, ts = (sc[:, 0:P], slice(0, P)) if t == 0 else (sc[:, P:P + S], slice(P, S))
                            keys = (t + 1) * P
                            fox = kind(h) == "fox"
                            ins = pe.matmul(dst, q[:, ts], k[:, 0:keys], start=True, stop=not fox)
                            if fox:
                                f = h - H_DIL
                                for s in range(t + 1):
                                    pe.matmul(dst[:, s * P:(s + 1) * P], forget_pos[:, ts], pick[:, f, :],
                                              start=False, stop=False)
                                ins = pe.matmul(dst, pick[:, f, :], forget_neg[:, 0:keys], start=False, stop=True)
                    ins.then_inc(scores, 1)

                def flip(i):
                    h = HEAD_ORDER[i]
                    if i >= 2:
                        pe.wait_ge(weights_t, H0 + i - 1)
                    dst = bank(2 + i % 2)
                    if kind(h) == "fox":
                        pe.wait_ge(expd, H0 + i + 1)
                    else:
                        pe.wait_ge(weighed, layer * (H_DIL + H_SB) + count_of(i, "dil", "stick"))
                    if kind(h) != "stick":
                        for c in range(3):
                            cs = slice(c * P, (c + 1) * P)
                            ins = pe.transpose(dst[:, cs], prob[:, i % 3, cs], ident[:, :])
                    else:
                        sp_t = stick[:, i % 3, :]
                        pe.matmul(dst[:, 0:S], since[:, :], sp_t[:, 0:S], start=True, stop=False)
                        pe.matmul(dst[:, P:S], ones[:, :], sp_t[:, S:S + P], start=False, stop=True)
                        ins = pe.matmul(dst[:, S:S + P], since[:, :], sp_t[:, S:S + P], start=True, stop=True)
                    ins.then_inc(flipped, 1)

                def mix_values(i):
                    h = HEAD_ORDER[i]
                    pe.wait_ge(weights_t, H0 + i + 1)
                    c0 = (h % (HEADS // 2)) * HEAD_DIM
                    half = h // (HEADS // 2)
                    pt = prob_t[:, i % 2, :]
                    v = v_rows[:, :, h * HEAD_DIM:(h + 1) * HEAD_DIM]
                    pe.matmul(bank(4 + half)[:, c0:c0 + HEAD_DIM], pt[:, 0:P], v[:, 0, :], start=True, stop=True)
                    dst = bank(6 + half)[:, c0:c0 + HEAD_DIM]
                    pe.matmul(dst, pt[:, P:S], v[:, 0, :], start=True, stop=False)
                    pe.matmul(dst, pt[:, S:S + P], v[:, 1, :], start=False, stop=True).then_inc(mixed, 1)

                for s in range(HEADS + 3):
                    if s < HEADS:
                        score(s)
                    if 2 <= s < HEADS + 2:
                        flip(s - 2)
                    if s >= 3:
                        mix_values(s - 3)

            def rows_times_unit(base, i, k0, banks, first, last):
                wh, wl = parts(split_slot(base, i), 4)
                pe.wait_ge(low_done, base + i + 1)
                for kk in range(4):
                    for t in range(TB):
                        ts = slice(t * P, (t + 1) * P)
                        ins = three(bank(banks[t]), act_high[:, k0 + kk, ts], act_low[:, k0 + kk, ts],
                                    wh[:, kk, :], wl[:, kk, :], first and kk == 0, last and kk == 3)
                ins.then_inc(used, 1)

            def mix(layer):
                base = MIX_BASE[layer]
                turn_rows(3 * layer, 3 * layer + 1)
                pe.wait_ge(act_low_done, 12 * layer + 4)
                pe.wait_ge(small_low_done, layer + 1)
                for t in range(TB):
                    ts = slice(t * P, (t + 1) * P)
                    for k in range(KC):
                        ins = three(bank(7)[:, 8 * t:8 * t + H_FOX + 1], act_high[:, k, ts], act_low[:, k, ts],
                                    forget_high[:, k, :], forget_low[:, k, :], k == 0, k == KC - 1)
                ins.then_inc(f_done, 1)
                for i in range(QK_UNITS):
                    if i == 1:
                        pe.wait_ge(f_log_done, layer + 1)
                        c = bank(7)[0:H_FOX, P:P + S]
                        pe.matmul(c[:, 0:P], f_log[:, 0, :], upto[:, :], start=True, stop=True)
                        pe.matmul(c[:, P:S], f_log[:, 0, :], ones[:, :], start=True, stop=False)
                        pe.matmul(c[:, P:S], f_log[:, 1, :], upto[:, :], start=False, stop=True).then_inc(c_done, 1)
                    wh, wl = parts(split_slot(base, i), KC)
                    if i >= 4:
                        pe.wait_ge(qk_copied, QK_UNITS * layer + i - 3)
                    pe.wait_ge(low_done, base + i + 1)
                    for c in range(2):
                        cs = slice(c * P, (c + 1) * P)
                        for k in range(KC):
                            ins = three(bank(i % 4)[:, c * S:(c + 1) * S], wh[:, k, cs], wl[:, k, cs],
                                        act_high[:, k, :], act_low[:, k, :], k == 0, k == KC - 1)
                    ins.then_inc(used, 1)
                pe.wait_ge(c_copied, 2 * layer + 2)
                for n in range(V_UNITS):
                    half = n // 2
                    rows_times_unit(base, QK_UNITS + n, 4 * (n % 2), (4 + 2 * half, 5 + 2 * half), n % 2 == 0, n % 2 == 1)
                pe.wait_ge(qk_copied, QK_UNITS * (layer + 1))
                pe.wait_ge(v_copied, 4 * layer + 4)
                pe.wait_ge(pick_done, layer + 1)
                attention(layer)
                turn_rows(3 * layer + 1, 3 * layer + 2)
                pe.wait_ge(act_low_done, 12 * layer + 8)
                for n in range(OUT_UNITS):
                    half = n // 2
                    rows_times_unit(base, QK_UNITS + V_UNITS + n, 4 * (n % 2), (4 + 2 * half, 5 + 2 * half),
                                    n % 2 == 0, n % 2 == 1)

            def ffn_steps(base, first_step, blocks):
                def split_of(i):
                    return (base_mod[0] + i) % SPLITS

                def gate_up(o, number):
                    for u in range(2):
                        wh, wl = parts(split_of(o + u), 4)
                        pe.wait_ge(low_done, number + (u + 1))
                        for kk in range(4):
                            for t in range(blocks):
                                ts = slice(t * P, (t + 1) * P)
                                k = 4 * u + kk
                                ins = three(bank(t), act_high[:, k, ts], act_low[:, k, ts], wh[:, kk, :],
                                            wl[:, kk, :], k == 0, k == KC - 1)
                        ins.then_inc(used, 1)

                def down(o, number, count, first, last):
                    wh, wl = parts(split_of(o), 2)
                    pe.wait_ge(low_done, number + 1)
                    pe.wait_ge(hid_low_done, count + 1)
                    for c in range(2):
                        for t in range(blocks):
                            for half in range(2):
                                ts, hs = slice(t * P, (t + 1) * P), slice(half * HALF, (half + 1) * HALF)
                                ins = three(bank(4 + 2 * t + half), hid_high[:, c, ts], hid_low[:, c, ts],
                                            wh[:, c, hs], wl[:, c, hs], first and c == 0, last and c == 1)
                    ins.then_inc(used, 1)

                def turn(count):
                    pe.wait_ge(hidden_done, count + 1)
                    for c in range(2):
                        for t in range(blocks):
                            d0 = (c * blocks + t) * P
                            ins = pe.transpose(bank(2)[:, d0:d0 + P], hidden[:, t, c * P:(c + 1) * P], ident[:, :])
                    ins.then_inc(hid_turned, 1)

                gate_up(0, base)
                turn(first_step)
                gate_up(2, base + 2)
                down(4, base + 4, first_step, True, False)
                turn(first_step + 1)
                with pe.Fori(2, STEPS) as j:
                    number = base + j * 3 - 1
                    gate_up(2, number)
                    down(4, number + 2, first_step + j - 1, False, False)
                    turn(first_step + j)
                down(FFN_UNITS - 1, base + FFN_UNITS - 1, first_step + STEPS - 1, False, True)

            base_mod = [0]
            pe.wait_ge(const_done, 8)
            mix(0)
            turn_rows(2, 3)
            pe.wait_ge(act_low_done, 12)
            base_mod[0] = DENSE_BASE % SPLITS
            ffn_steps(DENSE_BASE, 0, TB)
            mix(1)
            turn_rows(5, 6)
            pe.wait_ge(act_low_done, 24)
            pe.wait_ge(small_low_done, 3)
            E = EXPERTS
            for t in range(TB):
                ts = slice(t * P, (t + 1) * P)
                for k in range(KC):
                    ins = three(bank(4)[:, E * t:E * (t + 1)], act_high[:, k, ts], act_low[:, k, ts],
                                small_high[:, k, :], small_low[:, k, :], k == 0, k == KC - 1)
            ins.then_inc(logits_done, 1)
            pe.wait_ge(chosen_done, 1)
            r = bank(5)
            pe.matmul(r[:, 0:E], before[:, :], chosen[:, 0, :], start=True, stop=True)
            pe.matmul(r[:, E:2 * E], ones[:, :], chosen[:, 0, :], start=True, stop=False)
            pe.matmul(r[:, E:2 * E], before[:, :], chosen[:, 1, :], start=False, stop=True)
            pe.matmul(r[:, 2 * E:3 * E], ones[:, :], chosen[:, 0, :], start=True, stop=False)
            pe.matmul(r[:, 2 * E:3 * E], ones[:, :], chosen[:, 1, :], start=False, stop=True).then_inc(ranked, 1)
            pe.wait_ge(rows_low_done, TB)

            def experts(number):
                unit0 = MOE_BASE + number * EXPERTS * FFN_UNITS
                base_mod[0] = unit0 % SPLITS
                with pe.Fori(0, EXPERTS) as e:
                    n = e + number * EXPERTS
                    pe.wait_ge(take_done, n * 2 + 2)
                    for part, banks in ((rows_high, (1, 3)), (rows_low, (6, 7))):
                        for k in range(KC):
                            dst = bank(banks[k // 4])[:, (k % 4) * P:(k % 4 + 1) * P]
                            for t in range(TB):
                                ins = pe.matmul(dst, part[:, t, k * P:(k + 1) * P], take[:, t, :],
                                                start=t == 0, stop=t == TB - 1)
                    ins.then_inc(gathered, 1)
                    for t in range(TB):
                        ins = pe.transpose(bank(2)[:, t * P:(t + 1) * P], take[:, t, :].bitcast(F32), ident[:, :])
                    ins.then_inc(take_turned, 1)
                    pe.wait_ge(x_high_done, n * 2 + 2)
                    pe.wait_ge(x_low_done, n * 2 + 2)
                    pe.wait_ge(give_done, n + 1)
                    ffn_steps(unit0 + e * FFN_UNITS, STEPS + n * STEPS, 1)
                    pe.wait_ge(y_low_done, n + 1)
                    for half, t, g in ((0, 0, 0), (0, 1, 2), (1, 0, 4), (1, 1, 5)):
                        hs = slice(half * HALF, (half + 1) * HALF)
                        lhs = give[:, t * P:(t + 1) * P]
                        pe.matmul(bank(g), lhs, y_high[:, hs], start=True, stop=False)
                        pe.matmul(bank(g), lhs, y_low[:, hs], start=False, stop=True).then_inc(scattered, 1)

            experts(0)
            pe.wait_ge(spill_done, 1)
            with pe.If(pe.value_load(spill[0:1, 0:1], min_val=0, max_val=1) > 0):
                experts(1)


_INS = ["x", "mix_norm", "w_in", "forget_bias", "head_norm", "w_out", "ffn_norm", "dense_w_gate", "dense_w_up",
        "dense_w_down", "router_w", "moe_w_gate", "moe_w_up", "moe_w_down", "final_norm"]


def kernel(**inputs):
    import numpy as _np
    import concourse.bacc as _bacc
    from concourse import mybir as _mybir
    from concourse.bass_utils import run_bass_kernel_spmd as _run

    nc = _bacc.Bacc("TRN2", target_bir_lowering=False, num_devices=1)
    arrays, args = {}, []
    for name in _INS:
        a = _np.ascontiguousarray(inputs[name])
        arrays[f"in_{name}"] = a
        args.append(nc.dram_tensor(f"in_{name}", a.shape, _mybir.dt.from_np(a.dtype), kind="ExternalInput").ap())
    args.append(nc.dram_tensor("out_0", inputs["x"].shape, _mybir.dt.float32, kind="ExternalOutput").ap())
    hybrid_trunk(nc, *args)
    r = _run(nc, [arrays], core_ids=[0])
    return r.results[0]["out_0"]
```

```python
from contextlib import ExitStack

import concourse.bass as bass
from concourse import mybir

F32 = mybir.dt.float32
F32R = mybir.dt.float32r
BF16 = mybir.dt.bfloat16
I32 = mybir.dt.int32
ALU = mybir.AluOpType
ACT = mybir.ActivationFunctionType
AX_X = mybir.AxisListType.X

P = 128
HEAD_DIM = 64
DIL_PATTERNS = ((128, 1), (512, 4), (2048, 16))
TOP_K = 2
EPS = 1e-6
MASKED = -1e30


def hybrid_trunk(nc, x, mix_norm, w_in, forget_bias, head_norm, w_out, ffn_norm,
                 dense_w_gate, dense_w_up, dense_w_down, router_w,
                 moe_w_gate, moe_w_up, moe_w_down, final_norm, out, slots=P):
    _, S, D = x.shape
    DEPTH = mix_norm.shape[0]
    H_FOX = forget_bias.shape[1]
    HEADS = D // HEAD_DIM
    H_DIL = HEADS * 3 // 8
    H_SB = HEADS - H_DIL - H_FOX
    FF = dense_w_gate.shape[2]
    EXPERTS = moe_w_gate.shape[1]
    TB = S // P
    KC = D // P
    HALF = D // 2
    assert DEPTH == 2 and TB == 2 and D == 1024 and HALF == 512 and FF % 256 == 0
    SCALE = HEAD_DIM ** -0.5
    SOFT = H_DIL + H_FOX

    UNIT = 2048
    QK_UNITS, V_UNITS, OUT_UNITS = 2 * D // 256, 4, 4
    MIX_UNITS = QK_UNITS + V_UNITS + OUT_UNITS
    STEPS = FF // 256
    FFN_UNITS = 3 * STEPS
    PAIRS = (STEPS - 1) // 2
    assert STEPS % 2 == 1 and STEPS >= 5 and MIX_UNITS == 16
    MIX_BASE = [0, MIX_UNITS + FFN_UNITS]
    DENSE_BASE = MIX_UNITS
    MOE_BASE = 2 * MIX_UNITS + FFN_UNITS
    SPLITS = 3

    HEAD_ORDER = list(range(HEADS))
    slot_cols = 3 * P

    ctx = ExitStack()
    with ctx:
        def sb(name, shape, dt, stack=ctx):
            return stack.enter_context(nc.sbuf_tensor(name, shape, dt))

        def sem(name):
            return ctx.enter_context(nc.semaphore(name))

        raw = sb("raw", [P, 9, UNIT], F32)
        w_high = sb("w_high", [P, SPLITS, UNIT], F32R)
        w_low = sb("w_low", [P, SPLITS, UNIT], F32R)
        resid = sb("resid", [P, TB, D], F32)
        rows = sb("rows", [P, TB, D], F32)
        gain = sb("gain", [P, D], F32)
        act_high = sb("act_high", [P, KC, S], F32R)
        act_low = sb("act_low", [P, KC, S], F32R)
        ident = sb("ident", [P, P], F32)
        iota_row = sb("iota_row", [P, P], F32)
        before = sb("before", [P, P], F32)
        since = sb("since", [P, P], F32)
        ones = sb("ones", [P, P], F32)
        causal = sb("causal", [P, slot_cols], BF16)
        strict_t = sb("strict_t", [P, slot_cols], BF16)
        dil_dist = sb("dil_dist", [P, slot_cols], BF16)
        dil_times = sb("dil_times", [P, slot_cols], BF16)
        small_raw = sb("small_raw", [P, KC, EXPERTS], F32)
        small_high = sb("small_high", [P, KC, EXPERTS], F32R)
        small_low = sb("small_low", [P, KC, EXPERTS], F32R)
        forget_raw = sb("forget_raw", [P, KC, H_FOX], F32)
        forget_high = sb("forget_high", [P, KC, H_FOX], F32R)
        forget_low = sb("forget_low", [P, KC, H_FOX], F32R)
        bias_col = sb("bias_col", [H_FOX, 1], F32)
        ssq = sb("ssq", [P, TB], F32)
        rstd = sb("rstd", [P, TB], F32)
        half_power = sb("half_power", [P, TB], F32)
        head_mean = sb("head_mean", [P, TB, HEADS], F32)
        head_rstd = sb("head_rstd", [P, TB, HEADS], F32)
        head_fix = sb("head_fix", [P, TB, HEADS], F32)
        neg_max = sb("neg_max", [P, TB, HEADS], F32)
        den = sb("den", [P, TB, HEADS], F32)
        rden = sb("rden", [P, TB, HEADS], F32)
        forget_col = sb("forget_col", [P, TB, H_FOX], F32)

        mixer = ExitStack()
        q_t = sb("q_t", [P, KC, S], F32, mixer)
        k_t = sb("k_t", [P, KC, S], F32, mixer)
        v_rows = sb("v_rows", [P, TB, D], F32, mixer)
        prob = sb("prob", [P, 3, slot_cols], F32, mixer)
        stick = sb("stick", [P, 3, slot_cols], F32, mixer)
        prob_t = sb("prob_t", [P, 2, slot_cols], F32, mixer)
        alibi = sb("alibi", [P, 2, slot_cols], F32, mixer)
        forget_sum = sb("forget_sum", [H_FOX, S], F32, mixer)
        forget_neg = sb("forget_neg", [H_FOX, S], F32, mixer)
        pick = sb("pick", [H_FOX, H_FOX, P], F32, mixer)
        dist_i = alibi[:, 0, :].bitcast(I32)
        f_logit = stick[0:H_FOX, 0, 0:S]
        f_soft = stick[0:H_FOX, 1, 0:S]
        mixer.close()
        ffn = ExitStack()
        gated = sb("gated", [P, TB, 256], F32, ffn)
        hidden = sb("hidden", [P, TB, 256], F32, ffn)
        hid_high = sb("hid_high", [P, 2, S], F32R, ffn)
        hid_low = sb("hid_low", [P, 2, S], F32R, ffn)
        rows_high = sb("rows_high", [P, TB, D], F32R, ffn)
        rows_low = sb("rows_low", [P, TB, D], F32R, ffn)
        y_high = sb("y_high", [P, D], F32R, ffn)
        y_low = sb("y_low", [P, D], F32R, ffn)
        take = sb("take", [P, TB, P], F32R, ffn)
        x_rows = sb("x_rows", [P, D], F32, ffn)
        give = sb("give", [P, S], F32R, ffn)
        logits_t = sb("logits_t", [EXPERTS, S], F32, ffn)
        logits = sb("logits", [P, TB, EXPERTS], F32, ffn)
        beats = sb("beats", [P, TB, EXPERTS, EXPERTS], F32, ffn)
        ties = sb("ties", [P, TB, EXPERTS, EXPERTS], F32, ffn)
        place = sb("place", [P, TB, EXPERTS], F32, ffn)
        chosen = sb("chosen", [P, TB, EXPERTS], F32, ffn)
        top = sb("top", [P, TB], F32, ffn)
        gate = sb("gate", [P, TB, EXPERTS], F32, ffn)
        gate_sum = sb("gate_sum", [P, TB], F32, ffn)
        rank = sb("rank", [P, TB, EXPERTS], F32, ffn)
        most = sb("most", [P, 1], F32, ffn)
        spill = sb("spill", [P, 1], I32, ffn)
        earlier = sb("earlier", [P, TB, EXPERTS, EXPERTS], F32, ffn)
        ffn.close()

        psum = ctx.enter_context(nc.psum_tensor("psum", [P, 8, 512], F32))

        x_loaded = sem("x_loaded")
        small_loaded = sem("small_loaded")
        router_loaded = sem("router_loaded")
        gain_loaded = sem("gain_loaded")
        landed = [sem(f"unit_landed_{s}") for s in range(9)]
        high_done = sem("high_done")
        low_done = sem("low_done")
        used = sem("used")
        const_done = sem("const_done")
        dist_ready = sem("dist_ready")
        table_chain = sem("table_chain")
        tables_done = sem("tables_done")
        small_high_done = sem("small_high_done")
        small_low_done = sem("small_low_done")
        squares = sem("squares")
        scale_ready = sem("scale_ready")
        pool_chain = sem("pool_chain")
        normed = sem("normed")
        turned = sem("turned")
        act_high_done = sem("act_high_done")
        act_low_done = sem("act_low_done")
        resid_done = sem("resid_done")
        f_done = sem("f_done")
        f_biased = sem("f_biased")
        f_soft_done = sem("f_soft_done")
        f_act_chain = sem("f_act_chain")
        f_clipped = sem("f_clipped")
        c_summed = sem("c_summed")
        c_neg_done = sem("c_neg_done")
        c_turned = sem("c_turned")
        c_col_done = sem("c_col_done")
        qk_copied = sem("qk_copied")
        v_copied = sem("v_copied")
        term_done = sem("term_done")
        pick_chain = sem("pick_chain")
        pick_done = sem("pick_done")
        scores = sem("scores")
        masked = sem("masked")
        expd = sem("expd")
        stick_chain = sem("stick_chain")
        weighed = sem("weighed")
        flipped = sem("flipped")
        arg_done = sem("arg_done")
        weights_t = sem("weights_t")
        mixed = sem("mixed")
        o_squares = sem("o_squares")
        o_chain = sem("o_chain")
        o_mean_done = sem("o_mean_done")
        o_act_chain = sem("o_act_chain")
        o_rstd_done = sem("o_rstd_done")
        activated = sem("activated")
        hidden_done = sem("hidden_done")
        hid_turned = sem("hid_turned")
        hid_high_done = sem("hid_high_done")
        hid_low_done = sem("hid_low_done")
        rows_high_done = sem("rows_high_done")
        rows_low_done = sem("rows_low_done")
        logits_done = sem("logits_done")
        route_chain = sem("route_chain")
        shifted = sem("shifted")
        gate_exp = sem("gate_exp")
        chosen_done = sem("chosen_done")
        ranked = sem("ranked")
        spill_done = sem("spill_done")
        take_done = sem("take_done")
        gathered = sem("gathered")
        x_rows_done = sem("x_rows_done")
        x_turned = sem("x_turned")
        logits_turned = sem("logits_turned")
        logits_copied = sem("logits_copied")
        x_high_done = sem("x_high_done")
        x_low_done = sem("x_low_done")
        take_turned = sem("take_turned")
        give_done = sem("give_done")
        y_high_done = sem("y_high_done")
        y_low_done = sem("y_low_done")
        scattered = sem("scattered")
        summed = sem("summed")
        moe_done = sem("moe_done")
        stored = sem("stored")

        MIX_SLOTS = [0, 1, 3, 4, 5, 6, 7, 8]
        FIRST, LAST, RING_A, RING_B = (0, 1), 2, (3, 4, 5), (6, 7, 8)
        mix_loads = [2 * 16 if s != LAST else 0 for s in range(9)]
        ffn_loads = [32, 32, 16] + [PAIRS * 32, PAIRS * 32, PAIRS * 16] * 2
        at_mix = [[0] * 9, [mix_loads[s] + ffn_loads[s] for s in range(9)]]
        at_dense = mix_loads
        at_moe = [at_mix[1][s] + mix_loads[s] for s in range(9)]

        NORMED = [2, 6, 8, 10, 14, 16, 18]

        def mix_landed(layer, i):
            if i >= MIX_UNITS:
                s = (*FIRST, RING_A[0])[i - MIX_UNITS]
                return s, (at_dense, at_moe)[layer][s] + 32
            s = MIX_SLOTS[i % 8]
            return s, at_mix[layer][s] + 16 * (i // 8 + 1)

        def split_slot(base, i):
            return (base + i) % SPLITS

        def bank(i):
            return psum[:, i, :]

        def wrow(w, k0, kn, c0, cn):
            return w.rearrange("(k p) n -> p k n", p=P)[:, k0:k0 + kn, c0:c0 + cn]

        def raw_view(s, a):
            return raw[:, s, :].rearrange("p (a n) -> p a n", a=a)

        SCATTER = ((0, 0, 1), (0, 1, 3), (1, 0, 4), (1, 1, 5))

        dil_slopes = [2.0 ** (-8.0 * (h + 1) / H_DIL) for h in range(H_DIL)]

        def kind(h):
            return "dil" if h < H_DIL else ("fox" if h < SOFT else "stick")

        def count_of(i, *kinds):
            return sum(kind(h) in kinds for h in HEAD_ORDER[:i + 1])

        def masked_after(m):
            layer, left = (m - 1) // SOFT, (m - 1) % SOFT + 1
            i = next(i for i in range(HEADS) if count_of(i, "dil", "fox") == left)
            return layer * HEADS + i + 1

        def stick_before(layer, i):
            return layer * H_SB + (count_of(i - 3, "stick") if i >= 3 else 0)

        block = ctx.enter_context(nc.Block())

        @block.sync
        def _(sp):
            sp.dma_start(resid[:, :, :], x.rearrange("b (t p) d -> p (b t) d", p=P)).then_inc(x_loaded, 16)

            def mixer_units(layer):
                base = MIX_BASE[layer]
                for i in range(MIX_UNITS):
                    if i < QK_UNITS:
                        src, a = wrow(w_in[layer], 0, KC, i * 256, 256), KC
                    elif i < QK_UNITS + V_UNITS:
                        n = i - QK_UNITS
                        src, a = wrow(w_in[layer], 4 * (n % 2), 4, 2 * D + n // 2 * 512, 512), 4
                    else:
                        n = i - QK_UNITS - V_UNITS
                        src, a = wrow(w_out[layer], 4 * (n % 2), 4, n // 2 * 512, 512), 4
                    s, _ = mix_landed(layer, i)
                    if base + i >= 8:
                        sp.wait_ge(low_done, base + i - 7)
                    sp.dma_start(raw_view(s, a), src).then_inc(landed[s], 16)

            def gate_up_unit(w_gate, w_up, s, step, k0, number, back):
                sp.wait_ge(low_done, number - back)
                for w, c0 in ((w_gate, 0), (w_up, 256)):
                    src = w.rearrange("(k p) f -> p k f", p=P)[:, k0:k0 + 4, bass.ds(step * 256, 256)]
                    sp.dma_start(raw_view(s, 4)[:, :, c0:c0 + 256], src).then_inc(landed[s], 16)

            def down_unit(w_down, s, step, number, back):
                sp.wait_ge(low_done, number - back)
                src = w_down.rearrange("(j c p) n -> j p c n", c=2, p=P)[step]
                sp.dma_start(raw_view(s, 2), src).then_inc(landed[s], 16)

            def ffn_units(w_gate, w_up, w_down, base):
                for k in range(2):
                    gate_up_unit(w_gate, w_up, FIRST[k], 0, 4 * k, base + k, 7)
                with sp.Fori(0, PAIRS) as it:
                    for c, ring in enumerate((RING_A, RING_B)):
                        step = 2 * it + (1 + c)
                        number = base + it * 6 + (2 + 3 * c)
                        gate_up_unit(w_gate, w_up, ring[0], step, 0, number, 5)
                        gate_up_unit(w_gate, w_up, ring[1], step, 4, number + 1, 5)
                        down_unit(w_down, ring[2], step - 1, number + 2, 5)
                down_unit(w_down, LAST, STEPS - 1, base + FFN_UNITS - 1, 5)

            mixer_units(0)
            ffn_units(dense_w_gate[0], dense_w_up[0], dense_w_down[0], DENSE_BASE)
            mixer_units(1)

            def experts(base):
                with sp.Fori(0, EXPERTS) as e:
                    ffn_units(moe_w_gate[0, e], moe_w_up[0, e], moe_w_down[0, e], base + e * FFN_UNITS)

            experts(MOE_BASE)
            sp.wait_ge(spill_done, 1)
            with sp.If(sp.value_load(spill[0:1, 0:1], min_val=0, max_val=1) > 0):
                experts(MOE_BASE + EXPERTS * FFN_UNITS)

            sp.wait_ge(normed, NORMED[6])
            sp.dma_start(out.rearrange("b (t p) d -> p (b t) d", p=P), rows[:, :, :]).then_inc(stored, 16)
            sp.wait_ge(stored, 16)

        @block.gpsimd
        def _(pool):
            def load_gain(g):
                src = [mix_norm[0], head_norm[0], ffn_norm[0], mix_norm[1], head_norm[1], ffn_norm[1],
                       final_norm][g]
                if g:
                    pool.wait_ge(normed, NORMED[g - 1])
                pool.dma_start(gain[:, :], src.partition_broadcast(P)).then_inc(gain_loaded, 16)

            def load_forget(layer):
                pool.dma_start(forget_raw[:, :, :], wrow(w_in[layer], 0, KC, 3 * D, H_FOX)
                               ).then_inc(small_loaded, 16)
                pool.dma_start(bias_col[:, :], forget_bias[layer].rearrange("(f a) -> f a", a=1)
                               ).then_inc(small_loaded, 16)

            load_gain(0)
            load_forget(0)
            pool.dma_start(small_raw[:, :, :], router_w[0].rearrange("(k p) e -> p k e", p=P)).then_inc(router_loaded, 16)

            n = [0]

            def chain(ins):
                n[0] += 1
                ins.then_inc(const_done, 1)
                pool.wait_ge(const_done, n[0])

            chain(pool.memset(half_power[:, :], -0.5))
            chain(pool.memset(ones[:, :], 1.0))
            chain(pool.iota(iota_row[:, :], [[1, P]], base=0, channel_multiplier=0,
                            allow_small_or_imprecise_dtypes=True))
            ge, gt, eq = ALU.is_ge, ALU.is_gt, ALU.is_equal
            for t, cmp, cm, step in ((ident, eq, 1, -1), (before, gt, -1, 1), (since, ge, 1, -1)):
                chain(pool.affine_select(out=t[:, :], in_=ones[:, :], compare_op=cmp, fill=0.0, base=0,
                                         pattern=[[step, P]], channel_multiplier=cm))
            chain(pool.memset(causal[:, :], 0.0))
            chain(pool.affine_select(out=causal[:, 0:P], in_=causal[:, 0:P], compare_op=ge, fill=MASKED, base=0,
                                     pattern=[[-1, P]], channel_multiplier=1))
            chain(pool.affine_select(out=causal[:, P:], in_=causal[:, P:], compare_op=ge, fill=MASKED, base=P,
                                     pattern=[[-1, S]], channel_multiplier=1))
            chain(pool.memset(strict_t[:, :], 0.0))
            chain(pool.affine_select(out=strict_t[:, 0:S], in_=strict_t[:, 0:S], compare_op=gt, fill=MASKED, base=0,
                                     pattern=[[1, S]], channel_multiplier=-1))
            chain(pool.affine_select(out=strict_t[:, S:], in_=strict_t[:, S:], compare_op=gt, fill=MASKED, base=0,
                                     pattern=[[1, P]], channel_multiplier=-1))
            chain(pool.iota(dist_i[:, 0:P], [[-1, P]], base=0, channel_multiplier=1))
            pool.iota(dist_i[:, P:], [[-1, S]], base=P, channel_multiplier=1).then_inc(dist_ready, 1)

            def scale_of(count):
                pool.wait_ge(squares, 2 * count)
                pool.tensor_scalar(ssq[:, :], ssq[:, :], 1.0 / D, EPS, ALU.mult, ALU.add).then_inc(pool_chain, 1)
                pool.wait_ge(pool_chain, count)
                pool.tensor_tensor(rstd[:, :], ssq[:, :], half_power[:, 0:TB], ALU.pow).then_inc(scale_ready, 1)

            for layer in range(DEPTH):
                scale_of(2 * layer + 1)
                load_gain(3 * layer + 1)
                pool.memset(pick[:, :, :], 1.0).then_inc(pick_chain, 1)
                pool.wait_ge(pick_chain, layer + 1)
                pool.affine_select(out=pick[:, :, :], in_=pick[:, :, :], compare_op=eq, fill=0.0, base=0,
                                   pattern=[[-1, H_FOX], [0, P]], channel_multiplier=1).then_inc(pick_done, 1)
                if layer == 0:
                    pool.wait_ge(tables_done, 1)
                for i, h in enumerate(HEAD_ORDER):
                    if kind(h) == "stick":
                        continue
                    m = layer * SOFT + count_of(i, "dil", "fox")
                    if m > 2:
                        pool.wait_ge(masked, masked_after(m - 2))
                    if kind(h) == "dil":
                        pool.tensor_scalar(alibi[:, m % 2, :], dil_dist[:, :], -dil_slopes[h], 0.0, ALU.mult,
                                           ALU.add).then_inc(term_done, 1)
                    else:
                        pool.wait_ge(c_col_done, layer + 1)
                        for t, (a, b) in enumerate(((0, P), (P, 3 * P))):
                            ins = pool.tensor_scalar(alibi[:, m % 2, a:b], causal[:, a:b], 1.0,
                                                     forget_col[:, t, h - H_DIL:h - H_DIL + 1], ALU.mult, ALU.add)
                        ins.then_inc(term_done, 1)
                load_gain(3 * layer + 2)
                if layer + 1 < DEPTH:
                    pool.wait_ge(small_high_done, layer + 1)
                    pool.wait_ge(small_low_done, layer + 1)
                    pool.wait_ge(f_biased, layer + 1)
                    load_forget(layer + 1)
                scale_of(2 * layer + 2)
                load_gain(3 * layer + 3)
            scale_of(2 * DEPTH + 1)

        @block.scalar
        def _(act):
            def high(slot, need, number, split):
                act.wait_ge(landed[slot], need)
                if not (isinstance(number, int) and number < SPLITS):
                    act.wait_ge(used, number - (SPLITS - 1))
                act.activation(w_high[:, split, :], raw[:, slot, :], ACT.Copy).then_inc(high_done, 1)

            def mix_high(layer, i):
                slot, need = mix_landed(layer, i)
                high(slot, need, MIX_BASE[layer] + i, split_slot(MIX_BASE[layer], i))

            def sum_squares(count, waits):
                if waits:
                    act.wait_ge(resid_done, waits)
                    act.wait_ge(turned, 4 * (3 * ((count - 1) // 2) + 2 * ((count - 1) % 2)))
                else:
                    act.wait_ge(x_loaded, 16)
                for t in range(TB):
                    act.activation(rows[:, t, :], resid[:, t, :], ACT.Square,
                                   accum_out=ssq[:, t:t + 1]).then_inc(squares, 1)

            def split_turned(times):
                for b in range(4):
                    act.wait_ge(turned, 4 * times + b + 1)
                    act.activation(act_high[:, 2 * b:2 * b + 2, :].rearrange("p k s -> p (k s)"), bank(b),
                                   ACT.Copy).then_inc(act_high_done, 1)

            def attention(layer):
                H0 = layer * HEADS

                def exps(i):
                    h = HEAD_ORDER[i]
                    act.wait_ge(masked, H0 + i + 1)
                    if kind(h) != "stick":
                        for t, (a, b) in enumerate(((0, P), (P, 3 * P))):
                            p = prob[:, i % 3, a:b]
                            acc = {"accum_out": den[:, t, h:h + 1]} if kind(h) == "fox" else {}
                            ins = act.activation(p, p, ACT.Exp, bias=neg_max[:, t, h:h + 1], scale=-1.0, **acc)
                        ins.then_inc(expd, 1)
                        return
                    m = 2 * (layer * H_SB + count_of(i, "stick") - 1)
                    if H0 + i >= 3:
                        act.wait_ge(flipped, H0 + i - 2)
                        act.wait_ge(weights_t, H0 + i - 2)
                    st = stick[:, i % 3, :]
                    act.activation(st, prob[:, i % 3, :], ACT.Abs).then_inc(stick_chain, 1)
                    act.wait_ge(stick_chain, m + 1)
                    act.activation(st, st, ACT.Exp, scale=-1.0).then_inc(stick_chain, 1)
                    act.wait_ge(stick_chain, m + 2)
                    act.activation(st, st, ACT.Ln, bias=1.0).then_inc(expd, 1)

                def turn(i):
                    h = HEAD_ORDER[i]
                    act.wait_ge(flipped, H0 + i + 1)
                    if i >= 2:
                        act.wait_ge(mixed, H0 + i - 1)
                    if kind(h) != "stick":
                        act.activation(prob_t[:, i % 2, :], bank(2 + i % 2)[:, 0:slot_cols], ACT.Copy
                                       ).then_inc(weights_t, 1)
                    else:
                        act.wait_ge(arg_done, layer * H_SB + count_of(i, "stick"))
                        act.activation(prob_t[:, i % 2, :], stick[:, i % 3, :], ACT.Exp).then_inc(weights_t, 1)

                def o_square(half):
                    act.wait_ge(mixed, H0 + (half + 1) * HEADS // 2)
                    for t in range(TB):
                        act.activation(rows[:, t, half * HALF:(half + 1) * HALF], bank(4 + 2 * t + half), ACT.Square
                                       ).then_inc(o_squares, 1)

                def o_power(half):
                    hs = slice(half * HEADS // 2, (half + 1) * HEADS // 2)
                    act.wait_ge(o_mean_done, 2 * layer + half + 1)
                    act.activation(head_rstd[:, :, hs], head_mean[:, :, hs], ACT.Ln).then_inc(o_act_chain, 1)
                    act.wait_ge(o_act_chain, 2 * layer + half + 1)
                    act.activation(head_rstd[:, :, hs], head_rstd[:, :, hs], ACT.Exp, scale=-0.5
                                   ).then_inc(o_rstd_done, 1)

                for s in range(HEADS + 2):
                    if s < HEADS:
                        exps(s)
                    if s >= 2:
                        turn(s - 2)
                    if s == HEADS // 2 + 3:
                        o_square(0)
                    if s == HEADS // 2 + 4:
                        o_power(0)
                o_square(1)
                o_power(1)

            def mix(layer):
                act.preload_act_table_set("natural_log_exp_and_others")
                sum_squares(2 * layer + 1, 8 * layer)
                if layer == 0:
                    act.wait_ge(small_loaded, 32)
                else:
                    act.wait_ge(small_loaded, 64)
                act.activation(forget_high[:, :, :], forget_raw[:, :, :], ACT.Copy).then_inc(small_high_done, 1)
                if layer == 0:
                    for i in range(SPLITS):
                        mix_high(layer, i)
                split_turned(3 * layer)
                act.wait_ge(f_biased, layer + 1)
                act.activation(f_soft, f_logit, ACT.Abs).then_inc(f_act_chain, 1)
                act.wait_ge(f_act_chain, 2 * layer + 1)
                act.activation(f_soft, f_soft, ACT.Exp, scale=-1.0).then_inc(f_act_chain, 1)
                act.wait_ge(f_act_chain, 2 * layer + 2)
                act.activation(f_soft, f_soft, ACT.Ln, bias=1.0).then_inc(f_soft_done, 1)
                for i in range(QK_UNITS):
                    act.wait_ge(used, MIX_BASE[layer] + i + 1)
                    dst, c = (q_t, i) if i < QK_UNITS // 2 else (k_t, i - QK_UNITS // 2)
                    act.activation(dst[:, 2 * c:2 * c + 2, :].rearrange("p k s -> p (k s)"), bank(i % 4), ACT.Copy,
                                   scale=SCALE if i < QK_UNITS // 2 else 1.0).then_inc(qk_copied, 1)
                    mix_high(layer, i + SPLITS)
                for i in range(QK_UNITS, QK_UNITS + V_UNITS):
                    mix_high(layer, i + SPLITS)
                attention(layer)
                split_turned(3 * layer + 1)
                for i in range(OUT_UNITS):
                    mix_high(layer, MIX_UNITS - 1 + i)

            def ffn_steps(base, first_step, blocks, need, split0, begun, x_part, following):
                def unit_high(i, number, slot, times):
                    high(slot, need(slot, times), number, (split0 + i) % SPLITS)

                def silu(number, count):
                    act.wait_ge(used, number + 2)
                    if not isinstance(count, int) or count:
                        act.wait_ge(hidden_done, count)
                    act.activation(gated[:, 0:blocks, :], psum[:, 0:blocks, 0:256], ACT.Silu).then_inc(activated, 1)

                def hid(count):
                    act.wait_ge(hid_turned, count + 1)
                    act.activation(hid_high[:, :, 0:blocks * P], bank(2)[:, 0:2 * blocks * P]
                                   .rearrange("p (c s) -> p c s", c=2), ACT.Copy).then_inc(hid_high_done, 1)

                def step(number, count, ring, times):
                    unit_high(2, number + 3, ring[0], times)
                    silu(number, count)
                    unit_high(3, number + 4, ring[1], times)
                    hid(count)
                    unit_high(4, number + 5, ring[2], times)

                unit_high(3, base + 3, RING_A[1], 1)
                silu(base, first_step)
                unit_high(4, base + 4, RING_A[2], 1)
                hid(first_step)
                begun()
                with act.Fori(0, PAIRS - 1) as it:
                    step(base + it * 6 + 2, first_step + it * 2 + 1, RING_B, it + 1)
                    step(base + it * 6 + 5, first_step + it * 2 + 2, RING_A, it + 2)
                step(base + 3 * (STEPS - 2) - 1, first_step + STEPS - 2, RING_B, PAIRS)
                number, count = base + 3 * (STEPS - 1) - 1, first_step + STEPS - 1
                unit_high(2, number + 3, LAST, 1)
                silu(number, count)
                if following:
                    following(0)
                x_part()
                hid(count)
                if following:
                    following(1)

            def nothing():
                pass

            mix(0)
            sum_squares(2, 4)
            split_turned(2)
            act.preload_act_table_set("silu_and_others")
            ffn_steps(DENSE_BASE, 0, TB, lambda s, t: at_dense[s] + (16 if s in (LAST, 5, 8) else 32) * t,
                      DENSE_BASE % SPLITS, nothing, nothing, lambda i: mix_high(1, i))
            mix_high(1, 2)
            mix(1)
            sum_squares(4, 12)
            act.wait_ge(router_loaded, 16)
            act.activation(small_high[:, :, :], small_raw[:, :, :], ACT.Copy).then_inc(small_high_done, 1)
            split_turned(5)
            for t in range(TB):
                act.activation(rows_high[:, t, :], rows[:, t, :], ACT.Copy).then_inc(rows_high_done, 1)
            act.wait_ge(shifted, 1)
            act.activation(gate[:, :, :], gate[:, :, :], ACT.Exp).then_inc(gate_exp, 1)
            act.preload_act_table_set("silu_and_others")

            def experts(number):
                unit0 = MOE_BASE + number * EXPERTS * FFN_UNITS
                split0 = unit0 % SPLITS

                def take_x(n):
                    act.wait_ge(gathered, n + 1)
                    for b, g in enumerate((1, 3)):
                        act.activation(x_rows[:, b * HALF:(b + 1) * HALF], bank(g), ACT.Copy).then_inc(x_rows_done, 1)

                def split_x(n):
                    act.wait_ge(x_turned, n + 1)
                    for b, g in enumerate((1, 3)):
                        act.activation(act_high[:, 4 * b:4 * b + 4, 0:P], bank(g)
                                       .rearrange("p (k s) -> p k s", k=4), ACT.Copy).then_inc(x_high_done, 1)

                def expert(n, base, last):
                    def need(s, t, n=n):
                        each = 16 if s in (LAST, 5, 8) else 32
                        per = 1 if s < 3 else PAIRS
                        return (n * per + t) * each + at_moe[s]

                    def give_copy():
                        act.wait_ge(take_turned, n + 1)
                        act.activation(give[:, :], bank(6)[:, 0:S], ACT.Copy).then_inc(give_done, 1)

                    def x_part():
                        if not last:
                            take_x(n + 1)

                    def following(i):
                        slot = (*FIRST, RING_A[0])[i]
                        high(slot, need(slot, 1, n + 1), base + (FFN_UNITS + i), (split0 + i) % SPLITS)

                    ffn_steps(base, STEPS + n * STEPS, 1, need, split0, give_copy, x_part,
                              None if last else following)
                    if not last:
                        split_x(n + 1)
                    act.wait_ge(used, base + FFN_UNITS)
                    act.activation(y_high[:, :], psum[:, 4:6, :].rearrange("p b n -> p (b n)"), ACT.Copy
                                   ).then_inc(y_high_done, 1)
                    if not last:
                        following(2)

                n0 = number * EXPERTS
                if number:
                    for i, slot in enumerate((*FIRST, RING_A[0])):
                        per = 1 if slot < 3 else PAIRS
                        high(slot, (n0 * per + 1) * 32 + at_moe[slot], unit0 + i, (split0 + i) % SPLITS)
                take_x(n0)
                split_x(n0)
                with act.Fori(0, EXPERTS - 1) as e:
                    expert(e + n0, unit0 + e * FFN_UNITS, False)
                expert(n0 + EXPERTS - 1, unit0 + (EXPERTS - 1) * FFN_UNITS, True)

            experts(0)
            act.wait_ge(spill_done, 1)
            with act.If(act.value_load(spill[0:1, 0:1], min_val=0, max_val=1) > 0):
                experts(1)
            act.wait_ge(moe_done, 1)
            for t in range(TB):
                act.activation(rows[:, t, :], resid[:, t, :], ACT.Square,
                               accum_out=ssq[:, t:t + 1]).then_inc(squares, 1)

        @block.vector
        def _(dve):
            def low(slot, number, split):
                dve.wait_ge(high_done, number + 1)
                dve.tensor_tensor(w_low[:, split, :], raw[:, slot, :], w_high[:, split, :].bitcast(F32),
                                  ALU.subtract).then_inc(low_done, 1)

            def mix_low(layer, i):
                slot, _ = mix_landed(layer, i)
                low(slot, MIX_BASE[layer] + i, split_slot(MIX_BASE[layer], i))

            def norm(count, use):
                dve.wait_ge(scale_ready, count)
                dve.wait_ge(gain_loaded, 16 * use)
                for t in range(TB):
                    dve.scalar_tensor_tensor(rows[:, t, :], resid[:, t, :], rstd[:, t:t + 1], gain[:, :],
                                             ALU.mult, ALU.mult).then_inc(normed, 1)

            def split_turned(times):
                for b in range(4):
                    dve.wait_ge(act_high_done, 4 * times + b + 1)
                    hi = act_high[:, 2 * b:2 * b + 2, :].rearrange("p k s -> p (k s)")
                    lo = act_low[:, 2 * b:2 * b + 2, :].rearrange("p k s -> p (k s)")
                    dve.tensor_tensor(lo, bank(b), hi.bitcast(F32), ALU.subtract).then_inc(act_low_done, 1)

            def tables():
                n = [0]

                def chain(ins):
                    n[0] += 1
                    ins.then_inc(table_chain, 1)
                    dve.wait_ge(table_chain, n[0])

                dist, work, part = prob[:, 0, :], prob[:, 1, :], prob[:, 2, :]
                mod_i = stick[:, 0, :].bitcast(I32)
                dve.wait_ge(dist_ready, 1)
                chain(dve.tensor_copy(dist, dist_i))
                chain(dve.memset(work, 0.0))
                for window, dilation in DIL_PATTERNS:
                    assert dilation & (dilation - 1) == 0 and S % dilation == 0
                    chain(dve.tensor_scalar(mod_i, dist_i, dilation - 1, None, ALU.bitwise_and))
                    chain(dve.tensor_copy(part, mod_i))
                    chain(dve.tensor_scalar(part, part, 0.0, None, ALU.is_equal))
                    chain(dve.scalar_tensor_tensor(part, dist, float(window), part, ALU.is_le, ALU.mult))
                    chain(dve.tensor_tensor(work, work, part, ALU.add))
                chain(dve.scalar_tensor_tensor(work, dist, 0.0, work, ALU.is_ge, ALU.mult))
                chain(dve.tensor_copy(dil_times[:, :], work))
                chain(dve.tensor_scalar(part, work, 0.0, -MASKED, ALU.is_equal, ALU.mult))
                dve.tensor_tensor(dil_dist[:, :], part, dist, ALU.add).then_inc(tables_done, 1)

            def attention(layer):
                H0 = layer * HEADS

                def mask(i):
                    h = HEAD_ORDER[i]
                    dve.wait_ge(scores, H0 + i + 1)
                    if H0 + i >= 3:
                        dve.wait_ge(flipped, H0 + i - 2)
                        if stick_before(layer, i):
                            dve.wait_ge(arg_done, stick_before(layer, i))
                    sc = bank(i % 2)
                    if kind(h) == "stick":
                        dve.tensor_tensor(prob[:, i % 3, :], sc[:, 0:slot_cols], strict_t[:, :], ALU.add
                                          ).then_inc(masked, 1)
                        return
                    m = layer * SOFT + count_of(i, "dil", "fox")
                    dve.wait_ge(term_done, m)
                    term = alibi[:, m % 2, :]
                    for t, (a, b) in enumerate(((0, P), (P, 3 * P))):
                        ins = dve.tensor_tensor_reduce(prob[:, i % 3, a:b], sc[:, a:b], term[:, a:b], -1.0, 3e38,
                                                       ALU.add, ALU.min, neg_max[:, t, h:h + 1])
                    ins.then_inc(masked, 1)

                def weigh(i):
                    h = HEAD_ORDER[i]
                    if kind(h) == "fox":
                        return
                    dve.wait_ge(expd, H0 + i + 1)
                    if kind(h) == "dil":
                        for t, (a, b) in enumerate(((0, P), (P, 3 * P))):
                            p = prob[:, i % 3, a:b]
                            ins = dve.tensor_tensor_reduce(p, p, dil_times[:, a:b], 1.0, 0.0, ALU.mult, ALU.add,
                                                           den[:, t, h:h + 1])
                    else:
                        ins = dve.scalar_tensor_tensor(stick[:, i % 3, :], prob[:, i % 3, :], 0.0,
                                                       stick[:, i % 3, :], ALU.max, ALU.add)
                    ins.then_inc(weighed, 1)

                def subtract_tail(i):
                    if kind(HEAD_ORDER[i]) != "stick":
                        return
                    dve.wait_ge(flipped, H0 + i + 1)
                    dve.tensor_tensor(stick[:, i % 3, :], prob[:, i % 3, :], bank(2 + i % 2)[:, 0:slot_cols],
                                      ALU.subtract).then_inc(arg_done, 1)

                chained = [25 * layer]

                def chain(ins):
                    chained[0] += 1
                    ins.then_inc(o_chain, 1)
                    dve.wait_ge(o_chain, chained[0])

                def o_mean(half):
                    hs = slice(half * HEADS // 2, (half + 1) * HEADS // 2)
                    if half == 0 and layer == 0:
                        chain(dve.memset(rden[:, :, SOFT:], 1.0))
                    soft = slice(hs.start, min(hs.stop, SOFT))
                    if half:
                        dve.wait_ge(expd, H0 + HEADS)
                    chain(dve.reciprocal(rden[:, :, soft], den[:, :, soft]))
                    for t in range(TB):
                        dve.wait_ge(o_squares, 4 * layer + 2 * half + t + 1)
                        chain(dve.tensor_reduce(head_mean[:, t, hs], rows[:, t, half * HALF:(half + 1) * HALF]
                                                .rearrange("p (h d) -> p h d", d=HEAD_DIM), AX_X, ALU.add))
                    m, r = head_mean[:, :, hs], rden[:, :, hs]
                    chain(dve.tensor_tensor(m, m, r, ALU.mult))
                    chain(dve.tensor_tensor(m, m, r, ALU.mult))
                    dve.tensor_scalar(m, m, 1.0 / HEAD_DIM, EPS, ALU.mult, ALU.add).then_inc(o_mean_done, 1)

                def o_norm(half):
                    hs = slice(half * HEADS // 2, (half + 1) * HEADS // 2)
                    m, y, f = head_mean[:, :, hs], head_rstd[:, :, hs], head_fix[:, :, hs]
                    dve.wait_ge(o_rstd_done, 2 * layer + half + 1)
                    chain(dve.tensor_tensor(f, m, y, ALU.mult))
                    chain(dve.tensor_tensor(f, f, y, ALU.mult))
                    chain(dve.tensor_scalar(f, f, -0.5, 1.5, ALU.mult, ALU.add))
                    chain(dve.tensor_tensor(y, y, f, ALU.mult))
                    chain(dve.tensor_tensor(y, y, rden[:, :, hs], ALU.mult))
                    for t in range(TB):
                        chain(dve.tensor_tensor(rows[:, t, half * HALF:(half + 1) * HALF]
                                                .rearrange("p (h d) -> p h d", d=HEAD_DIM),
                                                bank(4 + 2 * t + half).rearrange("p (h d) -> p h d", d=HEAD_DIM),
                                                y[:, t, :].unsqueeze(2).to_broadcast([P, HEADS // 2, HEAD_DIM]),
                                                ALU.mult))
                    dve.wait_ge(gain_loaded, 16 * (3 * layer + 2))
                    for t in range(TB):
                        r = rows[:, t, half * HALF:(half + 1) * HALF]
                        dve.tensor_tensor(r, r, gain[:, half * HALF:(half + 1) * HALF], ALU.mult).then_inc(normed, 1)

                for s in range(HEADS + 2):
                    if s < HEADS:
                        mask(s)
                    if 1 <= s <= HEADS:
                        weigh(s - 1)
                    if s >= 2:
                        subtract_tail(s - 2)
                    if s == HEADS // 2 + 3:
                        o_mean(0)
                    if s == HEADS // 2 + 5:
                        o_norm(0)
                o_mean(1)
                o_norm(1)

            def mix(layer):
                base = MIX_BASE[layer]
                norm(2 * layer + 1, 3 * layer + 1)
                dve.wait_ge(small_high_done, layer + 1)
                dve.tensor_tensor(forget_low[:, :, :], forget_raw[:, :, :], forget_high[:, :, :].bitcast(F32),
                                  ALU.subtract).then_inc(small_low_done, 1)
                if layer == 0:
                    for i in range(SPLITS):
                        mix_low(layer, i)
                split_turned(3 * layer)
                dve.wait_ge(f_done, layer + 1)
                dve.tensor_scalar(f_logit, bank(7)[0:H_FOX, 0:S], bias_col[:, 0:1], None, ALU.add
                                  ).then_inc(f_biased, 1)
                dve.wait_ge(f_soft_done, layer + 1)
                dve.tensor_scalar(f_logit, f_logit, 0.0, None, ALU.min).then_inc(f_clipped, 1)
                dve.wait_ge(f_clipped, layer + 1)
                dve.tensor_tensor_scan(forget_sum[:, :], f_logit, f_soft, 0.0, ALU.add, ALU.subtract
                                       ).then_inc(c_summed, 1)
                for i in range(SPLITS, QK_UNITS + V_UNITS):
                    mix_low(layer, i)
                    if i == SPLITS:
                        dve.wait_ge(c_summed, layer + 1)
                        dve.tensor_scalar(forget_neg[:, :], forget_sum[:, :], -1.0, None, ALU.mult
                                          ).then_inc(c_neg_done, 1)
                        dve.wait_ge(c_turned, layer + 1)
                        dve.tensor_copy(forget_col[:, :, :], bank(6)[:, 0:TB * 8]
                                        .rearrange("p (t f) -> p t f", t=TB)[:, :, 0:H_FOX]).then_inc(c_col_done, 1)
                        if layer == 0:
                            tables()
                for half in range(2):
                    dve.wait_ge(used, base + QK_UNITS + 2 * half + 2)
                    for t in range(TB):
                        dve.tensor_copy(v_rows[:, t, half * HALF:(half + 1) * HALF], bank(4 + 2 * half + t)
                                        ).then_inc(v_copied, 1)
                for i in range(QK_UNITS + V_UNITS, MIX_UNITS - 1):
                    mix_low(layer, i)
                attention(layer)
                split_turned(3 * layer + 1)
                mix_low(layer, MIX_UNITS - 1)
                mix_low(layer, MIX_UNITS)
                for half in range(2):
                    dve.wait_ge(used, base + MIX_UNITS - 2 + 2 * half)
                    for t in range(TB):
                        r = resid[:, t, half * HALF:(half + 1) * HALF]
                        dve.tensor_tensor(r, r, bank(4 + 2 * half + t), ALU.add).then_inc(resid_done, 1)
                    mix_low(layer, MIX_UNITS + 1 + half)

            def ffn_steps(base, first_step, blocks, split0, begun, x_part, following):
                def unit_low(i, number, slot):
                    low(slot, number, (split0 + i) % SPLITS)

                def mul(count):
                    dve.wait_ge(activated, count + 1)
                    if not isinstance(count, int) or count:
                        dve.wait_ge(hid_turned, count)
                    dve.tensor_tensor(hidden[:, 0:blocks, :], gated[:, 0:blocks, :], psum[:, 0:blocks, 256:512],
                                      ALU.mult).then_inc(hidden_done, 1)

                def hid(count):
                    dve.wait_ge(hid_high_done, count + 1)
                    dve.tensor_tensor(hid_low[:, :, 0:blocks * P],
                                      bank(2)[:, 0:2 * blocks * P].rearrange("p (c s) -> p c s", c=2),
                                      hid_high[:, :, 0:blocks * P].bitcast(F32), ALU.subtract
                                      ).then_inc(hid_low_done, 1)

                def step(number, count, ring):
                    unit_low(2, number + 3, ring[0])
                    mul(count)
                    unit_low(3, number + 4, ring[1])
                    hid(count)
                    unit_low(4, number + 5, ring[2])

                mul(first_step)
                unit_low(3, base + 3, RING_A[1])
                hid(first_step)
                unit_low(4, base + 4, RING_A[2])
                begun()
                with dve.Fori(0, PAIRS - 1) as it:
                    step(base + it * 6 + 2, first_step + it * 2 + 1, RING_B)
                    step(base + it * 6 + 5, first_step + it * 2 + 2, RING_A)
                step(base + 3 * (STEPS - 2) - 1, first_step + STEPS - 2, RING_B)
                number, count = base + 3 * (STEPS - 1) - 1, first_step + STEPS - 1
                unit_low(2, number + 3, LAST)
                mul(count)
                if following:
                    following(0)
                hid(count)
                if following:
                    following(1)
                x_part()

            def nothing():
                pass

            mix(0)
            norm(2, 3)
            split_turned(2)
            ffn_steps(DENSE_BASE, 0, TB, DENSE_BASE % SPLITS, nothing, nothing, lambda i: mix_low(1, i))
            dve.wait_ge(used, DENSE_BASE + FFN_UNITS)
            for t in range(TB):
                for half in range(2):
                    r = resid[:, t, half * HALF:(half + 1) * HALF]
                    dve.tensor_tensor(r, r, bank(4 + 2 * t + half), ALU.add).then_inc(resid_done, 1)
            mix_low(1, 2)
            mix(1)
            norm(4, 6)
            dve.wait_ge(small_high_done, 3)
            dve.tensor_tensor(small_low[:, :, :], small_raw[:, :, :], small_high[:, :, :].bitcast(F32),
                              ALU.subtract).then_inc(small_low_done, 1)
            split_turned(5)
            for t in range(TB):
                dve.wait_ge(rows_high_done, t + 1)
                dve.tensor_tensor(rows_low[:, t, :], rows[:, t, :], rows_high[:, t, :].bitcast(F32),
                                  ALU.subtract).then_inc(rows_low_done, 1)

            n = [0]

            def chain(ins):
                n[0] += 1
                ins.then_inc(route_chain, 1)
                dve.wait_ge(route_chain, n[0])

            E = EXPERTS
            chain(dve.memset(earlier[:, :, :, :], 0.0))
            for e in range(1, E):
                chain(dve.memset(earlier[:, :, e, 0:e], 1.0))
            dve.wait_ge(logits_done, 1)
            dve.tensor_copy(logits_t[:, :], bank(4)[0:E, 0:S]).then_inc(logits_copied, 1)
            dve.wait_ge(logits_turned, 1)
            chain(dve.tensor_copy(logits[:, :, :], bank(6)[:, 0:TB * E].rearrange("p (t e) -> p t e", t=TB)))
            by_j = logits[:, :, :].unsqueeze(2).to_broadcast([P, TB, E, E])
            by_e = logits[:, :, :].unsqueeze(3).to_broadcast([P, TB, E, E])
            chain(dve.tensor_tensor(beats[:, :, :, :], by_j, by_e, ALU.is_gt))
            chain(dve.tensor_tensor(ties[:, :, :, :], by_j, by_e, ALU.is_equal))
            chain(dve.tensor_tensor(ties[:, :, :, :], ties[:, :, :, :], earlier[:, :, :, :], ALU.mult))
            chain(dve.tensor_tensor(beats[:, :, :, :], beats[:, :, :, :], ties[:, :, :, :], ALU.add))
            chain(dve.tensor_reduce(place[:, :, :], beats[:, :, :, :], AX_X, ALU.add))
            dve.tensor_scalar(chosen[:, :, :], place[:, :, :], float(TOP_K), None, ALU.is_lt).then_inc(chosen_done, 1)
            chain(dve.tensor_reduce(top[:, :], logits[:, :, :], AX_X, ALU.max))
            dve.tensor_tensor(gate[:, :, :], logits[:, :, :], top[:, :].unsqueeze(2).to_broadcast([P, TB, E]),
                              ALU.subtract).then_inc(shifted, 1)
            dve.wait_ge(gate_exp, 1)
            dve.wait_ge(chosen_done, 1)
            chain(dve.tensor_tensor(gate[:, :, :], gate[:, :, :], chosen[:, :, :], ALU.mult))
            chain(dve.tensor_reduce(gate_sum[:, :], gate[:, :, :], AX_X, ALU.add))
            chain(dve.reciprocal(gate_sum[:, :], gate_sum[:, :]))
            chain(dve.tensor_tensor(gate[:, :, :], gate[:, :, :],
                                    gate_sum[:, :].unsqueeze(2).to_broadcast([P, TB, E]), ALU.mult))
            dve.wait_ge(ranked, 1)
            chain(dve.tensor_copy(rank[:, :, :], bank(5)[:, 0:TB * E].rearrange("p (t e) -> p t e", t=TB)))
            chain(dve.tensor_reduce(most[:, :], bank(5)[:, TB * E:(TB + 1) * E], AX_X, ALU.max))
            dve.tensor_scalar(spill[:, :], most[:, :], float(slots), None, ALU.is_gt).then_inc(spill_done, 1)

            def experts(number):
                unit0 = MOE_BASE + number * EXPERTS * FFN_UNITS
                split0 = unit0 % SPLITS
                n0 = number * EXPERTS

                def make_take(e):
                    for t in range(TB):
                        dve.tensor_scalar(take[:, t, 0:slots], iota_row[:, 0:slots], rank[:, t, bass.ds(e, 1)],
                                          chosen[:, t, bass.ds(e, 1)], ALU.is_equal, ALU.mult
                                          ).then_inc(take_done, 1)

                def low_x(n):
                    for b, g in enumerate((1, 3)):
                        dve.wait_ge(x_high_done, n * 2 + (b + 1))
                        dve.tensor_tensor(act_low[:, 4 * b:4 * b + 4, 0:P],
                                          bank(g).rearrange("p (k s) -> p k s", k=4),
                                          act_high[:, 4 * b:4 * b + 4, 0:P].bitcast(F32), ALU.subtract
                                          ).then_inc(x_low_done, 1)

                def expert(e, n, base, last):
                    def begun():
                        if not last:
                            dve.wait_ge(take_turned, n + 1)
                            make_take(e + 1)

                    def x_part():
                        if not last:
                            low_x(n + 1)

                    def following(i):
                        low((*FIRST, RING_A[0])[i], base + (FFN_UNITS + i), (split0 + i) % SPLITS)

                    ffn_steps(base, STEPS + n * STEPS, 1, split0, begun, x_part, None if last else following)
                    dve.wait_ge(y_high_done, n + 1)
                    dve.tensor_tensor(y_low[:, :], psum[:, 4:6, :].rearrange("p b n -> p (b n)"),
                                      y_high[:, :].bitcast(F32), ALU.subtract).then_inc(y_low_done, 1)
                    if not last:
                        following(2)
                    for m, (half, t, g) in enumerate(SCATTER):
                        dve.wait_ge(scattered, n * 4 + (m + 1))
                        r = resid[:, t, half * HALF:(half + 1) * HALF]
                        dve.scalar_tensor_tensor(r, bank(g), gate[:, t, bass.ds(e, 1)], r, ALU.mult, ALU.add
                                                 ).then_inc(summed, 1)

                if number:
                    chain(dve.tensor_scalar(rank[:, :, :], rank[:, :, :], -float(slots), None, ALU.add))
                    for i, slot in enumerate((*FIRST, RING_A[0])):
                        low(slot, unit0 + i, (split0 + i) % SPLITS)
                make_take(0)
                low_x(n0)
                with dve.Fori(0, EXPERTS - 1) as e:
                    expert(e, e + n0, unit0 + e * FFN_UNITS, False)
                expert(EXPERTS - 1, n0 + EXPERTS - 1, unit0 + (EXPERTS - 1) * FFN_UNITS, True)

            if slots < P:
                chain(dve.memset(take[:, :, :].bitcast(F32), 0.0))
            experts(0)
            with dve.If(dve.value_load(spill[0:1, 0:1], min_val=0, max_val=1) > 0):
                experts(1)
            dve.memset(most[:, :], 0.0).then_inc(moe_done, 1)
            norm(5, 7)

        @block.tensor
        def _(pe):
            def turn_rows(times, use):
                pe.wait_ge(normed, NORMED[use - 1])
                for b in range(4):
                    for k in (2 * b, 2 * b + 1):
                        for t in range(TB):
                            c = (k % 2) * S + t * P
                            ins = pe.transpose(bank(b)[:, c:c + P], rows[:, t, k * P:(k + 1) * P], ident[:, :])
                    ins.then_inc(turned, 1)

            def three(dst, lhs_high, lhs_low, rhs_high, rhs_low, first, last):
                pe.matmul(dst, lhs_high, rhs_high, start=first, stop=False)
                pe.matmul(dst, lhs_high, rhs_low, start=False, stop=False)
                return pe.matmul(dst, lhs_low, rhs_high, start=False, stop=last)

            def parts(split, a):
                return (w_high[:, split, :].rearrange("p (a n) -> p a n", a=a),
                        w_low[:, split, :].rearrange("p (a n) -> p a n", a=a))

            def attention(layer):
                H0 = layer * HEADS

                def score(i):
                    h = HEAD_ORDER[i]
                    if H0 + i >= 2 and i >= 2:
                        pe.wait_ge(masked, H0 + i - 1)
                    rows_of = slice(HEAD_DIM * (h % 2), HEAD_DIM * (h % 2) + HEAD_DIM)
                    q, k = q_t[rows_of, h // 2, :], k_t[rows_of, h // 2, :]
                    sc = bank(i % 2)
                    if kind(h) == "stick":
                        pe.matmul(sc[:, 0:S], k[:, 0:P], q, start=True, stop=True)
                        ins = pe.matmul(sc[:, S:S + P], k[:, P:S], q[:, P:S], start=True, stop=True)
                    else:
                        for t in range(TB):
                            dst, ts = (sc[:, 0:P], slice(0, P)) if t == 0 else (sc[:, P:P + S], slice(P, S))
                            keys = (t + 1) * P
                            fox = kind(h) == "fox"
                            ins = pe.matmul(dst, q[:, ts], k[:, 0:keys], start=True, stop=not fox)
                            if fox:
                                ins = pe.matmul(dst, pick[:, h - H_DIL, :], forget_neg[:, 0:keys],
                                                start=False, stop=True)
                    ins.then_inc(scores, 1)

                def flip(i):
                    h = HEAD_ORDER[i]
                    if i >= 2:
                        pe.wait_ge(weights_t, H0 + i - 1)
                    dst = bank(2 + i % 2)
                    if kind(h) == "fox":
                        pe.wait_ge(expd, H0 + i + 1)
                    else:
                        pe.wait_ge(weighed, layer * (H_DIL + H_SB) + count_of(i, "dil", "stick"))
                    if kind(h) != "stick":
                        for c in range(3):
                            cs = slice(c * P, (c + 1) * P)
                            ins = pe.transpose(dst[:, cs], prob[:, i % 3, cs], ident[:, :])
                    else:
                        sp_t = stick[:, i % 3, :]
                        pe.matmul(dst[:, 0:S], since[:, :], sp_t[:, 0:S], start=True, stop=False)
                        pe.matmul(dst[:, P:S], ones[:, :], sp_t[:, S:S + P], start=False, stop=True)
                        ins = pe.matmul(dst[:, S:S + P], since[:, :], sp_t[:, S:S + P], start=True, stop=True)
                    ins.then_inc(flipped, 1)

                def mix_values(i):
                    h = HEAD_ORDER[i]
                    pe.wait_ge(weights_t, H0 + i + 1)
                    c0 = (h % (HEADS // 2)) * HEAD_DIM
                    half = h // (HEADS // 2)
                    pt = prob_t[:, i % 2, :]
                    v = v_rows[:, :, h * HEAD_DIM:(h + 1) * HEAD_DIM]
                    pe.matmul(bank(4 + half)[:, c0:c0 + HEAD_DIM], pt[:, 0:P], v[:, 0, :], start=True, stop=True)
                    dst = bank(6 + half)[:, c0:c0 + HEAD_DIM]
                    pe.matmul(dst, pt[:, P:S], v[:, 0, :], start=True, stop=False)
                    pe.matmul(dst, pt[:, S:S + P], v[:, 1, :], start=False, stop=True).then_inc(mixed, 1)

                for s in range(HEADS + 3):
                    if s < HEADS:
                        score(s)
                    if 2 <= s < HEADS + 2:
                        flip(s - 2)
                    if s >= 3:
                        mix_values(s - 3)

            def rows_times_unit(base, i, k0, banks, first, last):
                wh, wl = parts(split_slot(base, i), 4)
                pe.wait_ge(low_done, base + i + 1)
                for kk in range(4):
                    for t in range(TB):
                        ts = slice(t * P, (t + 1) * P)
                        ins = three(bank(banks[t]), act_high[:, k0 + kk, ts], act_low[:, k0 + kk, ts],
                                    wh[:, kk, :], wl[:, kk, :], first and kk == 0, last and kk == 3)
                ins.then_inc(used, 1)

            def mix(layer):
                base = MIX_BASE[layer]
                turn_rows(3 * layer, 3 * layer + 1)
                pe.wait_ge(act_low_done, 12 * layer + 4)
                pe.wait_ge(small_low_done, layer + 1)
                for k in range(KC):
                    ins = three(bank(7)[0:H_FOX, 0:S], forget_high[:, k, :], forget_low[:, k, :], act_high[:, k, :],
                                act_low[:, k, :], k == 0, k == KC - 1)
                ins.then_inc(f_done, 1)
                for i in range(QK_UNITS):
                    if i == 2:
                        pe.wait_ge(c_summed, layer + 1)
                        for t in range(TB):
                            ins = pe.transpose(bank(6)[:, 8 * t:8 * t + H_FOX], forget_sum[:, t * P:(t + 1) * P],
                                               ident[0:H_FOX, 0:H_FOX])
                        ins.then_inc(c_turned, 1)
                    wh, wl = parts(split_slot(base, i), KC)
                    if i >= 4:
                        pe.wait_ge(qk_copied, QK_UNITS * layer + i - 3)
                    pe.wait_ge(low_done, base + i + 1)
                    for c in range(2):
                        cs = slice(c * P, (c + 1) * P)
                        for k in range(KC):
                            ins = three(bank(i % 4)[:, c * S:(c + 1) * S], wh[:, k, cs], wl[:, k, cs],
                                        act_high[:, k, :], act_low[:, k, :], k == 0, k == KC - 1)
                    ins.then_inc(used, 1)
                pe.wait_ge(c_col_done, layer + 1)
                pe.wait_ge(c_neg_done, layer + 1)
                for n in range(V_UNITS):
                    half = n // 2
                    rows_times_unit(base, QK_UNITS + n, 4 * (n % 2), (4 + 2 * half, 5 + 2 * half), n % 2 == 0, n % 2 == 1)
                pe.wait_ge(qk_copied, QK_UNITS * (layer + 1))
                pe.wait_ge(v_copied, 4 * layer + 4)
                pe.wait_ge(pick_done, layer + 1)
                attention(layer)
                turn_rows(3 * layer + 1, 3 * layer + 2)
                pe.wait_ge(act_low_done, 12 * layer + 8)
                for n in range(OUT_UNITS):
                    half = n // 2
                    rows_times_unit(base, QK_UNITS + V_UNITS + n, 4 * (n % 2), (4 + 2 * half, 5 + 2 * half),
                                    n % 2 == 0, n % 2 == 1)

            def channel(blocks, split0):
                def gate_up_part(u, o, number):
                    wh, wl = parts((split0 + o) % SPLITS, 4)
                    pe.wait_ge(low_done, number + 1)
                    for kk in range(4):
                        for t in range(blocks):
                            ts = slice(t * P, (t + 1) * P)
                            k = 4 * u + kk
                            ins = three(bank(t), act_high[:, k, ts], act_low[:, k, ts], wh[:, kk, :],
                                        wl[:, kk, :], k == 0, k == KC - 1)
                    ins.then_inc(used, 1)

                def gate_up(o, number):
                    gate_up_part(0, o, number)
                    gate_up_part(1, o + 1, number + 1)

                def down(o, number, count, first, last):
                    wh, wl = parts((split0 + o) % SPLITS, 2)
                    pe.wait_ge(low_done, number + 1)
                    pe.wait_ge(hid_low_done, count + 1)
                    for c in range(2):
                        for t in range(blocks):
                            for half in range(2):
                                ts, hs = slice(t * P, (t + 1) * P), slice(half * HALF, (half + 1) * HALF)
                                ins = three(bank(4 + 2 * t + half), hid_high[:, c, ts], hid_low[:, c, ts],
                                            wh[:, c, hs], wl[:, c, hs], first and c == 0, last and c == 1)
                    ins.then_inc(used, 1)

                def turn(count):
                    pe.wait_ge(hidden_done, count + 1)
                    for c in range(2):
                        for t in range(blocks):
                            d0 = (c * blocks + t) * P
                            ins = pe.transpose(bank(2)[:, d0:d0 + P], hidden[:, t, c * P:(c + 1) * P], ident[:, :])
                    ins.then_inc(hid_turned, 1)

                return gate_up_part, gate_up, down, turn

            def ffn_steps(base, first_step, blocks, split0, in_step_before, in_last_step):
                _, gate_up, down, turn = channel(blocks, split0)
                turn(first_step)
                gate_up(2, base + 2)
                down(4, base + 4, first_step, True, False)
                turn(first_step + 1)
                with pe.Fori(2, STEPS - 2) as j:
                    number = base + j * 3 - 1
                    gate_up(2, number)
                    down(4, number + 2, first_step + j - 1, False, False)
                    turn(first_step + j)
                for j, extra in ((STEPS - 2, in_step_before), (STEPS - 1, in_last_step)):
                    number = base + (3 * j - 1)
                    gate_up(2, number)
                    extra()
                    down(4, number + 2, first_step + (j - 1), False, False)
                    turn(first_step + j)
                down(FFN_UNITS - 1, base + (FFN_UNITS - 1), first_step + (STEPS - 1), False, True)

            def nothing():
                pass

            pe.wait_ge(const_done, 7)
            mix(0)
            turn_rows(2, 3)
            pe.wait_ge(act_low_done, 12)
            channel(TB, DENSE_BASE % SPLITS)[1](0, DENSE_BASE)
            ffn_steps(DENSE_BASE, 0, TB, DENSE_BASE % SPLITS, nothing, nothing)
            mix(1)
            turn_rows(5, 6)
            pe.wait_ge(act_low_done, 24)
            pe.wait_ge(small_low_done, 3)
            E = EXPERTS
            for k in range(KC):
                ins = three(bank(4)[0:E, 0:S], small_high[:, k, :], small_low[:, k, :], act_high[:, k, :],
                            act_low[:, k, :], k == 0, k == KC - 1)
            ins.then_inc(logits_done, 1)
            pe.wait_ge(logits_copied, 1)
            for t in range(TB):
                ins = pe.transpose(bank(6)[:, E * t:E * (t + 1)], logits_t[:, t * P:(t + 1) * P], ident[0:E, 0:E])
            ins.then_inc(logits_turned, 1)
            pe.wait_ge(chosen_done, 1)
            r = bank(5)
            pe.matmul(r[:, 0:E], before[:, :], chosen[:, 0, :], start=True, stop=True)
            pe.matmul(r[:, E:2 * E], ones[:, :], chosen[:, 0, :], start=True, stop=False)
            pe.matmul(r[:, E:2 * E], before[:, :], chosen[:, 1, :], start=False, stop=True)
            pe.matmul(r[:, 2 * E:3 * E], ones[:, :], chosen[:, 0, :], start=True, stop=False)
            pe.matmul(r[:, 2 * E:3 * E], ones[:, :], chosen[:, 1, :], start=False, stop=True).then_inc(ranked, 1)
            pe.wait_ge(rows_low_done, TB)

            def experts(number):
                unit0 = MOE_BASE + number * EXPERTS * FFN_UNITS
                split0 = unit0 % SPLITS
                n0 = number * EXPERTS
                gate_up_part = channel(1, split0)[0]

                def gather(n):
                    pe.wait_ge(take_done, n * 2 + 2)
                    for b, g in enumerate((1, 3)):
                        cs = slice(b * HALF, (b + 1) * HALF)
                        for t in range(TB):
                            pe.matmul(bank(g), take[:, t, :], rows_high[:, t, cs], start=t == 0, stop=False)
                            ins = pe.matmul(bank(g), take[:, t, :], rows_low[:, t, cs], start=False, stop=t == TB - 1)
                    ins.then_inc(gathered, 1)
                    for t in range(TB):
                        ins = pe.transpose(bank(6)[:, t * P:(t + 1) * P], take[:, t, :].bitcast(F32), ident[:, :])
                    ins.then_inc(take_turned, 1)

                def turn_x(n):
                    pe.wait_ge(x_rows_done, n * 2 + 2)
                    for k in range(KC):
                        ins = pe.transpose(bank((1, 3)[k // 4])[:, (k % 4) * P:(k % 4 + 1) * P],
                                           x_rows[:, k * P:(k + 1) * P], ident[:, :])
                    ins.then_inc(x_turned, 1)

                def expert(n, base, last):
                    ffn_steps(base, STEPS + n * STEPS, 1, split0, nothing if last else lambda: gather(n + 1),
                              nothing if last else lambda: turn_x(n + 1))
                    if not last:
                        pe.wait_ge(x_high_done, n * 2 + 4)
                        pe.wait_ge(x_low_done, n * 2 + 4)
                        gate_up_part(0, 0, base + FFN_UNITS)
                    pe.wait_ge(y_low_done, n + 1)
                    pe.wait_ge(give_done, n + 1)
                    for half, t, g in SCATTER:
                        hs = slice(half * HALF, (half + 1) * HALF)
                        lhs = give[:, t * P:(t + 1) * P]
                        pe.matmul(bank(g), lhs, y_high[:, hs], start=True, stop=False)
                        pe.matmul(bank(g), lhs, y_low[:, hs], start=False, stop=True).then_inc(scattered, 1)
                    if not last:
                        gate_up_part(1, 1, base + (FFN_UNITS + 1))

                gather(n0)
                turn_x(n0)
                pe.wait_ge(x_high_done, n0 * 2 + 2)
                pe.wait_ge(x_low_done, n0 * 2 + 2)
                gate_up_part(0, 0, unit0)
                gate_up_part(1, 1, unit0 + 1)
                with pe.Fori(0, EXPERTS - 1) as e:
                    expert(e + n0, unit0 + e * FFN_UNITS, False)
                expert(n0 + EXPERTS - 1, unit0 + (EXPERTS - 1) * FFN_UNITS, True)

            experts(0)
            pe.wait_ge(spill_done, 1)
            with pe.If(pe.value_load(spill[0:1, 0:1], min_val=0, max_val=1) > 0):
                experts(1)


_INS = ["x", "mix_norm", "w_in", "forget_bias", "head_norm", "w_out", "ffn_norm", "dense_w_gate", "dense_w_up",
        "dense_w_down", "router_w", "moe_w_gate", "moe_w_up", "moe_w_down", "final_norm"]


def kernel(**inputs):
    import numpy as _np
    import concourse.bacc as _bacc
    from concourse import mybir as _mybir
    from concourse.bass_utils import run_bass_kernel_spmd as _run

    nc = _bacc.Bacc("TRN2", target_bir_lowering=False, num_devices=1)
    arrays, args = {}, []
    for name in _INS:
        a = _np.ascontiguousarray(inputs[name])
        arrays[f"in_{name}"] = a
        args.append(nc.dram_tensor(f"in_{name}", a.shape, _mybir.dt.from_np(a.dtype), kind="ExternalInput").ap())
    args.append(nc.dram_tensor("out_0", inputs["x"].shape, _mybir.dt.float32, kind="ExternalOutput").ap())
    hybrid_trunk(nc, *args)
    r = _run(nc, [arrays], core_ids=[0])
    return r.results[0]["out_0"]
```

```python
from contextlib import ExitStack

import concourse.bass as bass
from concourse import mybir

F32 = mybir.dt.float32
F32R = mybir.dt.float32r
BF16 = mybir.dt.bfloat16
I32 = mybir.dt.int32
ALU = mybir.AluOpType
ACT = mybir.ActivationFunctionType
AX_X = mybir.AxisListType.X

P = 128
HEAD_DIM = 64
DIL_PATTERNS = ((128, 1), (512, 4), (2048, 16))
TOP_K = 2
EPS = 1e-6
MASKED = -1e30


def hybrid_trunk(nc, x, mix_norm, w_in, forget_bias, head_norm, w_out, ffn_norm,
                 dense_w_gate, dense_w_up, dense_w_down, router_w,
                 moe_w_gate, moe_w_up, moe_w_down, final_norm, out, slots=P):
    _, S, D = x.shape
    DEPTH = mix_norm.shape[0]
    H_FOX = forget_bias.shape[1]
    HEADS = D // HEAD_DIM
    H_DIL = HEADS * 3 // 8
    H_SB = HEADS - H_DIL - H_FOX
    FF = dense_w_gate.shape[2]
    EXPERTS = moe_w_gate.shape[1]
    TB = S // P
    KC = D // P
    HALF = D // 2
    assert DEPTH == 2 and TB == 2 and D == 1024 and HALF == 512 and FF % 256 == 0
    SCALE = HEAD_DIM ** -0.5
    SOFT = H_DIL + H_FOX

    UNIT = 2048
    QK_UNITS, V_UNITS, OUT_UNITS = 2 * D // 256, 4, 4
    MIX_UNITS = QK_UNITS + V_UNITS + OUT_UNITS
    STEPS = FF // 256
    FFN_UNITS = 3 * STEPS
    PAIRS = (STEPS - 1) // 2
    assert STEPS % 2 == 1 and STEPS >= 5 and MIX_UNITS == 16
    MIX_BASE = [0, MIX_UNITS + FFN_UNITS]
    DENSE_BASE = MIX_UNITS
    MOE_BASE = 2 * MIX_UNITS + FFN_UNITS
    SPLITS = 3

    GROUPS, HALVES = (3, 2, 1, 0), (1, 0)
    HEAD_ORDER = [4 * g + i for g in GROUPS for i in range(4)]
    slot_cols = 3 * P

    ctx = ExitStack()
    with ctx:
        def sb(name, shape, dt, stack=ctx):
            return stack.enter_context(nc.sbuf_tensor(name, shape, dt))

        def sem(name):
            return ctx.enter_context(nc.semaphore(name))

        raw = sb("raw", [P, 9, UNIT], F32)
        w_high = sb("w_high", [P, SPLITS, UNIT], F32R)
        w_low = sb("w_low", [P, SPLITS, UNIT], F32R)
        resid = sb("resid", [P, TB, D], F32)
        rows = sb("rows", [P, TB, D], F32)
        gain = sb("gain", [P, D], F32)
        act_high = sb("act_high", [P, KC, S], F32R)
        act_low = sb("act_low", [P, KC, S], F32R)
        ident = sb("ident", [P, P], F32)
        iota_row = sb("iota_row", [P, P], F32)
        before = sb("before", [P, P], F32)
        since = sb("since", [P, P], F32)
        ones = sb("ones", [P, P], F32)
        causal = sb("causal", [P, slot_cols], BF16)
        strict_t = sb("strict_t", [P, slot_cols], BF16)
        dil_dist = sb("dil_dist", [P, slot_cols], BF16)
        dil_times = sb("dil_times", [P, slot_cols], BF16)
        small_raw = sb("small_raw", [P, KC, EXPERTS], F32)
        small_high = sb("small_high", [P, KC, EXPERTS], F32R)
        small_low = sb("small_low", [P, KC, EXPERTS], F32R)
        forget_raw = sb("forget_raw", [P, KC, H_FOX], F32)
        forget_high = sb("forget_high", [P, KC, H_FOX], F32R)
        forget_low = sb("forget_low", [P, KC, H_FOX], F32R)
        bias_col = sb("bias_col", [H_FOX, 1], F32)
        ssq = sb("ssq", [P, TB], F32)
        rstd = sb("rstd", [P, TB], F32)
        half_power = sb("half_power", [P, TB], F32)
        head_mean = sb("head_mean", [P, TB, HEADS], F32)
        head_rstd = sb("head_rstd", [P, TB, HEADS], F32)
        head_fix = sb("head_fix", [P, TB, HEADS], F32)
        neg_max = sb("neg_max", [P, TB, HEADS], F32)
        den = sb("den", [P, TB, HEADS], F32)
        rden = sb("rden", [P, TB, HEADS], F32)
        forget_col = sb("forget_col", [P, TB, H_FOX], F32)

        mixer = ExitStack()
        q_t = sb("q_t", [P, KC, S], F32, mixer)
        k_t = sb("k_t", [P, KC, S], F32, mixer)
        v_rows = sb("v_rows", [P, TB, D], F32, mixer)
        prob = sb("prob", [P, 3, slot_cols], F32, mixer)
        stick = sb("stick", [P, 3, slot_cols], F32, mixer)
        prob_t = sb("prob_t", [P, 2, slot_cols], F32, mixer)
        alibi = sb("alibi", [P, 2, slot_cols], F32, mixer)
        forget_sum = sb("forget_sum", [H_FOX, S], F32, mixer)
        forget_neg = sb("forget_neg", [H_FOX, S], F32, mixer)
        pick = sb("pick", [H_FOX, H_FOX, P], F32, mixer)
        dist_i = alibi[:, 0, :].bitcast(I32)
        f_logit = stick[0:H_FOX, 0, 0:S]
        f_soft = stick[0:H_FOX, 1, 0:S]
        mixer.close()
        ffn = ExitStack()
        gated = sb("gated", [P, TB, 256], F32, ffn)
        hidden = sb("hidden", [P, TB, 256], F32, ffn)
        hid_high = sb("hid_high", [P, 2, S], F32R, ffn)
        hid_low = sb("hid_low", [P, 2, S], F32R, ffn)
        rows_high = sb("rows_high", [P, TB, D], F32R, ffn)
        rows_low = sb("rows_low", [P, TB, D], F32R, ffn)
        y_high = sb("y_high", [P, D], F32R, ffn)
        y_low = sb("y_low", [P, D], F32R, ffn)
        take = sb("take", [P, TB, P], F32R, ffn)
        x_rows = sb("x_rows", [P, D], F32, ffn)
        give = sb("give", [P, S], F32R, ffn)
        logits_t = sb("logits_t", [EXPERTS, S], F32, ffn)
        logits = sb("logits", [P, TB, EXPERTS], F32, ffn)
        beats = sb("beats", [P, TB, EXPERTS, EXPERTS], F32, ffn)
        ties = sb("ties", [P, TB, EXPERTS, EXPERTS], F32, ffn)
        place = sb("place", [P, TB, EXPERTS], F32, ffn)
        chosen = sb("chosen", [P, TB, EXPERTS], F32, ffn)
        top = sb("top", [P, TB], F32, ffn)
        gate = sb("gate", [P, TB, EXPERTS], F32, ffn)
        gate_sum = sb("gate_sum", [P, TB], F32, ffn)
        rank = sb("rank", [P, TB, EXPERTS], F32, ffn)
        most = sb("most", [P, 1], F32, ffn)
        spill = sb("spill", [P, 1], I32, ffn)
        earlier = sb("earlier", [P, TB, EXPERTS, EXPERTS], F32, ffn)
        ffn.close()

        psum = ctx.enter_context(nc.psum_tensor("psum", [P, 8, 512], F32))

        x_loaded = [sem(f"x_block_loaded_{t}") for t in range(TB)]
        small_loaded = sem("small_loaded")
        router_loaded = sem("router_loaded")
        gain_loaded = sem("gain_loaded")
        landed = [sem(f"unit_landed_{s}") for s in range(9)]
        high_done = sem("high_done")
        low_done = sem("low_done")
        used = sem("used")
        const_done = sem("const_done")
        dist_ready = sem("dist_ready")
        table_chain = sem("table_chain")
        tables_done = sem("tables_done")
        forget_high_done = sem("forget_high_done")
        forget_low_done = sem("forget_low_done")
        router_high_done = sem("router_high_done")
        router_low_done = sem("router_low_done")
        squares = sem("squares")
        scale_ready = sem("scale_ready")
        pool_chain = sem("pool_chain")
        normed = sem("normed")
        turned = sem("turned")
        act_high_done = sem("act_high_done")
        act_low_done = sem("act_low_done")
        resid_done = sem("resid_done")
        first_block_out = sem("first_block_out")
        f_done = sem("f_done")
        f_biased = sem("f_biased")
        f_soft_done = sem("f_soft_done")
        f_act_chain = sem("f_act_chain")
        f_clipped = sem("f_clipped")
        c_summed = sem("c_summed")
        c_neg_done = sem("c_neg_done")
        c_turned = sem("c_turned")
        c_col_done = sem("c_col_done")
        qk_copied = sem("qk_copied")
        v_copied = sem("v_copied")
        term_done = sem("term_done")
        pick_chain = sem("pick_chain")
        pick_done = sem("pick_done")
        scores = sem("scores")
        masked = sem("masked")
        expd = sem("expd")
        stick_chain = sem("stick_chain")
        weighed = sem("weighed")
        flipped = sem("flipped")
        arg_done = sem("arg_done")
        weights_t = sem("weights_t")
        mixed = sem("mixed")
        o_squares = sem("o_squares")
        o_copied = sem("o_copied")
        o_chain = sem("o_chain")
        o_mean_done = sem("o_mean_done")
        o_act_chain = sem("o_act_chain")
        o_rstd_done = sem("o_rstd_done")
        activated = sem("activated")
        hidden_done = sem("hidden_done")
        hid_turned = sem("hid_turned")
        hid_high_done = sem("hid_high_done")
        hid_low_done = sem("hid_low_done")
        rows_high_done = sem("rows_high_done")
        rows_low_done = sem("rows_low_done")
        logits_done = sem("logits_done")
        earlier_done = sem("earlier_done")
        route_chain = sem("route_chain")
        shifted = sem("shifted")
        gate_exp = sem("gate_exp")
        chosen_done = sem("chosen_done")
        ranked = sem("ranked")
        spill_done = sem("spill_done")
        take_done = sem("take_done")
        gathered = sem("gathered")
        x_rows_done = sem("x_rows_done")
        x_turned = sem("x_turned")
        logits_turned = sem("logits_turned")
        logits_copied = sem("logits_copied")
        x_high_done = sem("x_high_done")
        x_low_done = sem("x_low_done")
        take_turned = sem("take_turned")
        give_done = sem("give_done")
        y_high_done = sem("y_high_done")
        y_low_done = sem("y_low_done")
        scattered = sem("scattered")
        summed = sem("summed")
        moe_done = sem("moe_done")
        stored = sem("stored")

        MIX_SLOTS = [0, 1, 3, 4, 5, 6, 7, 8]
        FIRST, LAST, RING_A, RING_B = (0, 1), 2, (3, 4, 5), (6, 7, 8)
        mix_loads = [2 * 16 if s != LAST else 0 for s in range(9)]
        ffn_loads = [32, 32, 16] + [PAIRS * 32, PAIRS * 32, PAIRS * 16] * 2
        at_mix = [[0] * 9, [mix_loads[s] + ffn_loads[s] for s in range(9)]]
        at_dense = mix_loads
        at_moe = [at_mix[1][s] + mix_loads[s] for s in range(9)]

        NORMED = [2, 6, 8, 10, 14, 16, 18]

        def mix_landed(layer, i):
            if i >= MIX_UNITS:
                s = (*FIRST, RING_A[0])[i - MIX_UNITS]
                return s, (at_dense, at_moe)[layer][s] + 32
            s = MIX_SLOTS[i % 8]
            return s, at_mix[layer][s] + 16 * (i // 8 + 1)

        def split_slot(base, i):
            return (base + i) % SPLITS

        def bank(i):
            return psum[:, i, :]

        HALF_BANKS = ((6, 7), (2, 3))

        def qk_bank(j):
            return (2, 3)[j % 2] if j < 2 else 6 + j % 2

        def wrow(w, k0, kn, c0, cn):
            return w.rearrange("(k p) n -> p k n", p=P)[:, k0:k0 + kn, c0:c0 + cn]

        def raw_view(s, a):
            return raw[:, s, :].rearrange("p (a n) -> p a n", a=a)

        SCATTER = ((0, 0, 1), (0, 1, 3), (1, 0, 4), (1, 1, 5))

        dil_slopes = [2.0 ** (-8.0 * (h + 1) / H_DIL) for h in range(H_DIL)]

        def kind(h):
            return "dil" if h < H_DIL else ("fox" if h < SOFT else "stick")

        def half_heads(half):
            return slice(HALVES[half] * HEADS // 2, (HALVES[half] + 1) * HEADS // 2)

        def count_of(i, *kinds):
            return sum(kind(h) in kinds for h in HEAD_ORDER[:i + 1])

        def masked_after(m):
            layer, left = (m - 1) // SOFT, (m - 1) % SOFT + 1
            i = next(i for i in range(HEADS) if count_of(i, "dil", "fox") == left)
            return layer * HEADS + i + 1

        def stick_before(layer, i):
            return layer * H_SB + (count_of(i - 3, "stick") if i >= 3 else 0)

        block = ctx.enter_context(nc.Block())

        @block.sync
        def _(sp):
            x_blocks = x.rearrange("b (t p) d -> p (b t) d", p=P)
            for t in range(TB):
                sp.dma_start(resid[:, t, :], x_blocks[:, t, :]).then_inc(x_loaded[t], 16)

            def load_forget(layer):
                sp.dma_start(forget_raw[:, :, :], wrow(w_in[layer], 0, KC, 3 * D, H_FOX)).then_inc(small_loaded, 16)
                sp.dma_start(bias_col[:, :], forget_bias[layer].rearrange("(f a) -> f a", a=1)
                             ).then_inc(small_loaded, 16)

            def mixer_units(layer):
                base = MIX_BASE[layer]
                for i in range(MIX_UNITS):
                    if i < V_UNITS:
                        src, a = wrow(w_in[layer], 4 * (i % 2), 4, 2 * D + i // 2 * 512, 512), 4
                    elif i < V_UNITS + QK_UNITS:
                        j = i - V_UNITS
                        src, a = wrow(w_in[layer], 0, KC, j % 2 * D + GROUPS[j // 2] * 256, 256), KC
                    else:
                        n = i - V_UNITS - QK_UNITS
                        src, a = wrow(w_out[layer], 4 * HALVES[n // 2], 4, n % 2 * 512, 512), 4
                    s, _ = mix_landed(layer, i)
                    if base + i >= 8:
                        sp.wait_ge(low_done, base + i - 7)
                    sp.dma_start(raw_view(s, a), src).then_inc(landed[s], 16)
                    if layer == 0 and i == SPLITS - 1:
                        load_forget(0)
                        sp.dma_start(small_raw[:, :, :], router_w[0].rearrange("(k p) e -> p k e", p=P)
                                     ).then_inc(router_loaded, 16)

            def gate_up_unit(w_gate, w_up, s, step, k0, number, back):
                sp.wait_ge(low_done, number - back)
                for w, c0 in ((w_gate, 0), (w_up, 256)):
                    src = w.rearrange("(k p) f -> p k f", p=P)[:, k0:k0 + 4, bass.ds(step * 256, 256)]
                    sp.dma_start(raw_view(s, 4)[:, :, c0:c0 + 256], src).then_inc(landed[s], 16)

            def down_unit(w_down, s, step, number, back):
                sp.wait_ge(low_done, number - back)
                src = w_down.rearrange("(j c p) n -> j p c n", c=2, p=P)[step]
                sp.dma_start(raw_view(s, 2), src).then_inc(landed[s], 16)

            def ffn_units(w_gate, w_up, w_down, base):
                for k in range(2):
                    gate_up_unit(w_gate, w_up, FIRST[k], 0, 4 * k, base + k, 7)
                with sp.Fori(0, PAIRS) as it:
                    for c, ring in enumerate((RING_A, RING_B)):
                        step = 2 * it + (1 + c)
                        number = base + it * 6 + (2 + 3 * c)
                        gate_up_unit(w_gate, w_up, ring[0], step, 0, number, 5)
                        gate_up_unit(w_gate, w_up, ring[1], step, 4, number + 1, 5)
                        down_unit(w_down, ring[2], step - 1, number + 2, 5)
                down_unit(w_down, LAST, STEPS - 1, base + FFN_UNITS - 1, 5)

            mixer_units(0)
            sp.wait_ge(forget_high_done, 1)
            sp.wait_ge(forget_low_done, 1)
            sp.wait_ge(f_biased, 1)
            load_forget(1)
            ffn_units(dense_w_gate[0], dense_w_up[0], dense_w_down[0], DENSE_BASE)
            mixer_units(1)

            def experts(base):
                with sp.Fori(0, EXPERTS) as e:
                    ffn_units(moe_w_gate[0, e], moe_w_up[0, e], moe_w_down[0, e], base + e * FFN_UNITS)

            experts(MOE_BASE)
            sp.wait_ge(spill_done, 1)
            with sp.If(sp.value_load(spill[0:1, 0:1], min_val=0, max_val=1) > 0):
                experts(MOE_BASE + EXPERTS * FFN_UNITS)

            out_blocks = out.rearrange("b (t p) d -> p (b t) d", p=P)
            for t in range(TB):
                sp.wait_ge(normed, NORMED[6] - TB + t + 1)
                sp.dma_start(out_blocks[:, t, :], rows[:, t, :]).then_inc(stored, 16)
            sp.wait_ge(stored, 16 * TB)

        @block.gpsimd
        def _(pool):
            def load_gain(g):
                src = [mix_norm[0], head_norm[0], ffn_norm[0], mix_norm[1], head_norm[1], ffn_norm[1],
                       final_norm][g]
                if g:
                    pool.wait_ge(normed, NORMED[g - 1])
                pool.dma_start(gain[:, :], src.partition_broadcast(P)).then_inc(gain_loaded, 16)

            load_gain(0)

            n = [0]

            def chain(ins):
                n[0] += 1
                ins.then_inc(const_done, 1)
                pool.wait_ge(const_done, n[0])

            def scale_of(count):
                for t in range(TB):
                    times = TB * (count - 1) + t + 1
                    pool.wait_ge(squares, times)
                    pool.tensor_scalar(ssq[:, t:t + 1], ssq[:, t:t + 1], 1.0 / D, EPS, ALU.mult, ALU.add
                                       ).then_inc(pool_chain, 1)
                    pool.wait_ge(pool_chain, times)
                    pool.tensor_tensor(rstd[:, t:t + 1], ssq[:, t:t + 1], half_power[:, t:t + 1], ALU.pow
                                       ).then_inc(scale_ready, 1)

            ge, gt, eq = ALU.is_ge, ALU.is_gt, ALU.is_equal

            def triangle(t, cmp, cm, step):
                chain(pool.affine_select(out=t[:, :], in_=ones[:, :], compare_op=cmp, fill=0.0, base=0,
                                         pattern=[[step, P]], channel_multiplier=cm))

            chain(pool.memset(half_power[:, :], -0.5))
            chain(pool.memset(ones[:, :], 1.0))
            triangle(ident, eq, 1, -1)
            scale_of(1)
            triangle(before, gt, -1, 1)
            triangle(since, ge, 1, -1)
            chain(pool.iota(iota_row[:, :], [[1, P]], base=0, channel_multiplier=0,
                            allow_small_or_imprecise_dtypes=True))
            chain(pool.memset(causal[:, :], 0.0))
            chain(pool.affine_select(out=causal[:, 0:P], in_=causal[:, 0:P], compare_op=ge, fill=MASKED, base=0,
                                     pattern=[[-1, P]], channel_multiplier=1))
            chain(pool.affine_select(out=causal[:, P:], in_=causal[:, P:], compare_op=ge, fill=MASKED, base=P,
                                     pattern=[[-1, S]], channel_multiplier=1))
            chain(pool.memset(strict_t[:, :], 0.0))
            chain(pool.affine_select(out=strict_t[:, 0:S], in_=strict_t[:, 0:S], compare_op=gt, fill=MASKED, base=0,
                                     pattern=[[1, S]], channel_multiplier=-1))
            chain(pool.affine_select(out=strict_t[:, S:], in_=strict_t[:, S:], compare_op=gt, fill=MASKED, base=0,
                                     pattern=[[1, P]], channel_multiplier=-1))
            chain(pool.iota(dist_i[:, 0:P], [[-1, P]], base=0, channel_multiplier=1))
            pool.iota(dist_i[:, P:], [[-1, S]], base=P, channel_multiplier=1).then_inc(dist_ready, 1)

            for layer in range(DEPTH):
                if layer:
                    scale_of(2 * layer + 1)
                load_gain(3 * layer + 1)
                pool.memset(pick[:, :, :], 1.0).then_inc(pick_chain, 1)
                pool.wait_ge(pick_chain, layer + 1)
                pool.affine_select(out=pick[:, :, :], in_=pick[:, :, :], compare_op=eq, fill=0.0, base=0,
                                   pattern=[[-1, H_FOX], [0, P]], channel_multiplier=1).then_inc(pick_done, 1)
                if layer == 0:
                    pool.wait_ge(tables_done, 1)
                for i, h in enumerate(HEAD_ORDER):
                    if kind(h) == "stick":
                        continue
                    m = layer * SOFT + count_of(i, "dil", "fox")
                    if m > 2:
                        pool.wait_ge(masked, masked_after(m - 2))
                    if kind(h) == "dil":
                        pool.tensor_scalar(alibi[:, m % 2, :], dil_dist[:, :], -dil_slopes[h], 0.0, ALU.mult,
                                           ALU.add).then_inc(term_done, 1)
                    else:
                        pool.wait_ge(c_col_done, layer + 1)
                        for t, (a, b) in enumerate(((0, P), (P, 3 * P))):
                            ins = pool.tensor_scalar(alibi[:, m % 2, a:b], causal[:, a:b], 1.0,
                                                     forget_col[:, t, h - H_DIL:h - H_DIL + 1], ALU.mult, ALU.add)
                        ins.then_inc(term_done, 1)
                load_gain(3 * layer + 2)
                scale_of(2 * layer + 2)
                load_gain(3 * layer + 3)
            pool.memset(earlier[:, :, :, :], 0.0).then_inc(earlier_done, 1)
            pool.wait_ge(earlier_done, 1)
            for e in range(EXPERTS):
                pool.memset(earlier[:, :, e, 0:max(e, 1)], min(e, 1) * 1.0).then_inc(earlier_done, 1)
            scale_of(2 * DEPTH + 1)

        @block.scalar
        def _(act):
            def high(slot, need, number, split):
                act.wait_ge(landed[slot], need)
                if not (isinstance(number, int) and number < SPLITS):
                    act.wait_ge(used, number - (SPLITS - 1))
                act.activation(w_high[:, split, :], raw[:, slot, :], ACT.Copy).then_inc(high_done, 1)

            def mix_high(layer, i):
                slot, need = mix_landed(layer, i)
                high(slot, need, MIX_BASE[layer] + i, split_slot(MIX_BASE[layer], i))

            def sum_squares(count, t):
                if count == 1:
                    act.wait_ge(x_loaded[t], 16)
                elif count <= 2 * DEPTH:
                    act.wait_ge(resid_done, 4 * (count - 2) + 2 * (t + 1))
                    act.wait_ge(turned, 4 * (3 * ((count - 1) // 2) + 2 * ((count - 1) % 2)))
                act.activation(rows[:, t, :], resid[:, t, :], ACT.Square,
                               accum_out=ssq[:, t:t + 1]).then_inc(squares, 1)

            def split_block(times, first_bank, t):
                for j in range(2):
                    act.wait_ge(turned, 4 * times + 2 * t + j + 1)
                    act.activation(act_high[:, 4 * j:4 * j + 4, t * P:(t + 1) * P], bank(first_bank + 2 * t + j)
                                   .rearrange("p (k s) -> p k s", k=4), ACT.Copy).then_inc(act_high_done, 1)

            def split_half(times, half):
                for j in range(2):
                    act.wait_ge(turned, 4 * times + 2 * half + j + 1)
                    c = 4 * HALVES[half] + 2 * j
                    act.activation(act_high[:, c:c + 2, :].rearrange("p k s -> p (k s)"),
                                   bank(HALF_BANKS[half][j]), ACT.Copy).then_inc(act_high_done, 1)

            def qk_copy(layer, j):
                act.wait_ge(used, MIX_BASE[layer] + V_UNITS + j + 1)
                dst, g = (q_t, k_t)[j % 2], GROUPS[j // 2]
                act.activation(dst[:, 2 * g:2 * g + 2, :].rearrange("p k s -> p (k s)"), bank(qk_bank(j)), ACT.Copy,
                               scale=1.0 if j % 2 else SCALE).then_inc(qk_copied, 1)

            def attention(layer):
                H0 = layer * HEADS

                def exps(i):
                    h = HEAD_ORDER[i]
                    act.wait_ge(masked, H0 + i + 1)
                    if kind(h) != "stick":
                        for t, (a, b) in enumerate(((0, P), (P, 3 * P))):
                            p = prob[:, i % 3, a:b]
                            acc = {"accum_out": den[:, t, h:h + 1]} if kind(h) == "fox" else {}
                            ins = act.activation(p, p, ACT.Exp, bias=neg_max[:, t, h:h + 1], scale=-1.0, **acc)
                        ins.then_inc(expd, 1)
                        return
                    m = 2 * (layer * H_SB + count_of(i, "stick") - 1)
                    if H0 + i >= 3:
                        act.wait_ge(flipped, H0 + i - 2)
                        act.wait_ge(weights_t, H0 + i - 2)
                    st = stick[:, i % 3, :]
                    act.activation(st, prob[:, i % 3, :], ACT.Abs).then_inc(stick_chain, 1)
                    act.wait_ge(stick_chain, m + 1)
                    act.activation(st, st, ACT.Exp, scale=-1.0).then_inc(stick_chain, 1)
                    act.wait_ge(stick_chain, m + 2)
                    act.activation(st, st, ACT.Ln, bias=1.0).then_inc(expd, 1)

                def turn(i):
                    h = HEAD_ORDER[i]
                    act.wait_ge(flipped, H0 + i + 1)
                    if i >= 2:
                        act.wait_ge(mixed, H0 + i - 1)
                    if kind(h) != "stick":
                        act.activation(prob_t[:, i % 2, :], bank(2 + i % 2)[:, 0:slot_cols], ACT.Copy
                                       ).then_inc(weights_t, 1)
                    else:
                        act.wait_ge(arg_done, layer * H_SB + count_of(i, "stick"))
                        act.activation(prob_t[:, i % 2, :], stick[:, i % 3, :], ACT.Exp).then_inc(weights_t, 1)

                def o_square(g):
                    act.wait_ge(o_copied, 4 * layer + g + 1)
                    g = GROUPS[g]
                    act.activation(q_t[:, 2 * g:2 * g + 2, :], rows[:, :, g * 256:(g + 1) * 256], ACT.Square
                                   ).then_inc(o_squares, 1)

                def o_power(half):
                    hs = half_heads(half)
                    act.wait_ge(o_mean_done, 2 * layer + half + 1)
                    act.activation(head_rstd[:, :, hs], head_mean[:, :, hs], ACT.Ln).then_inc(o_act_chain, 1)
                    act.wait_ge(o_act_chain, 2 * layer + half + 1)
                    act.activation(head_rstd[:, :, hs], head_rstd[:, :, hs], ACT.Exp, scale=-0.5
                                   ).then_inc(o_rstd_done, 1)

                for s in range(HEADS + 2):
                    if s < HEADS:
                        exps(s)
                    if s >= 2:
                        turn(s - 2)
                    if s % 2 == 0 and s // 2 + 2 < QK_UNITS:
                        qk_copy(layer, s // 2 + 2)
                        if s // 2 + 3 < QK_UNITS:
                            mix_high(layer, V_UNITS + s // 2 + 2 + SPLITS)
                    if s == 15:
                        mix_high(layer, V_UNITS + QK_UNITS + 2)
                    if s % 4 == 3 and s >= 7:
                        o_square(s // 4 - 1)
                    if s == 12:
                        o_power(0)
                    if s == 16:
                        split_half(3 * layer + 1, 0)
                o_square(3)
                o_power(1)

            def mix(layer):
                times = 3 * layer
                act.preload_act_table_set("natural_log_exp_and_others")
                sum_squares(2 * layer + 1, 0)
                if layer == 0:
                    sum_squares(1, 1)
                    split_block(times, 0, 0)
                    mix_high(layer, 0)
                    mix_high(layer, 1)
                else:
                    split_block(times, 0, 0)
                    sum_squares(2 * layer + 1, 1)
                split_block(times, 0, 1)
                mix_high(layer, 2)
                act.wait_ge(small_loaded, 32 * (layer + 1))
                act.activation(forget_high[:, :, :], forget_raw[:, :, :], ACT.Copy).then_inc(forget_high_done, 1)
                mix_high(layer, SPLITS)
                mix_high(layer, SPLITS + 1)
                act.wait_ge(f_biased, layer + 1)
                act.activation(f_soft, f_logit, ACT.Abs).then_inc(f_act_chain, 1)
                act.wait_ge(f_act_chain, 2 * layer + 1)
                act.activation(f_soft, f_soft, ACT.Exp, scale=-1.0).then_inc(f_act_chain, 1)
                act.wait_ge(f_act_chain, 2 * layer + 2)
                act.activation(f_soft, f_soft, ACT.Ln, bias=1.0).then_inc(f_soft_done, 1)
                for i in range(2, V_UNITS):
                    mix_high(layer, i + SPLITS)
                for j in range(2):
                    qk_copy(layer, j)
                    mix_high(layer, V_UNITS + j + SPLITS)
                attention(layer)
                mix_high(layer, MIX_UNITS - 1)
                split_half(times + 1, 1)
                mix_high(layer, MIX_UNITS)
                sum_squares(2 * layer + 2, 0)
                mix_high(layer, MIX_UNITS + 1)
                split_block(times + 2, 2, 0)
                sum_squares(2 * layer + 2, 1)
                split_block(times + 2, 2, 1)

            def ffn_steps(base, first_step, blocks, need, split0, begun, rows_part, x_part, following):
                def unit_high(i, number, slot, times):
                    high(slot, need(slot, times), number, (split0 + i) % SPLITS)

                def silu(number, count):
                    act.wait_ge(used, number + 2)
                    if not isinstance(count, int) or count:
                        act.wait_ge(hidden_done, count)
                    act.activation(gated[:, 0:blocks, :], psum[:, 0:blocks, 0:256], ACT.Silu).then_inc(activated, 1)

                def hid(count):
                    act.wait_ge(hid_turned, count + 1)
                    act.activation(hid_high[:, :, 0:blocks * P], bank(2)[:, 0:2 * blocks * P]
                                   .rearrange("p (c s) -> p c s", c=2), ACT.Copy).then_inc(hid_high_done, 1)

                def step(number, count, ring, times, behind=None):
                    unit_high(2, number + 3, ring[0], times)
                    silu(number, count)
                    unit_high(3, number + 4, ring[1], times)
                    hid(count)
                    if behind:
                        behind()
                    unit_high(4, number + 5, ring[2], times)

                unit_high(3, base + 3, RING_A[1], 1)
                silu(base, first_step)
                unit_high(4, base + 4, RING_A[2], 1)
                hid(first_step)
                begun()
                with act.Fori(0, PAIRS - 1) as it:
                    step(base + it * 6 + 2, first_step + it * 2 + 1, RING_B, it + 1)
                    step(base + it * 6 + 5, first_step + it * 2 + 2, RING_A, it + 2)
                step(base + 3 * (STEPS - 2) - 1, first_step + STEPS - 2, RING_B, PAIRS, rows_part)
                number, count = base + 3 * (STEPS - 1) - 1, first_step + STEPS - 1
                unit_high(2, number + 3, LAST, 1)
                silu(number, count)
                if following:
                    following(0)
                x_part()
                hid(count)
                if following:
                    following(1)

            def nothing():
                pass

            mix(0)
            act.preload_act_table_set("silu_and_others")
            mix_high(0, MIX_UNITS + 2)
            act.wait_ge(router_loaded, 16)
            act.activation(small_high[:, :, :], small_raw[:, :, :], ACT.Copy).then_inc(router_high_done, 1)
            ffn_steps(DENSE_BASE, 0, TB, lambda s, t: at_dense[s] + (16 if s in (LAST, 5, 8) else 32) * t,
                      DENSE_BASE % SPLITS, nothing, nothing, nothing, lambda i: mix_high(1, i))
            mix(1)
            for t in range(TB):
                act.activation(rows_high[:, t, :], rows[:, t, :], ACT.Copy).then_inc(rows_high_done, 1)
            mix_high(1, MIX_UNITS + 2)
            act.wait_ge(shifted, 1)
            act.activation(gate[:, :, :], gate[:, :, :], ACT.Exp).then_inc(gate_exp, 1)
            act.preload_act_table_set("silu_and_others")

            def experts(number):
                unit0 = MOE_BASE + number * EXPERTS * FFN_UNITS
                split0 = unit0 % SPLITS

                def take_x(n):
                    act.wait_ge(gathered, n + 1)
                    for b, g in enumerate((1, 3)):
                        act.activation(x_rows[:, b * HALF:(b + 1) * HALF], bank(g), ACT.Copy).then_inc(x_rows_done, 1)

                def split_x(n):
                    act.wait_ge(x_turned, n + 1)
                    for b, g in enumerate((1, 3)):
                        act.activation(act_high[:, 4 * b:4 * b + 4, 0:P], bank(g)
                                       .rearrange("p (k s) -> p k s", k=4), ACT.Copy).then_inc(x_high_done, 1)

                def expert(n, base, last):
                    def need(s, t, n=n):
                        each = 16 if s in (LAST, 5, 8) else 32
                        per = 1 if s < 3 else PAIRS
                        return (n * per + t) * each + at_moe[s]

                    def give_copy():
                        act.wait_ge(take_turned, n + 1)
                        act.activation(give[:, :], bank(6)[:, 0:S], ACT.Copy).then_inc(give_done, 1)

                    def rows_part():
                        if not last:
                            take_x(n + 1)

                    def x_part():
                        if not last:
                            split_x(n + 1)

                    def following(i):
                        slot = (*FIRST, RING_A[0])[i]
                        high(slot, need(slot, 1, n + 1), base + (FFN_UNITS + i), (split0 + i) % SPLITS)

                    ffn_steps(base, STEPS + n * STEPS, 1, need, split0, give_copy, rows_part, x_part,
                              None if last else following)
                    act.wait_ge(used, base + FFN_UNITS)
                    act.activation(y_high[:, :], psum[:, 4:6, :].rearrange("p b n -> p (b n)"), ACT.Copy
                                   ).then_inc(y_high_done, 1)
                    if not last:
                        following(2)

                n0 = number * EXPERTS
                if number:
                    for i, slot in enumerate((*FIRST, RING_A[0])):
                        per = 1 if slot < 3 else PAIRS
                        high(slot, (n0 * per + 1) * 32 + at_moe[slot], unit0 + i, (split0 + i) % SPLITS)
                take_x(n0)
                split_x(n0)
                with act.Fori(0, EXPERTS - 1) as e:
                    expert(e + n0, unit0 + e * FFN_UNITS, False)
                expert(n0 + EXPERTS - 1, unit0 + (EXPERTS - 1) * FFN_UNITS, True)

            experts(0)
            act.wait_ge(spill_done, 1)
            with act.If(act.value_load(spill[0:1, 0:1], min_val=0, max_val=1) > 0):
                experts(1)
            act.wait_ge(moe_done, 1)
            for t in range(TB):
                sum_squares(2 * DEPTH + 1, t)

        @block.vector
        def _(dve):
            def low(slot, number, split):
                dve.wait_ge(high_done, number + 1)
                dve.tensor_tensor(w_low[:, split, :], raw[:, slot, :], w_high[:, split, :].bitcast(F32),
                                  ALU.subtract).then_inc(low_done, 1)

            def mix_low(layer, i):
                slot, _ = mix_landed(layer, i)
                low(slot, MIX_BASE[layer] + i, split_slot(MIX_BASE[layer], i))

            def norm(count, use, t):
                dve.wait_ge(scale_ready, TB * (count - 1) + t + 1)
                dve.wait_ge(gain_loaded, 16 * use)
                dve.scalar_tensor_tensor(rows[:, t, :], resid[:, t, :], rstd[:, t:t + 1], gain[:, :],
                                         ALU.mult, ALU.mult).then_inc(normed, 1)

            def split_block(times, first_bank, t):
                for j in range(2):
                    dve.wait_ge(act_high_done, 4 * times + 2 * t + j + 1)
                    ks, ts = slice(4 * j, 4 * j + 4), slice(t * P, (t + 1) * P)
                    dve.tensor_tensor(act_low[:, ks, ts], bank(first_bank + 2 * t + j)
                                      .rearrange("p (k s) -> p k s", k=4), act_high[:, ks, ts].bitcast(F32),
                                      ALU.subtract).then_inc(act_low_done, 1)

            def split_half(times, half):
                for j in range(2):
                    dve.wait_ge(act_high_done, 4 * times + 2 * half + j + 1)
                    c = 4 * HALVES[half] + 2 * j
                    hi = act_high[:, c:c + 2, :].rearrange("p k s -> p (k s)")
                    lo = act_low[:, c:c + 2, :].rearrange("p k s -> p (k s)")
                    dve.tensor_tensor(lo, bank(HALF_BANKS[half][j]), hi.bitcast(F32), ALU.subtract
                                      ).then_inc(act_low_done, 1)

            def residual(t, banks):
                for half in range(2):
                    r = resid[:, t, half * HALF:(half + 1) * HALF]
                    dve.tensor_tensor(r, r, bank(banks[half]), ALU.add).then_inc(resid_done, 1)

            def tables():
                n = [0]

                def chain(ins):
                    n[0] += 1
                    ins.then_inc(table_chain, 1)
                    dve.wait_ge(table_chain, n[0])

                dist, work, part = prob[:, 0, :], prob[:, 1, :], prob[:, 2, :]
                mod_i = stick[:, 0, :].bitcast(I32)
                dve.wait_ge(dist_ready, 1)
                chain(dve.tensor_copy(dist, dist_i))
                chain(dve.memset(work, 0.0))
                for window, dilation in DIL_PATTERNS:
                    assert dilation & (dilation - 1) == 0 and S % dilation == 0
                    chain(dve.tensor_scalar(mod_i, dist_i, dilation - 1, None, ALU.bitwise_and))
                    chain(dve.tensor_copy(part, mod_i))
                    chain(dve.tensor_scalar(part, part, 0.0, None, ALU.is_equal))
                    chain(dve.scalar_tensor_tensor(part, dist, float(window), part, ALU.is_le, ALU.mult))
                    chain(dve.tensor_tensor(work, work, part, ALU.add))
                chain(dve.scalar_tensor_tensor(work, dist, 0.0, work, ALU.is_ge, ALU.mult))
                chain(dve.tensor_copy(dil_times[:, :], work))
                chain(dve.tensor_scalar(part, work, 0.0, -MASKED, ALU.is_equal, ALU.mult))
                dve.tensor_tensor(dil_dist[:, :], part, dist, ALU.add).then_inc(tables_done, 1)

            def attention(layer):
                H0 = layer * HEADS

                def mask(i):
                    h = HEAD_ORDER[i]
                    dve.wait_ge(scores, H0 + i + 1)
                    if H0 + i >= 3:
                        dve.wait_ge(flipped, H0 + i - 2)
                        if stick_before(layer, i):
                            dve.wait_ge(arg_done, stick_before(layer, i))
                    sc = bank(i % 2)
                    if kind(h) == "stick":
                        dve.tensor_tensor(prob[:, i % 3, :], sc[:, 0:slot_cols], strict_t[:, :], ALU.add
                                          ).then_inc(masked, 1)
                        return
                    m = layer * SOFT + count_of(i, "dil", "fox")
                    dve.wait_ge(term_done, m)
                    term = alibi[:, m % 2, :]
                    for t, (a, b) in enumerate(((0, P), (P, 3 * P))):
                        ins = dve.tensor_tensor_reduce(prob[:, i % 3, a:b], sc[:, a:b], term[:, a:b], -1.0, 3e38,
                                                       ALU.add, ALU.min, neg_max[:, t, h:h + 1])
                    ins.then_inc(masked, 1)

                def weigh(i):
                    h = HEAD_ORDER[i]
                    if kind(h) == "fox":
                        return
                    dve.wait_ge(expd, H0 + i + 1)
                    if kind(h) == "dil":
                        for t, (a, b) in enumerate(((0, P), (P, 3 * P))):
                            p = prob[:, i % 3, a:b]
                            ins = dve.tensor_tensor_reduce(p, p, dil_times[:, a:b], 1.0, 0.0, ALU.mult, ALU.add,
                                                           den[:, t, h:h + 1])
                    else:
                        ins = dve.scalar_tensor_tensor(stick[:, i % 3, :], prob[:, i % 3, :], 0.0,
                                                       stick[:, i % 3, :], ALU.max, ALU.add)
                    ins.then_inc(weighed, 1)

                def subtract_tail(i):
                    if kind(HEAD_ORDER[i]) != "stick":
                        return
                    dve.wait_ge(flipped, H0 + i + 1)
                    dve.tensor_tensor(stick[:, i % 3, :], prob[:, i % 3, :], bank(2 + i % 2)[:, 0:slot_cols],
                                      ALU.subtract).then_inc(arg_done, 1)

                chained = [25 * layer]

                def chain(ins):
                    chained[0] += 1
                    ins.then_inc(o_chain, 1)
                    dve.wait_ge(o_chain, chained[0])

                def o_copy(g):
                    dve.wait_ge(mixed, H0 + 4 * g + 4)
                    cs = slice(GROUPS[g] * 256, (GROUPS[g] + 1) * 256)
                    dve.tensor_copy(rows[:, :, cs], bank(4 + g % 2)
                                    .rearrange("p (t c) -> p t c", t=TB)).then_inc(o_copied, 1)

                def o_mean(half):
                    hs = half_heads(half)
                    if half == 0 and layer == 0:
                        chain(dve.memset(rden[:, :, SOFT:], 1.0))
                    soft = slice(hs.start, min(hs.stop, SOFT))
                    dve.wait_ge(o_squares, 4 * layer + 2 * half + 2)
                    dve.wait_ge(expd, H0 + (half + 1) * HEADS // 2)
                    chain(dve.reciprocal(rden[:, :, soft], den[:, :, soft]))
                    for t in range(TB):
                        sq = q_t[:, :, :].rearrange("p (g t) (h d) -> p g t h d", t=TB, d=HEAD_DIM)
                        chain(dve.tensor_reduce(head_mean[:, t, hs].rearrange("p (g h) -> p g h", g=2),
                                                sq[:, 2 * HALVES[half]:2 * HALVES[half] + 2, t, :, :], AX_X, ALU.add))
                    m, r = head_mean[:, :, hs], rden[:, :, hs]
                    chain(dve.tensor_tensor(m, m, r, ALU.mult))
                    chain(dve.tensor_tensor(m, m, r, ALU.mult))
                    dve.tensor_scalar(m, m, 1.0 / HEAD_DIM, EPS, ALU.mult, ALU.add).then_inc(o_mean_done, 1)

                def o_norm(half):
                    hs = half_heads(half)
                    cs = slice(HALVES[half] * HALF, (HALVES[half] + 1) * HALF)
                    m, y, f = head_mean[:, :, hs], head_rstd[:, :, hs], head_fix[:, :, hs]
                    dve.wait_ge(o_rstd_done, 2 * layer + half + 1)
                    chain(dve.tensor_tensor(f, m, y, ALU.mult))
                    chain(dve.tensor_tensor(f, f, y, ALU.mult))
                    chain(dve.tensor_scalar(f, f, -0.5, 1.5, ALU.mult, ALU.add))
                    chain(dve.tensor_tensor(y, y, f, ALU.mult))
                    chain(dve.tensor_tensor(y, y, rden[:, :, hs], ALU.mult))
                    for t in range(TB):
                        r = rows[:, t, cs].rearrange("p (h d) -> p h d", d=HEAD_DIM)
                        chain(dve.tensor_tensor(r, r, y[:, t, :].unsqueeze(2)
                                                .to_broadcast([P, HEADS // 2, HEAD_DIM]), ALU.mult))

                def o_gain(half):
                    cs = slice(HALVES[half] * HALF, (HALVES[half] + 1) * HALF)
                    dve.wait_ge(gain_loaded, 16 * (3 * layer + 2))
                    for t in range(TB):
                        r = rows[:, t, cs]
                        dve.tensor_tensor(r, r, gain[:, cs], ALU.mult).then_inc(normed, 1)

                for s in range(HEADS + 2):
                    if s < HEADS:
                        mask(s)
                    if 1 <= s <= HEADS:
                        weigh(s - 1)
                    if s >= 2:
                        subtract_tail(s - 2)
                    if s % 2 == 1 and s // 2 + 3 < QK_UNITS:
                        mix_low(layer, V_UNITS + s // 2 + 2 + SPLITS)
                    if s % 4 == 3 and s >= 7:
                        o_copy(s // 4 - 1)
                    if s == 12:
                        o_mean(0)
                    if s == 13:
                        o_norm(0)
                    if s == 14:
                        o_gain(0)
                    if s == 16:
                        mix_low(layer, V_UNITS + QK_UNITS + 2)
                        split_half(3 * layer + 1, 0)
                o_copy(3)
                o_mean(1)
                o_norm(1)
                o_gain(1)

            def mix(layer):
                base, times = MIX_BASE[layer], 3 * layer
                if layer == 0:
                    norm(1, 1, 0)
                    norm(1, 1, 1)
                    split_block(times, 0, 0)
                    mix_low(layer, 0)
                    mix_low(layer, 1)
                else:
                    dve.wait_ge(first_block_out, 4)
                    residual(0, (4, 5))
                    mix_low(layer, 1)
                    norm(2 * layer + 1, 3 * layer + 1, 0)
                    dve.wait_ge(used, base)
                    residual(1, (6, 7))
                    split_block(times, 0, 0)
                    norm(2 * layer + 1, 3 * layer + 1, 1)
                split_block(times, 0, 1)
                mix_low(layer, 2)
                dve.wait_ge(forget_high_done, layer + 1)
                dve.tensor_tensor(forget_low[:, :, :], forget_raw[:, :, :], forget_high[:, :, :].bitcast(F32),
                                  ALU.subtract).then_inc(forget_low_done, 1)

                def v_copy(half):
                    dve.wait_ge(used, base + 2 * half + 2)
                    for t in range(TB):
                        dve.tensor_copy(v_rows[:, t, half * HALF:(half + 1) * HALF], bank(4 + 2 * half + t)
                                        ).then_inc(v_copied, 1)

                mix_low(layer, SPLITS)
                v_copy(0)
                mix_low(layer, SPLITS + 1)
                dve.wait_ge(f_done, layer + 1)
                dve.tensor_scalar(f_logit, bank(0)[0:H_FOX, 0:S], bias_col[:, 0:1], None, ALU.add
                                  ).then_inc(f_biased, 1)
                dve.wait_ge(f_soft_done, layer + 1)
                dve.tensor_scalar(f_logit, f_logit, 0.0, None, ALU.min).then_inc(f_clipped, 1)
                dve.wait_ge(f_clipped, layer + 1)
                dve.tensor_tensor_scan(forget_sum[:, :], f_logit, f_soft, 0.0, ALU.add, ALU.subtract
                                       ).then_inc(c_summed, 1)
                dve.wait_ge(c_summed, layer + 1)
                dve.tensor_scalar(forget_neg[:, :], forget_sum[:, :], -1.0, None, ALU.mult
                                  ).then_inc(c_neg_done, 1)
                mix_low(layer, 2 + SPLITS)
                dve.wait_ge(c_turned, layer + 1)
                dve.tensor_copy(forget_col[:, :, :], bank(1)[:, 0:TB * 8]
                                .rearrange("p (t f) -> p t f", t=TB)[:, :, 0:H_FOX]).then_inc(c_col_done, 1)
                mix_low(layer, 3 + SPLITS)
                v_copy(1)
                if layer == 0:
                    tables()
                for j in range(2):
                    mix_low(layer, V_UNITS + j + SPLITS)
                dve.wait_ge(tables_done, 1)
                attention(layer)
                mix_low(layer, MIX_UNITS - 1)
                split_half(times + 1, 1)
                mix_low(layer, MIX_UNITS)
                dve.wait_ge(first_block_out, 4 * layer + 2)
                residual(0, (6, 0))
                norm(2 * layer + 2, 3 * layer + 3, 0)
                dve.wait_ge(used, base + MIX_UNITS)
                residual(1, (7, 1))
                split_block(times + 2, 2, 0)
                if layer == 0:
                    mix_low(layer, MIX_UNITS + 1)
                norm(2 * layer + 2, 3 * layer + 3, 1)
                split_block(times + 2, 2, 1)

            def ffn_steps(base, first_step, blocks, split0, begun, x_part, following):
                def unit_low(i, number, slot):
                    low(slot, number, (split0 + i) % SPLITS)

                def mul(count):
                    dve.wait_ge(activated, count + 1)
                    if not isinstance(count, int) or count:
                        dve.wait_ge(hid_turned, count)
                    dve.tensor_tensor(hidden[:, 0:blocks, :], gated[:, 0:blocks, :], psum[:, 0:blocks, 256:512],
                                      ALU.mult).then_inc(hidden_done, 1)

                def hid(count):
                    dve.wait_ge(hid_high_done, count + 1)
                    dve.tensor_tensor(hid_low[:, :, 0:blocks * P],
                                      bank(2)[:, 0:2 * blocks * P].rearrange("p (c s) -> p c s", c=2),
                                      hid_high[:, :, 0:blocks * P].bitcast(F32), ALU.subtract
                                      ).then_inc(hid_low_done, 1)

                def step(number, count, ring):
                    unit_low(2, number + 3, ring[0])
                    mul(count)
                    unit_low(3, number + 4, ring[1])
                    hid(count)
                    unit_low(4, number + 5, ring[2])

                mul(first_step)
                unit_low(3, base + 3, RING_A[1])
                hid(first_step)
                unit_low(4, base + 4, RING_A[2])
                begun()
                with dve.Fori(0, PAIRS - 1) as it:
                    step(base + it * 6 + 2, first_step + it * 2 + 1, RING_B)
                    step(base + it * 6 + 5, first_step + it * 2 + 2, RING_A)
                step(base + 3 * (STEPS - 2) - 1, first_step + STEPS - 2, RING_B)
                number, count = base + 3 * (STEPS - 1) - 1, first_step + STEPS - 1
                unit_low(2, number + 3, LAST)
                mul(count)
                x_part()
                hid(count)
                if following:
                    following(0)
                    if blocks == 1:
                        following(1)

            def nothing():
                pass

            mix(0)
            mix_low(0, MIX_UNITS + 2)
            dve.wait_ge(router_high_done, 1)
            dve.tensor_tensor(small_low[:, :, :], small_raw[:, :, :], small_high[:, :, :].bitcast(F32),
                              ALU.subtract).then_inc(router_low_done, 1)
            ffn_steps(DENSE_BASE, 0, TB, DENSE_BASE % SPLITS, nothing, nothing, lambda i: mix_low(1, i))
            mix(1)
            for t in range(TB):
                dve.wait_ge(rows_high_done, t + 1)
                dve.tensor_tensor(rows_low[:, t, :], rows[:, t, :], rows_high[:, t, :].bitcast(F32),
                                  ALU.subtract).then_inc(rows_low_done, 1)
            mix_low(1, MIX_UNITS + 1)

            n = [0]

            def chain(ins):
                n[0] += 1
                ins.then_inc(route_chain, 1)
                dve.wait_ge(route_chain, n[0])

            E = EXPERTS
            dve.wait_ge(logits_done, 1)
            dve.tensor_copy(logits_t[:, :], bank(0)[0:E, 0:S]).then_inc(logits_copied, 1)
            dve.wait_ge(logits_turned, 1)
            chain(dve.tensor_copy(logits[:, :, :], bank(6)[:, 0:TB * E].rearrange("p (t e) -> p t e", t=TB)))
            by_j = logits[:, :, :].unsqueeze(2).to_broadcast([P, TB, E, E])
            by_e = logits[:, :, :].unsqueeze(3).to_broadcast([P, TB, E, E])
            chain(dve.tensor_tensor(beats[:, :, :, :], by_j, by_e, ALU.is_gt))
            chain(dve.tensor_tensor(ties[:, :, :, :], by_j, by_e, ALU.is_equal))
            dve.wait_ge(earlier_done, 1 + EXPERTS)
            chain(dve.tensor_tensor(ties[:, :, :, :], ties[:, :, :, :], earlier[:, :, :, :], ALU.mult))
            chain(dve.tensor_tensor(beats[:, :, :, :], beats[:, :, :, :], ties[:, :, :, :], ALU.add))
            chain(dve.tensor_reduce(place[:, :, :], beats[:, :, :, :], AX_X, ALU.add))
            dve.tensor_scalar(chosen[:, :, :], place[:, :, :], float(TOP_K), None, ALU.is_lt).then_inc(chosen_done, 1)
            chain(dve.tensor_reduce(top[:, :], logits[:, :, :], AX_X, ALU.max))
            dve.tensor_tensor(gate[:, :, :], logits[:, :, :], top[:, :].unsqueeze(2).to_broadcast([P, TB, E]),
                              ALU.subtract).then_inc(shifted, 1)
            dve.wait_ge(gate_exp, 1)
            dve.wait_ge(chosen_done, 1)
            chain(dve.tensor_tensor(gate[:, :, :], gate[:, :, :], chosen[:, :, :], ALU.mult))
            chain(dve.tensor_reduce(gate_sum[:, :], gate[:, :, :], AX_X, ALU.add))
            chain(dve.reciprocal(gate_sum[:, :], gate_sum[:, :]))
            chain(dve.tensor_tensor(gate[:, :, :], gate[:, :, :],
                                    gate_sum[:, :].unsqueeze(2).to_broadcast([P, TB, E]), ALU.mult))
            dve.wait_ge(ranked, 1)
            chain(dve.tensor_copy(rank[:, :, :], bank(5)[:, 0:TB * E].rearrange("p (t e) -> p t e", t=TB)))
            chain(dve.tensor_reduce(most[:, :], bank(5)[:, TB * E:(TB + 1) * E], AX_X, ALU.max))
            dve.tensor_scalar(spill[:, :], most[:, :], float(slots), None, ALU.is_gt).then_inc(spill_done, 1)

            def experts(number):
                unit0 = MOE_BASE + number * EXPERTS * FFN_UNITS
                split0 = unit0 % SPLITS
                n0 = number * EXPERTS

                def make_take(e):
                    for t in range(TB):
                        dve.tensor_scalar(take[:, t, 0:slots], iota_row[:, 0:slots], rank[:, t, bass.ds(e, 1)],
                                          chosen[:, t, bass.ds(e, 1)], ALU.is_equal, ALU.mult
                                          ).then_inc(take_done, 1)

                def low_x(n):
                    for b, g in enumerate((1, 3)):
                        dve.wait_ge(x_high_done, n * 2 + (b + 1))
                        dve.tensor_tensor(act_low[:, 4 * b:4 * b + 4, 0:P],
                                          bank(g).rearrange("p (k s) -> p k s", k=4),
                                          act_high[:, 4 * b:4 * b + 4, 0:P].bitcast(F32), ALU.subtract
                                          ).then_inc(x_low_done, 1)

                def expert(e, n, base, last):
                    def begun():
                        if not last:
                            dve.wait_ge(take_turned, n + 1)
                            make_take(e + 1)

                    def x_part():
                        if not last:
                            low_x(n + 1)

                    def following(i):
                        low((*FIRST, RING_A[0])[i], base + (FFN_UNITS + i), (split0 + i) % SPLITS)

                    ffn_steps(base, STEPS + n * STEPS, 1, split0, begun, x_part, None if last else following)
                    dve.wait_ge(y_high_done, n + 1)
                    dve.tensor_tensor(y_low[:, :], psum[:, 4:6, :].rearrange("p b n -> p (b n)"),
                                      y_high[:, :].bitcast(F32), ALU.subtract).then_inc(y_low_done, 1)
                    if not last:
                        following(2)
                    for m, (half, t, g) in enumerate(SCATTER):
                        dve.wait_ge(scattered, n * 4 + (m + 1))
                        r = resid[:, t, half * HALF:(half + 1) * HALF]
                        dve.scalar_tensor_tensor(r, bank(g), gate[:, t, bass.ds(e, 1)], r, ALU.mult, ALU.add
                                                 ).then_inc(summed, 1)

                if number:
                    chain(dve.tensor_scalar(rank[:, :, :], rank[:, :, :], -float(slots), None, ALU.add))
                    for i, slot in enumerate((*FIRST, RING_A[0])):
                        low(slot, unit0 + i, (split0 + i) % SPLITS)
                make_take(0)
                if not number:
                    mix_low(1, MIX_UNITS + 2)
                low_x(n0)
                with dve.Fori(0, EXPERTS - 1) as e:
                    expert(e, e + n0, unit0 + e * FFN_UNITS, False)
                expert(EXPERTS - 1, n0 + EXPERTS - 1, unit0 + (EXPERTS - 1) * FFN_UNITS, True)

            if slots < P:
                chain(dve.memset(take[:, :, :].bitcast(F32), 0.0))
            experts(0)
            with dve.If(dve.value_load(spill[0:1, 0:1], min_val=0, max_val=1) > 0):
                experts(1)
            dve.memset(most[:, :], 0.0).then_inc(moe_done, 1)
            for t in range(TB):
                norm(2 * DEPTH + 1, 7, t)

        @block.tensor
        def _(pe):
            def turn_block(use, first_bank, t):
                pe.wait_ge(normed, NORMED[use - 1] - TB + t + 1)
                for j in range(2):
                    for k in range(4):
                        ins = pe.transpose(bank(first_bank + 2 * t + j)[:, k * P:(k + 1) * P],
                                           rows[:, t, (4 * j + k) * P:(4 * j + k + 1) * P], ident[:, :])
                    ins.then_inc(turned, 1)

            def turn_half(use, half):
                pe.wait_ge(normed, NORMED[use - 1] - 2 + 2 * half)
                for j in range(2):
                    for k in range(2):
                        for t in range(TB):
                            c0 = HALVES[half] * HALF + (2 * j + k) * P
                            ins = pe.transpose(bank(HALF_BANKS[half][j])[:, k * S + t * P:k * S + (t + 1) * P],
                                               rows[:, t, c0:c0 + P], ident[:, :])
                    ins.then_inc(turned, 1)

            def three(dst, lhs_high, lhs_low, rhs_high, rhs_low, first, last):
                pe.matmul(dst, lhs_high, rhs_high, start=first, stop=False)
                pe.matmul(dst, lhs_high, rhs_low, start=False, stop=False)
                return pe.matmul(dst, lhs_low, rhs_high, start=False, stop=last)

            def parts(split, a):
                return (w_high[:, split, :].rearrange("p (a n) -> p a n", a=a),
                        w_low[:, split, :].rearrange("p (a n) -> p a n", a=a))

            def attention(layer):
                H0 = layer * HEADS

                def score(i):
                    h = HEAD_ORDER[i]
                    pe.wait_ge(qk_copied, QK_UNITS * layer + 2 * (i // 4) + 2)
                    if H0 + i >= 2 and i >= 2:
                        pe.wait_ge(masked, H0 + i - 1)
                    rows_of = slice(HEAD_DIM * (h % 2), HEAD_DIM * (h % 2) + HEAD_DIM)
                    q, k = q_t[rows_of, h // 2, :], k_t[rows_of, h // 2, :]
                    sc = bank(i % 2)
                    if kind(h) == "stick":
                        pe.matmul(sc[:, 0:S], k[:, 0:P], q, start=True, stop=True)
                        ins = pe.matmul(sc[:, S:S + P], k[:, P:S], q[:, P:S], start=True, stop=True)
                    else:
                        for t in range(TB):
                            dst, ts = (sc[:, 0:P], slice(0, P)) if t == 0 else (sc[:, P:P + S], slice(P, S))
                            keys = (t + 1) * P
                            fox = kind(h) == "fox"
                            ins = pe.matmul(dst, q[:, ts], k[:, 0:keys], start=True, stop=not fox)
                            if fox:
                                ins = pe.matmul(dst, pick[:, h - H_DIL, :], forget_neg[:, 0:keys],
                                                start=False, stop=True)
                    ins.then_inc(scores, 1)

                def flip(i):
                    h = HEAD_ORDER[i]
                    if i >= 2:
                        pe.wait_ge(weights_t, H0 + i - 1)
                    dst = bank(2 + i % 2)
                    if kind(h) == "fox":
                        pe.wait_ge(expd, H0 + i + 1)
                    else:
                        pe.wait_ge(weighed, layer * (H_DIL + H_SB) + count_of(i, "dil", "stick"))
                    if kind(h) != "stick":
                        for c in range(3):
                            cs = slice(c * P, (c + 1) * P)
                            ins = pe.transpose(dst[:, cs], prob[:, i % 3, cs], ident[:, :])
                    else:
                        sp_t = stick[:, i % 3, :]
                        pe.matmul(dst[:, 0:S], since[:, :], sp_t[:, 0:S], start=True, stop=False)
                        pe.matmul(dst[:, P:S], ones[:, :], sp_t[:, S:S + P], start=False, stop=True)
                        ins = pe.matmul(dst[:, S:S + P], since[:, :], sp_t[:, S:S + P], start=True, stop=True)
                    ins.then_inc(flipped, 1)

                def mix_values(i):
                    h = HEAD_ORDER[i]
                    pe.wait_ge(weights_t, H0 + i + 1)
                    g = i // 4
                    if i % 4 == 0 and g >= 2:
                        pe.wait_ge(o_copied, 4 * layer + g - 1)
                    pt = prob_t[:, i % 2, :]
                    v = v_rows[:, :, h * HEAD_DIM:(h + 1) * HEAD_DIM]
                    dst = [bank(4 + g % 2)[:, t * 256 + h % 4 * HEAD_DIM:t * 256 + (h % 4 + 1) * HEAD_DIM]
                           for t in range(TB)]
                    pe.matmul(dst[0], pt[:, 0:P], v[:, 0, :], start=True, stop=True)
                    pe.matmul(dst[1], pt[:, P:S], v[:, 0, :], start=True, stop=False)
                    pe.matmul(dst[1], pt[:, S:S + P], v[:, 1, :], start=False, stop=True).then_inc(mixed, 1)

                qk_part(layer, 2, 0)
                for s in range(HEADS + 3):
                    if s < HEADS:
                        score(s)
                    if s + 1 < 2 * (QK_UNITS - 2):
                        qk_part(layer, 2 + (s + 1) // 2, (s + 1) % 2)
                    if s == 15:
                        turn_half(3 * layer + 2, 0)
                    if 2 <= s < HEADS + 2:
                        flip(s - 2)
                    if s >= 3:
                        mix_values(s - 3)
                pe.wait_ge(act_low_done, 12 * layer + 6)
                out_part(layer, 0, 0)
                out_part(layer, 0, 1)
                pe.wait_ge(masked, H0 + HEADS)
                out_part(layer, 1, 0)
                out_part(layer, 1, 1)

            def block_times_unit(base, i, t, k0, dst, first, last):
                wh, wl = parts(split_slot(base, i), 4)
                pe.wait_ge(low_done, base + i + 1)
                for kk in range(4):
                    ts = slice(t * P, (t + 1) * P)
                    ins = three(bank(dst), act_high[:, k0 + kk, ts], act_low[:, k0 + kk, ts],
                                wh[:, kk, :], wl[:, kk, :], first and kk == 0, last and kk == 3)
                if t == TB - 1:
                    ins.then_inc(used, 1)
                return ins

            def v_part(layer, n, t):
                block_times_unit(MIX_BASE[layer], n, t, 4 * (n % 2), 4 + n // 2 * 2 + t, n % 2 == 0, n % 2 == 1)

            def qk_part(layer, j, c):
                i = V_UNITS + j
                wh, wl = parts(split_slot(MIX_BASE[layer], i), KC)
                if j >= 4:
                    pe.wait_ge(qk_copied, QK_UNITS * layer + j - 1)
                pe.wait_ge(low_done, MIX_BASE[layer] + i + 1)
                cs = slice(c * P, (c + 1) * P)
                for k in range(KC):
                    ins = three(bank(qk_bank(j))[:, c * S:(c + 1) * S], wh[:, k, cs], wl[:, k, cs],
                                act_high[:, k, :], act_low[:, k, :], k == 0, k == KC - 1)
                if c == 1:
                    ins.then_inc(used, 1)

            def out_part(layer, n, t):
                dst = (6 + t, t)[n % 2]
                ins = block_times_unit(MIX_BASE[layer], V_UNITS + QK_UNITS + n, t, 4 * HALVES[n // 2], dst, n // 2 == 0,
                                       n // 2 == 1)
                if t == 0 and n // 2 == 1:
                    ins.then_inc(first_block_out, 1)

            def keep_warm(count):
                for _ in range(count):
                    pe.matmul(bank(7)[:, 0:P], ones[:, :], ones[:, :], start=True, stop=True)

            def start_stage(times, use, first_bank, part):
                turn_block(use, first_bank, 0)
                if times == 0:
                    keep_warm(20)
                pe.wait_ge(act_low_done, 4 * times + 2)
                part(0, 0)
                turn_block(use, first_bank, 1)
                part(1, 0)
                pe.wait_ge(act_low_done, 4 * times + 4)
                part(0, 1)
                part(1, 1)

            def mix(layer):
                times = 3 * layer
                start_stage(times, times + 1, 0, lambda n, t: v_part(layer, n, t))
                pe.wait_ge(forget_low_done, layer + 1)
                for k in range(KC):
                    ins = three(bank(0)[0:H_FOX, 0:S], forget_high[:, k, :], forget_low[:, k, :], act_high[:, k, :],
                                act_low[:, k, :], k == 0, k == KC - 1)
                ins.then_inc(f_done, 1)
                for t in range(TB):
                    v_part(layer, 2, t)
                pe.wait_ge(c_summed, layer + 1)
                for t in range(TB):
                    ins = pe.transpose(bank(1)[:, 8 * t:8 * t + H_FOX], forget_sum[:, t * P:(t + 1) * P],
                                       ident[0:H_FOX, 0:H_FOX])
                ins.then_inc(c_turned, 1)
                for t in range(TB):
                    v_part(layer, 3, t)
                for j in range(2):
                    for c in range(2):
                        qk_part(layer, j, c)
                pe.wait_ge(c_col_done, layer + 1)
                pe.wait_ge(c_neg_done, layer + 1)
                pe.wait_ge(v_copied, 4 * layer + 4)
                pe.wait_ge(pick_done, layer + 1)
                pe.wait_ge(const_done, 6)
                attention(layer)
                turn_half(times + 2, 1)
                pe.wait_ge(act_low_done, 12 * layer + 8)
                for t in range(TB):
                    for n in (2, 3):
                        out_part(layer, n, t)

            def channel(blocks, split0):
                def gate_up_blocks(u, o, number, ts_of):
                    wh, wl = parts((split0 + o) % SPLITS, 4)
                    pe.wait_ge(low_done, number + 1)
                    for kk in range(4):
                        for t in ts_of:
                            ts = slice(t * P, (t + 1) * P)
                            k = 4 * u + kk
                            ins = three(bank(t), act_high[:, k, ts], act_low[:, k, ts], wh[:, kk, :],
                                        wl[:, kk, :], k == 0, k == KC - 1)
                    if blocks - 1 in ts_of:
                        ins.then_inc(used, 1)

                def gate_up_part(u, o, number):
                    gate_up_blocks(u, o, number, range(blocks))

                def gate_up(o, number):
                    gate_up_part(0, o, number)
                    gate_up_part(1, o + 1, number + 1)

                def down(o, number, count, first, last):
                    wh, wl = parts((split0 + o) % SPLITS, 2)
                    pe.wait_ge(low_done, number + 1)
                    pe.wait_ge(hid_low_done, count + 1)

                    def part(c, t, half):
                        ts, hs = slice(t * P, (t + 1) * P), slice(half * HALF, (half + 1) * HALF)
                        return three(bank(4 + 2 * t + half), hid_high[:, c, ts], hid_low[:, c, ts],
                                     wh[:, c, hs], wl[:, c, hs], first and c == 0, last and c == 1)

                    if last and blocks > 1:
                        for t in range(blocks):
                            for half in range(2):
                                for c in range(2):
                                    ins = part(c, t, half)
                                if t == 0:
                                    ins.then_inc(first_block_out, 1)
                    else:
                        for c in range(2):
                            for t in range(blocks):
                                for half in range(2):
                                    ins = part(c, t, half)
                    ins.then_inc(used, 1)

                def turn(count):
                    pe.wait_ge(hidden_done, count + 1)
                    for c in range(2):
                        for t in range(blocks):
                            d0 = (c * blocks + t) * P
                            ins = pe.transpose(bank(2)[:, d0:d0 + P], hidden[:, t, c * P:(c + 1) * P], ident[:, :])
                    ins.then_inc(hid_turned, 1)

                return gate_up_blocks, gate_up_part, gate_up, down, turn

            def ffn_steps(base, first_step, blocks, split0, in_step_before, in_last_step):
                _, _, gate_up, down, turn = channel(blocks, split0)
                turn(first_step)
                gate_up(2, base + 2)
                down(4, base + 4, first_step, True, False)
                turn(first_step + 1)
                with pe.Fori(2, STEPS - 2) as j:
                    number = base + j * 3 - 1
                    gate_up(2, number)
                    down(4, number + 2, first_step + j - 1, False, False)
                    turn(first_step + j)
                for j, extra in ((STEPS - 2, in_step_before), (STEPS - 1, in_last_step)):
                    number = base + (3 * j - 1)
                    gate_up(2, number)
                    extra()
                    down(4, number + 2, first_step + (j - 1), False, False)
                    turn(first_step + j)
                down(FFN_UNITS - 1, base + (FFN_UNITS - 1), first_step + (STEPS - 1), False, True)

            def nothing():
                pass

            pe.wait_ge(const_done, 3)
            keep_warm(9)
            mix(0)
            gate_up_blocks = channel(TB, DENSE_BASE % SPLITS)[0]
            start_stage(2, 3, 2, lambda u, t: gate_up_blocks(u, u, DENSE_BASE + u, (t,)))
            ffn_steps(DENSE_BASE, 0, TB, DENSE_BASE % SPLITS, nothing, nothing)
            mix(1)
            for t in range(TB):
                turn_block(6, 2, t)
            keep_warm(5)
            pe.wait_ge(act_low_done, 24)
            pe.wait_ge(router_low_done, 1)
            E = EXPERTS
            for k in range(KC):
                ins = three(bank(0)[0:E, 0:S], small_high[:, k, :], small_low[:, k, :], act_high[:, k, :],
                            act_low[:, k, :], k == 0, k == KC - 1)
            ins.then_inc(logits_done, 1)
            keep_warm(4)
            pe.wait_ge(logits_copied, 1)
            for t in range(TB):
                ins = pe.transpose(bank(6)[:, E * t:E * (t + 1)], logits_t[:, t * P:(t + 1) * P], ident[0:E, 0:E])
            ins.then_inc(logits_turned, 1)
            keep_warm(9)
            pe.wait_ge(chosen_done, 1)
            r = bank(5)
            pe.matmul(r[:, 0:E], before[:, :], chosen[:, 0, :], start=True, stop=True)
            pe.matmul(r[:, E:2 * E], ones[:, :], chosen[:, 0, :], start=True, stop=False)
            pe.matmul(r[:, E:2 * E], before[:, :], chosen[:, 1, :], start=False, stop=True)
            pe.matmul(r[:, 2 * E:3 * E], ones[:, :], chosen[:, 0, :], start=True, stop=False)
            pe.matmul(r[:, 2 * E:3 * E], ones[:, :], chosen[:, 1, :], start=False, stop=True).then_inc(ranked, 1)
            pe.wait_ge(rows_low_done, TB)
            keep_warm(6)

            def experts(number):
                unit0 = MOE_BASE + number * EXPERTS * FFN_UNITS
                split0 = unit0 % SPLITS
                n0 = number * EXPERTS
                gate_up_part = channel(1, split0)[1]

                def gather(n):
                    pe.wait_ge(take_done, n * 2 + 2)
                    for b, g in enumerate((1, 3)):
                        cs = slice(b * HALF, (b + 1) * HALF)
                        for t in range(TB):
                            pe.matmul(bank(g), take[:, t, :], rows_high[:, t, cs], start=t == 0, stop=False)
                            ins = pe.matmul(bank(g), take[:, t, :], rows_low[:, t, cs], start=False, stop=t == TB - 1)
                    ins.then_inc(gathered, 1)
                    for t in range(TB):
                        ins = pe.transpose(bank(6)[:, t * P:(t + 1) * P], take[:, t, :].bitcast(F32), ident[:, :])
                    ins.then_inc(take_turned, 1)

                def turn_x(n):
                    pe.wait_ge(x_rows_done, n * 2 + 2)
                    for k in range(KC):
                        ins = pe.transpose(bank((1, 3)[k // 4])[:, (k % 4) * P:(k % 4 + 1) * P],
                                           x_rows[:, k * P:(k + 1) * P], ident[:, :])
                    ins.then_inc(x_turned, 1)

                def expert(n, base, last):
                    ffn_steps(base, STEPS + n * STEPS, 1, split0, nothing if last else lambda: gather(n + 1),
                              nothing if last else lambda: turn_x(n + 1))
                    if not last:
                        pe.wait_ge(x_high_done, n * 2 + 4)
                        pe.wait_ge(x_low_done, n * 2 + 4)
                        gate_up_part(0, 0, base + FFN_UNITS)
                    pe.wait_ge(y_low_done, n + 1)
                    pe.wait_ge(give_done, n + 1)
                    for half, t, g in SCATTER:
                        hs = slice(half * HALF, (half + 1) * HALF)
                        lhs = give[:, t * P:(t + 1) * P]
                        pe.matmul(bank(g), lhs, y_high[:, hs], start=True, stop=False)
                        pe.matmul(bank(g), lhs, y_low[:, hs], start=False, stop=True).then_inc(scattered, 1)
                    if not last:
                        gate_up_part(1, 1, base + (FFN_UNITS + 1))

                gather(n0)
                keep_warm(3)
                turn_x(n0)
                keep_warm(8)
                pe.wait_ge(x_high_done, n0 * 2 + 2)
                pe.wait_ge(x_low_done, n0 * 2 + 2)
                gate_up_part(0, 0, unit0)
                gate_up_part(1, 1, unit0 + 1)
                with pe.Fori(0, EXPERTS - 1) as e:
                    expert(e + n0, unit0 + e * FFN_UNITS, False)
                expert(n0 + EXPERTS - 1, unit0 + (EXPERTS - 1) * FFN_UNITS, True)

            experts(0)
            pe.wait_ge(spill_done, 1)
            with pe.If(pe.value_load(spill[0:1, 0:1], min_val=0, max_val=1) > 0):
                experts(1)


_INS = ["x", "mix_norm", "w_in", "forget_bias", "head_norm", "w_out", "ffn_norm", "dense_w_gate", "dense_w_up",
        "dense_w_down", "router_w", "moe_w_gate", "moe_w_up", "moe_w_down", "final_norm"]


def kernel(**inputs):
    import numpy as _np
    import concourse.bacc as _bacc
    from concourse import mybir as _mybir
    from concourse.bass_utils import run_bass_kernel_spmd as _run

    nc = _bacc.Bacc("TRN2", target_bir_lowering=False, num_devices=1)
    arrays, args = {}, []
    for name in _INS:
        a = _np.ascontiguousarray(inputs[name])
        arrays[f"in_{name}"] = a
        args.append(nc.dram_tensor(f"in_{name}", a.shape, _mybir.dt.from_np(a.dtype), kind="ExternalInput").ap())
    args.append(nc.dram_tensor("out_0", inputs["x"].shape, _mybir.dt.float32, kind="ExternalOutput").ap())
    hybrid_trunk(nc, *args)
    r = _run(nc, [arrays], core_ids=[0])
    return r.results[0]["out_0"]
```
